# Optimizing a Trainium2 kernel written in Bass

```python
import math
import jax, jax.numpy as jnp
from jax import lax
import numpy as np

D_MODEL = 1024
BATCH = 1
SEQ = 1024
DEPTH = 1
DEC_BATCH = 8
DEC_SEQ = 8
PAST_LEN = 512
PAGE_SIZE = 128

DIFF_HEADS = 8
DIFF_HEAD_DIM = 64
DIFF_V_DIM = 2 * DIFF_HEAD_DIM
ROT_DIM = DIFF_HEAD_DIM // 4
ROPE_THETA = 500000.0
Q_BLOCK = 128
RET_HEADS = 4
RET_KEY_DIM = 256
RET_VALUE_DIM = 512
RET_THETA = 10000.0
RET_CHUNK = 128
FFN_HIDDEN = ((8 * D_MODEL // 3 + 255) // 256) * 256
NORM_EPS = 1e-5
NEG_INF = -1e30

DIFF_QK_W = DIFF_HEADS * 2 * DIFF_HEAD_DIM
DIFF_V_W = DIFF_HEADS * DIFF_V_DIM
RET_QK_W = RET_HEADS * RET_KEY_DIM
RET_V_W = RET_HEADS * RET_VALUE_DIM
IN_WIDTHS = (DIFF_QK_W, DIFF_QK_W, DIFF_V_W, RET_QK_W, RET_QK_W, RET_V_W, RET_V_W, D_MODEL, D_MODEL)
IN_W = sum(IN_WIDTHS)

kernel_name = "hybrid_diffattn_retention_decode_step"

F32 = jnp.float32

def rms_norm(x, g):
    xf = x.astype(F32)
    y = xf * lax.rsqrt(jnp.mean(xf * xf, axis=-1, keepdims=True) + NORM_EPS)
    return (y * g.astype(F32)).astype(x.dtype)

def rms_plain(xf):
    return xf * lax.rsqrt(jnp.mean(xf * xf, axis=-1, keepdims=True) + NORM_EPS)

def partial_rope(x, pos):
    half = ROT_DIM // 2
    freqs = jnp.exp(-math.log(ROPE_THETA) * jnp.arange(half, dtype=F32) * (2.0 / ROT_DIM))
    ang = pos[:, None] * freqs[None, :]
    cos = jnp.cos(ang)[None, :, None, None, :]
    sin = jnp.sin(ang)[None, :, None, None, :]
    xf = x.astype(F32)
    x1 = xf[..., :half]
    x2 = xf[..., half:ROT_DIM]
    out = jnp.concatenate([x1 * cos - x2 * sin, x2 * cos + x1 * sin, xf[..., ROT_DIM:]], axis=-1)
    return out.astype(x.dtype)

def ret_rotate(x, pos):
    half = RET_KEY_DIM // 2
    angle = jnp.exp(-math.log(RET_THETA) * jnp.linspace(0.0, 1.0, half, dtype=F32))
    ang = pos[:, None] * angle[None, :]
    cos = jnp.cos(ang)[None, :, None, :]
    sin = jnp.sin(ang)[None, :, None, :]
    xf = x.astype(F32).reshape(x.shape[:-1] + (half, 2))
    xe, xo = xf[..., 0], xf[..., 1]
    out = jnp.stack([xe * cos - xo * sin, xo * cos + xe * sin], axis=-1).reshape(x.shape)
    return out.astype(x.dtype)

def project_in(xn, w_in, pos):
    B, T = xn.shape[:2]
    splits = [int(s) for s in np.cumsum(IN_WIDTHS)[:-1]]
    qa, ka, va, qr, kr, vr, gr, gate_a, gate_b = jnp.split(xn @ w_in, splits, axis=-1)
    qa = partial_rope(qa.reshape(B, T, DIFF_HEADS, 2, DIFF_HEAD_DIM), pos)
    ka = partial_rope(ka.reshape(B, T, DIFF_HEADS, 2, DIFF_HEAD_DIM), pos)
    va = va.reshape(B, T, DIFF_HEADS, DIFF_V_DIM)
    qr = ret_rotate(qr.reshape(B, T, RET_HEADS, RET_KEY_DIM), pos)
    kr = ret_rotate(kr.reshape(B, T, RET_HEADS, RET_KEY_DIM), pos) * (RET_KEY_DIM ** -0.5)
    vr = vr.reshape(B, T, RET_HEADS, RET_VALUE_DIM)
    return qa, ka, va, qr, kr, vr, gr, gate_a, gate_b

def diff_scores(q, k, v, mask, lam):
    s = jnp.einsum('bqhcd,bkhcd->bhcqk', q, k).astype(F32) * (DIFF_HEAD_DIM ** -0.5)
    s = jnp.where(mask[None, None, None], s, NEG_INF)
    p = jax.nn.softmax(s, axis=-1)
    w = p[:, :, 0] - lam * p[:, :, 1]
    return jnp.einsum('bhqk,bkhe->bqhe', w.astype(v.dtype), v)

def diff_attn_prompt(q, k, v, lam):
    B, T = q.shape[:2]
    nb = T // Q_BLOCK
    qb = q.reshape(B, nb, Q_BLOCK, DIFF_HEADS, 2, DIFF_HEAD_DIM).swapaxes(0, 1)
    kpos = jnp.arange(T)

    def one_block(args):
        qi, bi = args
        qpos = bi * Q_BLOCK + jnp.arange(Q_BLOCK)
        return diff_scores(qi, k, v, qpos[:, None] >= kpos[None, :], lam)

    ob = lax.map(one_block, (qb, jnp.arange(nb)))
    return ob.swapaxes(0, 1).reshape(B, T, DIFF_HEADS, DIFF_V_DIM)

def diff_attn_sample(q, k_new, v_new, k_cache, v_cache, page_table, lam):
    DB, T = q.shape[:2]
    k_past = k_cache[page_table].reshape(DB, -1, DIFF_HEADS, 2, DIFF_HEAD_DIM)
    v_past = v_cache[page_table].reshape(DB, -1, DIFF_HEADS, DIFF_V_DIM)
    P = k_past.shape[1]
    k_all = jnp.concatenate([k_past, k_new], axis=1)
    v_all = jnp.concatenate([v_past, v_new], axis=1)
    mask = jnp.concatenate([jnp.ones((T, P), bool), jnp.tril(jnp.ones((T, T), bool))], axis=1)
    return diff_scores(q, k_all, v_all, mask, lam)

def ret_chunk(S, q, k, v, log_gamma):
    C = q.shape[1]
    idx = jnp.arange(C, dtype=F32)
    rel = idx[:, None] - idx[None, :]
    decay = jnp.where(rel >= 0, jnp.exp(log_gamma[:, None, None] * jnp.maximum(rel, 0.0)), 0.0)
    qk = jnp.einsum('bihd,bjhd->bhij', q, k) * decay[None]
    o = jnp.einsum('bhij,bjhe->bihe', qk, v)
    q_dec = jnp.exp((idx[:, None] + 1.0) * log_gamma[None, :])
    o = o + jnp.einsum('bihd,bhde->bihe', q * q_dec[None, :, :, None], S)
    k_dec = jnp.exp((C - 1.0 - idx)[:, None] * log_gamma[None, :])
    S_new = jnp.exp(C * log_gamma)[None, :, None, None] * S + jnp.einsum('bjhd,bjhe->bhde', k * k_dec[None, :, :, None], v)
    return S_new, o

def retention_prompt(q, k, v, log_gamma):
    B, T = q.shape[:2]
    nc = T // RET_CHUNK

    def chunks(x):
        return x.astype(F32).reshape((B, nc, RET_CHUNK) + x.shape[2:]).swapaxes(0, 1)

    S0 = jnp.zeros((B, RET_HEADS, RET_KEY_DIM, RET_VALUE_DIM), F32)
    S, o = lax.scan(lambda S, c: ret_chunk(S, c[0], c[1], c[2], log_gamma), S0, (chunks(q), chunks(k), chunks(v)))
    return S, o.swapaxes(0, 1).reshape(B, T, RET_HEADS, RET_VALUE_DIM)

def merge_out(oa, orr, gr, gate_a, gate_b, b_gate, subln_g, lam_init, w_pa, w_pb, w_o):
    B, T = oa.shape[:2]
    dtype = gr.dtype
    a = (rms_plain(oa.astype(F32)) * subln_g.astype(F32) * (1.0 - lam_init)).reshape(B, T, DIFF_V_W).astype(dtype)
    r = rms_plain(orr.astype(F32)).reshape(B, T, RET_V_W).astype(dtype) * jax.nn.silu(gr)
    ba, bb = jnp.split(b_gate, 2)
    m = jax.nn.sigmoid(gate_a + ba) * (a @ w_pa) + jax.nn.sigmoid(gate_b + bb) * (r @ w_pb)
    return m @ w_o

def swiglu(x, w_gu, w_down):
    g, u = jnp.split(x @ w_gu, 2, axis=-1)
    return (jax.nn.silu(g) * u) @ w_down

def setup_inputs(seed: int = 0) -> dict:
    key = jax.random.key(seed)
    ks = jax.random.split(key, 24)
    n_pages = PAST_LEN // PAGE_SIZE
    n_used = DEC_BATCH * n_pages
    n_phys = n_used + n_used // 4
    page_table = jax.random.permutation(ks[0], n_phys)[:n_used].reshape(DEC_BATCH, n_pages).astype(jnp.int32)

    def nrm(k, shape, scale):
        return scale * jax.random.normal(k, shape, F32)

    return {
        "x_prompt": nrm(ks[1], (BATCH, SEQ, D_MODEL), 1.0),
        "x_sample": nrm(ks[2], (DEC_BATCH, DEC_SEQ, D_MODEL), 1.0),
        "cache_k": nrm(ks[3], (DEPTH, n_phys, PAGE_SIZE, DIFF_HEADS, 2, DIFF_HEAD_DIM), 1.0),
        "cache_v": nrm(ks[4], (DEPTH, n_phys, PAGE_SIZE, DIFF_HEADS, DIFF_V_DIM), 1.0),
        "state_ret": nrm(ks[5], (DEPTH, DEC_BATCH, RET_HEADS, RET_KEY_DIM, RET_VALUE_DIM), 0.5),
        "page_table": page_table,
        "norm_mix_g": 1.0 + nrm(ks[6], (DEPTH, D_MODEL), 0.02),
        "w_in": nrm(ks[7], (DEPTH, D_MODEL, IN_W), D_MODEL ** -0.5),
        "b_gate": nrm(ks[8], (DEPTH, 2 * D_MODEL), 0.02),
        "lambda_q1": nrm(ks[9], (DEPTH, DIFF_HEAD_DIM), 0.1),
        "lambda_k1": nrm(ks[10], (DEPTH, DIFF_HEAD_DIM), 0.1),
        "lambda_q2": nrm(ks[11], (DEPTH, DIFF_HEAD_DIM), 0.1),
        "lambda_k2": nrm(ks[12], (DEPTH, DIFF_HEAD_DIM), 0.1),
        "subln_g": 1.0 + nrm(ks[13], (DEPTH, DIFF_V_DIM), 0.02),
        "w_pa": nrm(ks[14], (DEPTH, DIFF_V_W, D_MODEL), DIFF_V_W ** -0.5),
        "w_pb": nrm(ks[15], (DEPTH, RET_V_W, D_MODEL), RET_V_W ** -0.5),
        "w_o": nrm(ks[16], (DEPTH, D_MODEL, D_MODEL), D_MODEL ** -0.5),
        "norm_ffn_g": 1.0 + nrm(ks[17], (DEPTH, D_MODEL), 0.02),
        "w_gu": nrm(ks[18], (DEPTH, D_MODEL, 2 * FFN_HIDDEN), D_MODEL ** -0.5),
        "w_down": nrm(ks[19], (DEPTH, FFN_HIDDEN, D_MODEL), FFN_HIDDEN ** -0.5),
        "norm_final_g": 1.0 + nrm(ks[20], (D_MODEL,), 0.02),
    }

def reference(x_prompt, x_sample, cache_k, cache_v, state_ret, page_table,
              norm_mix_g, w_in, b_gate, lambda_q1, lambda_k1, lambda_q2, lambda_k2,
              subln_g, w_pa, w_pb, w_o, norm_ffn_g, w_gu, w_down, norm_final_g):
    T_p = x_prompt.shape[1]
    T_s = x_sample.shape[1]
    past = page_table.shape[1] * cache_k.shape[2]
    pos_p = jnp.arange(T_p, dtype=F32)
    pos_s = jnp.arange(T_s, dtype=F32) + past
    log_gamma = jnp.log(1.0 - jnp.exp2(-5.0 - jnp.arange(RET_HEADS, dtype=F32)))

    hp, hs = x_prompt, x_sample
    kp_l, vp_l, sp_l, ks_l, vs_l, ss_l = [], [], [], [], [], []
    for l in range(DEPTH):
        lam_init = 0.8 - 0.6 * math.exp(-0.3 * l)
        lam = (jnp.exp(jnp.sum(lambda_q1[l].astype(F32) * lambda_k1[l].astype(F32)))
               - jnp.exp(jnp.sum(lambda_q2[l].astype(F32) * lambda_k2[l].astype(F32))) + lam_init)

        xn = rms_norm(hp, norm_mix_g[l])
        qa, ka, va, qr, kr, vr, gr, g_a, g_b = project_in(xn, w_in[l], pos_p)
        oa = diff_attn_prompt(qa, ka, va, lam)
        s_p, orr = retention_prompt(qr, kr, vr, log_gamma)
        hp = hp + merge_out(oa, orr, gr, g_a, g_b, b_gate[l], subln_g[l], lam_init, w_pa[l], w_pb[l], w_o[l])
        hp = hp + swiglu(rms_norm(hp, norm_ffn_g[l]), w_gu[l], w_down[l])
        kp_l.append(ka)
        vp_l.append(va)
        sp_l.append(s_p.astype(x_prompt.dtype))

        xn = rms_norm(hs, norm_mix_g[l])
        qa, ka, va, qr, kr, vr, gr, g_a, g_b = project_in(xn, w_in[l], pos_s)
        oa = diff_attn_sample(qa, ka, va, cache_k[l], cache_v[l], page_table, lam)
        s_s, orr = ret_chunk(state_ret[l].astype(F32), qr.astype(F32), kr.astype(F32), vr.astype(F32), log_gamma)
        hs = hs + merge_out(oa, orr, gr, g_a, g_b, b_gate[l], subln_g[l], lam_init, w_pa[l], w_pb[l], w_o[l])
        hs = hs + swiglu(rms_norm(hs, norm_ffn_g[l]), w_gu[l], w_down[l])
        ks_l.append(ka)
        vs_l.append(va)
        ss_l.append(s_s.astype(state_ret.dtype))

    y_prompt = rms_norm(hp, norm_final_g)
    y_sample = rms_norm(hs, norm_final_g)
    return (y_prompt, y_sample, jnp.stack(kp_l), jnp.stack(vp_l), jnp.stack(sp_l),
            jnp.stack(ks_l), jnp.stack(vs_l), jnp.stack(ss_l))


_drawn_inputs = setup_inputs


def setup_inputs(seed=0):
    import zlib

    import numpy as np

    out = dict(_drawn_inputs(seed))
    spreads = {}
    factors = {'b_gate': 8.0,
     'lambda_q1': 8.0,
     'lambda_k1': 8.0,
     'subln_g': 6.538,
     'norm_ffn_g': 4.284,
     'norm_final_g': 2.957}
    for name, (base, spread) in spreads.items():
        noise = np.random.default_rng([zlib.crc32(name.encode()), seed]).standard_normal(out[name].shape)
        drawn = base * np.exp(spread * noise) if base else spread * noise
        out[name] = __import__('jax').numpy.asarray(drawn.astype(out[name].dtype))
    for name, factor in factors.items():
        out[name] = (out[name] * factor).astype(out[name].dtype)
    return out
```

```python
import math
from contextlib import ExitStack

import numpy as np
import concourse.bass as bass
from concourse import mybir

F = mybir.dt.float32
R = mybir.dt.float32r
I32 = mybir.dt.int32
ALU = mybir.AluOpType
ACT = mybir.ActivationFunctionType
AX = mybir.AxisListType

D = 1024
TP = 1024
DB, DS = 8, 8
TS = DB * DS
T = TP + TS
NT = TP // 128 + 1
SAMPLE = NT - 1
KD = D // 128
PAST, PAGE = 512, 128
NPG = PAST // PAGE
N_PHYS = 40
DH, DHD, DV = 8, 64, 128
RH, RK, RV = 4, 256, 512
CH = 128
NC = TP // CH
FFN = 2816
NEG = -1e30
EPS = 1e-5
LAM_INIT = 0.8 - 0.6 * math.exp(-0.3 * 0)
WN = 512
N_TM = 14
N_FM = 8
N_GU = FFN // 256
DOWN_K = [8, 8, 6]
CHUNKS = [(0, 384), (384, 384), (768, 320)]
RING = 6
QA, KA, VA, QR, KR, VR = 0, 1024, 2048, 3072, 4096, 5120
PW = N_TM * WN
G_R, G_A, G_B = 0, 2048, 3072

W_TM, W_FM = 0, N_TM
W_PA = W_FM + N_FM
W_PB = W_PA + 2
W_O = W_PB + 4
W_GU = W_O + 2
W_DN = W_GU + N_GU
N_W = W_DN + 2 * len(DOWN_K)
W_NK = [KD] * W_DN + [k for k in DOWN_K for _ in range(2)]


def rows(t):
    return TS if t == SAMPLE else 128


def banks_before(w):
    n = 2 * NT
    for v in range(w):
        if v == W_GU:
            n += 2 * NT
        n += NT if v < W_FM or W_O <= v < W_GU or v >= W_DN else 12
    return n + (2 * NT if w == W_GU else 0)


class Count:

    def __init__(self, sem):
        self.sem, self.n, self.i, self.per = sem, 0, None, 0

    def loop(self, i, per):
        self.i, self.per, self.at = i, per, self.n

    def end(self, rounds):
        assert self.n - self.at == self.per, (self.n - self.at, self.per)
        self.n = self.at + self.per * rounds
        self.i = None

    def value(self):
        return self.n if self.i is None else self.i * self.per + self.n

    def done(self, ins):
        ins.then_inc(self.sem, 1)
        self.n += 1

    def wait(self, eng):
        eng.wait_ge(self.sem, self.value())


def hybrid_layer(nc, x_prompt, x_sample, cache_k, cache_v, state_ret, page_table, norm_mix_g, w_in, b_gate,
                 lambda_q1, lambda_k1, lambda_q2, lambda_k2, subln_g, w_pa, w_pb, w_o, norm_ffn_g, w_gu,
                 w_down, norm_final_g, c_ident, c_rope_diff, c_rope_ret, c_causal, c_new_mask, c_comb,
                 c_ret, c_ret_new, c_ret_qdec,
                 y_prompt, y_sample, k_prompt, v_prompt, ret_prompt, k_sample, v_sample, ret_sample):
    ctx = ExitStack()
    sb = lambda name, shape, dt=F, st=ctx: st.enter_context(nc.sbuf_tensor(name, shape, dt))
    sem = lambda name: ctx.enter_context(nc.semaphore(name))

    proj = nc.dram_tensor("proj", [T, PW], F).ap()
    gates = nc.dram_tensor("gates", [4 * D, T], F).ap()
    a_t = nc.dram_tensor("a_t", [D, T], F).ap()
    r_t = nc.dram_tensor("r_t", [2 * D, T], F).ap()
    h_t = nc.dram_tensor("h_t", [FFN, T], F).ap()

    ident = sb("ident", [128, 128])
    gain = sb("gain", [128, D])
    rope_diff = sb("rope_diff", [128, NT, 2, 16])
    stage = [sb(f"stage{h}", [128, KD // 2, WN]) for h in range(2)]
    w_h = [sb(f"w_h{s}", [128, KD, WN], R) for s in range(2)]
    w_l = [sb(f"w_l{s}", [128, KD, WN], R) for s in range(2)]
    edge = sb("edge", [128, 3328])
    bias = sb("bias", [128, 16])
    ss = sb("ss", [128, NT])
    rstd = sb("rstd", [128, NT])
    newton = sb("newton", [128, NT])
    ones = sb("ones", [128, 1])
    one = ones[:, :]
    exponent = sb("exponent", [128, NT])
    neg_lam = sb("neg_lam", [128, 1])
    sub_gain = sb("sub_gain", [128, 1])

    def activations(n, st):
        return (sb(f"xt_h{n}", [128, KD, T], R, st), sb(f"xt_l{n}", [128, KD, T], R, st),
                sb(f"xs_hl{n}", [128, KD, 128], R, st), sb(f"acc{n}", [128, NT * D], F, st))

    st = ExitStack()
    xt_h1, xt_l1, xs_hl1, acc1 = activations(1, st)
    st.close()
    st = ExitStack()
    xt_h2, xt_l2, xs_hl2, acc2 = activations(2, st)
    st.close()
    x_rows = acc1[:, :].rearrange("p (t d) -> p t d", d=D)
    rope_ret = acc1[:, 0:NT * 512].rearrange("p (t s d) -> p t s d", s=2, d=256)
    h_rows = acc2[:, :].rearrange("p (t d) -> p t d", d=D)
    m_t = acc2[:, 0:KD * T].rearrange("p (k n) -> p k n", n=T)

    psum = ctx.enter_context(nc.psum_tensor("psum", [128, 8, 512], F))

    stage_loaded = [sem("stage_loaded0"), sem("stage_loaded1")]
    ones_set = sem("ones_set")
    w_high = sem("w_high")
    w_split = sem("w_split")
    bank_full = sem("bank_full")
    bank_free = sem("bank_free")
    x_loaded = [sem(f"x_loaded{i}") for i in range(3)]
    const_loaded = sem("const_loaded")
    gain_loaded = sem("gain_loaded")
    dve_step = sem("dve_step")
    stage_end = sem("stage_end")
    norm_sems = {n: {k: sem(f"{k}_{n}") for k in ("squares", "variance", "deviation", "scaled", "high")
                     if (n, k) != ("final", "high")} for n in ("mix", "ffn", "final")}
    raw_ready = sem("raw_ready")
    roped = sem("roped")
    stored = [sem(f"stored{s}") for s in range(3)]
    sg_ready = sem("sg_ready")
    gate_ready = sem("gate_ready")
    gate_stored = [sem("gate_stored0"), sem("gate_stored1")]
    passed = [0]

    def end_stage(eng, n):
        eng.sem_inc(stage_end, 1)
        eng.wait_ge(stage_end, 4 * n)

    block = ctx.enter_context(nc.Block())

    def w_source(w):
        if w < W_PA:
            return w_in[0].rearrange("(k p) n -> p k n", p=128)[:, :, w * WN:(w + 1) * WN]
        if w < W_PB:
            return w_pa[0].rearrange("(k p) n -> p k n", p=128)[:, :, (w - W_PA) * WN:(w - W_PA + 1) * WN]
        if w < W_O:
            half, n = divmod(w - W_PB, 2)
            return w_pb[0].rearrange("(k p) n -> p k n", p=128)[:, half * KD:(half + 1) * KD, n * WN:(n + 1) * WN]
        if w < W_GU:
            return w_o[0].rearrange("(k p) n -> p k n", p=128)[:, :, (w - W_O) * WN:(w - W_O + 1) * WN]
        chunk, n = divmod(w - W_DN, 2)
        k0 = sum(DOWN_K[:chunk])
        return w_down[0].rearrange("(k p) n -> p k n", p=128)[:, k0:k0 + DOWN_K[chunk], n * WN:(n + 1) * WN]

    def load_half(sp, src, h, nk=KD):
        lo, hi = 4 * h, min(4 * h + 4, nk)
        mid = (lo + hi) // 2
        for a, b in ((lo, mid), (mid, hi)):
            sp.dma_start(stage[h][:, a - lo:b - lo, :], src[:, a:b, :]).then_inc(stage_loaded[h], 16)

    def load_w(sp, w):
        for h in range(2):
            if w >= 1:
                sp.wait_ge(w_split, 2 * (w - 1) + h + 1)
            load_half(sp, w_source(w), h, W_NK[w])

    def load_w_in(sp, i, w):
        col = i * (2 * WN) + w * WN
        src = w_in[0].rearrange("(k p) n -> p k n", p=128)[:, :, bass.ds(col, WN)]
        for h in range(2):
            sp.wait_ge(w_split, i * 4 + (2 * (w - 1) + h + 1))
            load_half(sp, src, h)

    def load_w_gu(sp, n):
        src = w_gu[0].rearrange("(k p) n -> p k n", p=128)
        for h in range(2):
            sp.wait_ge(w_split, n * 2 + (2 * (W_GU - 1) + h + 1))
            for u in range(2):
                sp.dma_start(stage[h][:, :, 256 * u:256 * u + 256],
                             src[:, 4 * h:4 * h + 4, bass.ds(n * 256 + u * FFN, 256)]).then_inc(stage_loaded[h], 16)

    def gpsimd_program(pool):
        def split(w, s, nk=KD, used=None):
            if used is not None:
                pool.wait_ge(bank_full, used)
            for h in range(2):
                lo, hi = 4 * h, min(4 * h + 4, nk)
                pairs = [(k, k + 2) for k in range(lo, hi, 2)]
                pool.wait_ge(stage_loaded[h], w * 32 + 32)
                for a, b in pairs:
                    src = stage[h][:, a - lo:b - lo, :]
                    last = nc.gpsimd.tensor_tensor(w_h[s][:, a:b, :], src, one.unsqueeze(1).to_broadcast([128, b - a, WN]),
                                                   ALU.mult)
                last.then_inc(w_high, 1)
                pool.wait_ge(w_high, w * 2 + (h + 1))
                for a, b in pairs:
                    last = nc.gpsimd.tensor_tensor(w_l[s][:, a:b, :], stage[h][:, a - lo:b - lo, :],
                                                   w_h[s][:, a:b, :].bitcast(F), ALU.subtract)
                last.then_inc(w_split, 1)

        nc.gpsimd.memset(ones[:, :], 1.0).then_inc(ones_set, 1)
        pool.wait_ge(ones_set, 1)
        split(0, 0)
        split(1, 1)

        def split_loop(w0, n):
            step = banks_before(w0 + 1) - banks_before(w0 - 1)
            for v in range(w0, w0 + 2 * n, 2):
                assert banks_before(v + 1) - banks_before(v - 1) == step or v + 2 >= w0 + 2 * n
                assert banks_before(v - 1) == banks_before(w0 - 1) + (v - w0) // 2 * step
                assert banks_before(v) == banks_before(w0) + (v - w0) // 2 * step
            with pool.Fori(0, n) as i:
                split(i * 2 + w0, w0 % 2, used=i * step + banks_before(w0 - 1))
                split(i * 2 + (w0 + 1), (w0 + 1) % 2, used=i * step + banks_before(w0))

        split_loop(2, 7)
        split_loop(16, 4)
        pool_powers(pool)
        pool_retention(pool)
        for w in range(W_PB, W_GU + 2):
            split(w, w % 2, used=banks_before(w - 1) if w - 2 != W_O + 1 else o1_place("O", SAMPLE) + 1)
        n_even = (N_GU - 2) // 2
        split_loop(W_GU + 2, n_even)
        for w in range(W_GU + 2 + 2 * n_even, N_W):
            split(w, w % 2, W_NK[w], used=banks_before(w - 1))

    def act_square(act, tag, src, t):
        p, squares = rows(t), norm_sems[tag]["squares"]
        if t:
            act.wait_ge(squares, t)
        nc.scalar.activation(edge[0:p, 2048:3072], src[0:p, t, :], ACT.Square,
                             accum_out=ss[0:p, t:t + 1]).then_inc(squares, 1)

    def act_deviation(act, tag, t):
        p, s = rows(t), norm_sems[tag]
        act.wait_ge(s["variance"], t + 1)
        nc.scalar.activation(rstd[0:p, t:t + 1], ss[0:p, t:t + 1], ACT.Sqrt).then_inc(s["deviation"], 1)

    def dve_rstd(dve, tag, t):
        p, s = rows(t), norm_sems[tag]
        v, y, z = ss[0:p, t:t + 1], rstd[0:p, t:t + 1], newton[0:p, t:t + 1]
        dve.wait_ge(s["squares"], t + 1)
        nc.vector.tensor_scalar(v, v, 1.0 / D, EPS, ALU.mult, ALU.add).then_inc(s["variance"], 1)
        dve.wait_ge(s["deviation"], t + 1)
        dstep.done(nc.vector.reciprocal(y, y))
        dstep.wait(dve)
        dstep.done(nc.vector.scalar_tensor_tensor(z, y, v, y, ALU.mult, ALU.mult))
        dstep.wait(dve)
        dstep.done(nc.vector.tensor_scalar(z, z, -0.5, 1.5, ALU.mult, ALU.add))
        dstep.wait(dve)
        dstep.done(nc.vector.tensor_tensor(y, y, z, ALU.mult))
        dstep.wait(dve)

    def dve_scale_tile(dve, tag, src, t, place):
        p, s = rows(t), norm_sems[tag]
        if t >= 2:
            dve.wait_ge(bank_full, place(1) + 1)
        nc.vector.scalar_tensor_tensor(edge[0:p, t % 2 * D:(t % 2 + 1) * D], src[0:p, t, :], rstd[0:p, t:t + 1],
                                       gain[0:p, :], ALU.mult, ALU.mult).then_inc(s["scaled"], 1)

    def pe_norm_tile(pe, tag, t, place):
        p = rows(t)
        pe.wait_ge(norm_sems[tag]["scaled"], t + 1)
        for b in range(2):
            g = place(b)
            pe.wait_ge(bank_free, g + 1)
            for k in range(4):
                f = t % 2 * D + (4 * b + k) * 128
                last = nc.tensor.transpose(psum[:, g % RING, 128 * k:128 * k + p], edge[0:p, f:f + 128], ident[0:p, 0:p])
            last.then_inc(bank_full, 1)

    def transposed(g, t):
        return psum[:, g % RING, :].rearrange("p (k n) -> p k n", k=4)[:, :, 0:rows(t)]

    def act_high_tile(act, tag, t, place, xh, xs):
        for b in range(2):
            g = place(b)
            act.wait_ge(bank_full, g + 1)
            if t == SAMPLE:
                nc.scalar.copy(xs[:, 4 * b:4 * b + 4, 0:TS], transposed(g, t))
            nc.scalar.copy(xh[:, 4 * b:4 * b + 4, t * 128:t * 128 + rows(t)],
                           transposed(g, t)).then_inc(norm_sems[tag]["high"], 1)

    def dve_low_tile(dve, tag, t, place, xh, xl, xs):
        for b in range(2):
            g = place(b)
            dve.wait_ge(norm_sems[tag]["high"], 2 * t + b + 1)
            ks = slice(4 * b, 4 * b + 4)
            high = xh[:, ks, t * 128:t * 128 + rows(t)].bitcast(F)
            if t == SAMPLE:
                nc.vector.tensor_tensor(xs[:, ks, TS:2 * TS], transposed(g, t), high, ALU.subtract)
            nc.vector.tensor_tensor(xl[:, ks, t * 128:t * 128 + rows(t)], transposed(g, t), high,
                                    ALU.subtract).then_inc(bank_free, 1)

    def pe_token_tile(pe, xh, xl, xs, s, split, g, nk=KD, ready=None, behind=None):
        for t in range(NT):
            count, bank = g(t)
            pe.wait_ge(bank_free, count + 1)
            for k in range(nk):
                if t == 0 and k % 4 == 0:
                    pe.wait_ge(w_split, split + k // 4)
                if ready is not None and ready(t, k) is not None:
                    pe.wait_ge(*ready(t, k))
                at = slice(t * 128, t * 128 + 128)
                if t == SAMPLE:
                    passes = ((xs[:, k, :], w_h), (xs[:, k, :], w_l))
                else:
                    passes = ((xh[:, k, at], w_h), (xl[:, k, at], w_h), (xh[:, k, at], w_l))
                for n, (x, w) in enumerate(passes):
                    last = nc.tensor.matmul(psum[:, bank, :], x, w[s][:, k, :], start=k == 0 and n == 0,
                                            stop=k == nk - 1 and n == len(passes) - 1)
            last.then_inc(bank_full, 1)
            if behind is not None:
                behind(t)

    def pe_feature_tile(pe, xh, xl, s, split, g, order=range(4), free=None, ready=None, beside=None):
        for j, m in enumerate(order):
            for c in range(3):
                count, bank = g(3 * j + c)
                if c == 0:
                    pe.wait_ge(bank_free, count + 3)
            for k in range(KD):
                if beside is not None:
                    beside(j, k)
                if j == 0 and k % 4 == 0:
                    pe.wait_ge(w_split, split + k // 4)
                if j == 0 and ready is not None:
                    pe.wait_ge(*ready(k))
                for n, (w, x) in enumerate(((w_h, xh), (w_h, xl), (w_l, xh))):
                    for c, (a, width) in enumerate(CHUNKS):
                        ins = nc.tensor.matmul(psum[:, g(3 * j + c)[1], 0:width], w[s][:, k, m * 128:(m + 1) * 128],
                                               x[:, k, a:a + width], start=k == 0 and n == 0,
                                               stop=k == KD - 1 and n == 2)
                        if k == KD - 1 and n == 2:
                            ins.then_inc(bank_full, 1)
                if free is not None and j == 3 and k < KD - 1:
                    ins.then_inc(free, 1)

    def sp_load_gain(sp, g):
        sp.dma_start(gain[:, :], g.partition_broadcast(128)).then_inc(gain_loaded, 16)

    def token_rows(x, xs, t):
        return x[0, t * 128:(t + 1) * 128, :] if t < SAMPLE else xs.rearrange("b t d -> (b t) d")

    def sp_project(sp):
        for t in range(NT):
            sp.dma_start(x_rows[0:rows(t), t, :], token_rows(x_prompt, x_sample, t)).then_inc(x_loaded[t // 3], 16)
        sp_load_gain(sp, norm_mix_g[0])
        sp.dma_start(ident[:, :], c_ident).then_inc(const_loaded, 16)
        sp.dma_start(rope_diff[:, :, :, :], c_rope_diff).then_inc(const_loaded, 16)
        with nc.allow_non_contiguous_dma(reason="16 biases a partition"):
            sp.dma_start(bias[:, :], b_gate[0].rearrange("(m p) -> p m", p=128)).then_inc(const_loaded, 16)
        load_w(sp, 0)
        load_w(sp, 1)
        for s in range(3):
            sp.sem_inc(stored[s], 16)
        sp.wait_ge(norm_sems["mix"]["scaled"], NT)
        sp.dma_start(rope_ret, c_rope_ret).then_inc(const_loaded, 16)

        def store(i, j, t, n_roped, n_raw):
            u = NT * j + t
            if n_roped is not None:
                sp.wait_ge(roped, n_roped)
            if n_raw is not None:
                sp.wait_ge(raw_ready, n_raw)
            col = i * (2 * WN) + j * WN
            sp.dma_start(proj[t * 128:t * 128 + rows(t), bass.ds(col, WN)],
                         edge[0:rows(t), u % 3 * WN:(u % 3 + 1) * WN]).then_inc(stored[u % 3], 16)

        def tiles(first, n, rotate, roped_before):
            with sp.Fori(first, first + n) as i:
                for j in range(2):
                    for t in range(NT):
                        if rotate:
                            store(i, j, t, (i - first) * (2 * NT) + (roped_before + NT * j + t + 1), None)
                        elif t == SAMPLE:
                            store(i, j, t, (i - first) * 2 + (roped_before + j + 1), None)
                        else:
                            store(i, j, t, None, i * (2 * NT) + (NT * j + t + 1))
                        if t == 4:
                            load_w_in(sp, i, j + 2)

        tiles(0, 2, True, 0)
        tiles(2, 1, False, 4 * NT)
        tiles(3, 2, True, 4 * NT + 2)
        tiles(5, 2, False, 8 * NT + 2)
        for s in range(3):
            sp.wait_ge(stored[s], 16 * (1 + N_TM * NT // 3))

        for s in range(2):
            sp.sem_inc(gate_stored[s], 16)
        sp_n_begin(sp)
        with sp.Fori(0, N_FM // 2 - 1) as i:
            for m in range(8):
                sp_n_unit(sp, i, m, False)
                sp_store_gate(sp, i, m)
                if m % 4 == 1:
                    load_w_in(sp, i, N_TM + m // 4 + 2)
            sp_n_end(sp, i)
        i = N_FM // 2 - 1
        for m in range(8):
            sp_n_unit(sp, i, m, True)
            sp_store_gate(sp, i, m)
            if m % 4 == 1:
                load_w(sp, W_PA + m // 4)
        sp_n_end(sp, i)
        for s in range(4):
            sp.wait_ge(ns_stored[s], 16 * (1 + RH * 2))
        sp.wait_ge(n_stored, 16 * (1 + RH))
        for s in range(2):
            sp.wait_ge(gate_stored[s], 16 * (1 + 4 * N_FM // 2))

    def sp_store_gate(sp, i, m):
        s = m % 2
        sp.wait_ge(gate_ready, i * 8 + (m + 1))
        sp.dma_start(gates[bass.ds(i * D + m * 128, 128), :], edge[:, s * T:(s + 1) * T]).then_inc(gate_stored[s], 16)

    G_TM = 2 * NT
    G_FM = banks_before(W_FM)

    def pe_project(pe):
        pe.wait_ge(const_loaded, 48)
        for t in range(NT):
            pe_norm_tile(pe, "mix", t, lambda b: 2 * t + b)
        pe.wait_ge(bank_free, RING + 2 * NT)
        with pe.Fori(0, N_TM // 2) as i:
            for j in range(2):
                pe_token_tile(pe, xt_h1, xt_l1, xs_hl1, j, i * 4 + (2 * j + 1),
                              lambda t: (i * (2 * NT) + (G_TM + NT * j + t), (G_TM + NT * j + t) % RING))
        with pe.Fori(0, N_FM // 2) as i:
            for j in range(2):
                pe_feature_tile(pe, xt_h1, xt_l1, j, i * 4 + (2 * (W_FM + j) + 1),
                                lambda c: (i * 24 + (G_FM + 12 * j + c), (G_FM + 12 * j + c) % RING),
                                beside=lambda m, k: pe_n_piece(pe, i, 4 * j + m, k))
            pe_n_end(pe, i)
        pe.wait_ge(bank_full, banks_before(W_PA))

    def act_project(act):
        for t in range(NT + 2):
            if 1 <= t <= NT:
                act_deviation(act, "mix", t - 1)
            if t < NT:
                act.wait_ge(x_loaded[t // 3], 48)
                act_square(act, "mix", x_rows, t)
            if t >= 2:
                act_high_tile(act, "mix", t - 2, lambda b: 2 * (t - 2) + b, xt_h1, xs_hl1)
        with act.Fori(0, N_TM // 2) as i:
            for u in range(2 * NT):
                t, g = u % NT, G_TM + u
                act.wait_ge(bank_full, i * (2 * NT) + (g + 1))
                act.wait_ge(stored[u % 3], i * (16 * 6) + 16 * (u // 3 + 1))
                slot = edge[0:rows(t), u % 3 * WN:(u % 3 + 1) * WN]
                nc.scalar.copy(slot, psum[0:rows(t), g % RING, :]).then_inc(raw_ready, 1)
                if t == SAMPLE:
                    act.wait_ge(raw_ready, i * (2 * NT) + (u + 1))
                    nc.scalar.copy(edge[0:TS, 2560:3072], psum[TS:2 * TS, g % RING, :]).then_inc(half_ready, 1)
                    act.wait_ge(half_ready, i * 2 + (u // NT + 1))
                else:
                    act.wait_ge(raw_ready, i * (2 * NT) + (u + 1))
                act.sem_inc(bank_free, 1)
        act.wait_ge(roped, 8 * NT + 6)
        with act.Fori(0, N_FM // 4) as i:
            for c in range(24):
                g = G_FM + c
                if c % 3 == 0:
                    act_n_unit(act, i, c // 3)
                act.wait_ge(bank_full, i * 24 + (g + 1))
                act.wait_ge(bank_free, i * 24 + (RING + g - 2))
                nc.scalar.activation(edge[:, 2176 + 384 * (c % 3):2176 + 384 * (c % 3) + CHUNKS[c % 3][1]],
                                     psum[:, g % RING, 0:CHUNKS[c % 3][1]], ACT.Sigmoid).then_inc(sg_ready, 1)
        act.wait_ge(bank_free, RING + G_FM + 48)
        act.wait_ge(gate_stored[1], 16 * 9)
        for m in range(16):
            act_n_unit(act, 2 + m // 8, m % 8)
            act.wait_ge(gate_stored[m % 2], 16 * (8 + m // 2 + 1))
            for c, (a, width) in enumerate(CHUNKS):
                g = G_FM + 48 + 3 * m + c
                act.wait_ge(bank_full, g + 1)
                nc.scalar.activation(edge[:, m % 2 * T + a:m % 2 * T + a + width], psum[:, g % RING, 0:width],
                                     ACT.Sigmoid, bias=bias[:, m:m + 1]).then_inc(bank_free, 1)
            act.wait_ge(bank_free, RING + G_FM + 48 + 3 * m + 3)
            act.sem_inc(gate_ready, 1)

    half_ready = sem("half_ready")
    dstep = Count(dve_step)

    def dve_project(dve):
        dve.sem_inc(bank_free, RING)
        dve.wait_ge(gain_loaded, 16)
        for t in range(NT + 1):
            if t < NT:
                dve_rstd(dve, "mix", t)
                dve_scale_tile(dve, "mix", x_rows, t, lambda b: 2 * (t - 2) + b)
            if t:
                dve_low_tile(dve, "mix", t - 1, lambda b: 2 * (t - 1) + b, xt_h1, xt_l1, xs_hl1)
        dve.wait_ge(const_loaded, 48)

        def combine(i, u, n_half):
            p = edge[0:TS, u % 3 * WN:(u % 3 + 1) * WN]
            dve.wait_ge(half_ready, n_half)
            return nc.vector.tensor_tensor(p, p, edge[0:TS, 2560:3072], ALU.add)

        def rotate_diff(u):
            p, t = rows(u % NT), u % NT
            slot = edge[0:p, u % 3 * WN:(u % 3 + 1) * WN].rearrange("p (g d) -> p g d", d=DHD)
            by_cos = edge[0:p, 1536:1664].rearrange("p (g d) -> p g d", d=16)
            by_sin = edge[0:p, 2048:2176].rearrange("p (g d) -> p g d", d=16)
            cos = rope_diff[0:p, t, 0, :].unsqueeze(1).to_broadcast([p, 8, 16])
            sin = rope_diff[0:p, t, 1, :].unsqueeze(1).to_broadcast([p, 8, 16])
            nc.vector.tensor_tensor(by_cos, slot[:, :, 0:16], cos, ALU.mult)
            nc.vector.tensor_tensor(by_sin[:, :, 0:8], slot[:, :, 8:16], sin[:, :, 0:8], ALU.mult)
            dstep.done(nc.vector.tensor_tensor(by_sin[:, :, 8:16], slot[:, :, 0:8], sin[:, :, 8:16], ALU.mult))
            dstep.wait(dve)
            nc.vector.tensor_tensor(slot[:, :, 0:16], by_cos, by_sin, ALU.add).then_inc(roped, 1)

        def rotate_ret(u):
            p, t = rows(u % NT), u % NT
            flat = edge[0:p, u % 3 * WN:(u % 3 + 1) * WN]
            slot = flat.rearrange("p (h d) -> p h d", d=RK)
            pair = flat.rearrange("p (h j c) -> p h j c", c=2, j=RK // 2)
            by_cos = edge[0:p, 1536:2048].rearrange("p (h d) -> p h d", d=RK)
            by_sin = edge[0:p, 2048:2560].rearrange("p (h j c) -> p h j c", c=2, j=RK // 2)
            cos = rope_ret[0:p, t, 0, :].unsqueeze(1).to_broadcast([p, 2, RK])
            sin = rope_ret[0:p, t, 1, :].rearrange("p (j c) -> p j c", c=2).unsqueeze(1)
            nc.vector.tensor_tensor(by_cos, slot, cos, ALU.mult)
            for c in range(2):
                last = nc.vector.tensor_tensor(by_sin[:, :, :, c], pair[:, :, :, 1 - c],
                                               sin[:, :, :, c].to_broadcast([p, 2, RK // 2]), ALU.mult)
            dstep.done(last)
            dstep.wait(dve)
            nc.vector.tensor_tensor(flat, edge[0:p, 1536:2048], edge[0:p, 2048:2560], ALU.add).then_inc(roped, 1)

        def rotations(first, n, rotate, roped_before):
            with dve.Fori(first, first + n) as i:
                dstep.loop(i - first, 2 * NT + 2)
                for u in range(2 * NT):
                    dve.wait_ge(raw_ready, i * (2 * NT) + (u + 1))
                    dve.wait_ge(roped, (i - first) * (2 * NT) + (roped_before + u))
                    if u % NT == SAMPLE:
                        dstep.done(combine(i, u, i * 2 + (u // NT + 1)))
                        dstep.wait(dve)
                    rotate(u)
                dstep.end(n)

        def copies(first, n):
            with dve.Fori(first, first + n) as i:
                for j in range(2):
                    combine(i, NT * j + SAMPLE, i * 2 + (j + 1)).then_inc(roped, 1)

        rotations(0, 2, rotate_diff, 0)
        copies(2, 1)
        dve.wait_ge(const_loaded, 64)
        rotations(3, 2, rotate_ret, 4 * NT + 2)
        copies(5, 2)
        dve.wait_ge(roped, 8 * NT + 6)
        dstep.done(nc.vector.memset(q_own, 0.0))
        dstep.wait(dve)
        with dve.Fori(0, N_FM // 4) as i:
            for c in range(24):
                g, m = G_FM + c, c // 3
                if c % 3 == 0:
                    dve_n_unit(dve, i, m)
                    dve.wait_ge(gate_stored[m % 2], i * 64 + 16 * (m // 2 + 1))
                dve.wait_ge(sg_ready, i * 24 + (c + 1))
                a, width = CHUNKS[c % 3]
                nc.vector.tensor_tensor(edge[:, m % 2 * T + a:m % 2 * T + a + width], psum[:, g % RING, 0:width],
                                        edge[:, 2176 + 384 * (c % 3):2176 + 384 * (c % 3) + width],
                                        ALU.mult).then_inc(bank_free, 1)
                if c % 3 == 2:
                    dve.wait_ge(bank_free, i * 24 + (RING + g + 1))
                    dve.sem_inc(gate_ready, 1)
            dve_n_end(dve, i)
        for i in range(2, RH):
            for m in range(DB):
                dve_n_unit(dve, i, m)
            dve_n_end(dve, i)

    NQ = TP // 128
    STEPS = 2 * NQ
    st = ExitStack()
    q_in = [sb(f"q_in{s}", [128, NQ, 128], F, st) for s in range(2)]
    k_in = [sb(f"k_in{s}", [128, NQ, 128], F, st) for s in range(2)]
    v_in = [sb(f"v_in{s}", [128, NQ, 128], F, st) for s in range(2)]
    q_t = [sb(f"q_t{s}", [128, TP], F, st) for s in range(2)]
    k_t = [sb(f"k_t{s}", [128, TP], F, st) for s in range(2)]
    prob = [sb(f"prob{s}", [128, 2, TP], F, st) for s in range(2)]
    mix = [sb(f"mix{s}", [128, TP], F, st) for s in range(2)]
    mix_t = [sb(f"mix_t{s}", [128, TP], F, st) for s in range(2)]
    o_head = [sb(f"o_head{s}", [128, NQ, 128], F, st) for s in range(2)]
    a_out = sb("a_out", [128, TP], F, st)
    causal = sb("causal", [128, 128], F, st)
    lam_in = sb("lam_in", [128, 4, DHD], F, st)
    lam_prod = sb("lam_prod", [128, 2, DHD], F, st)
    lam_sum = sb("lam_sum", [128, 2], F, st)
    lam_exp = sb("lam_exp", [128, 2], F, st)
    neg_max = [sb(f"neg_max{s}", [128, 2], F, st) for s in range(2)]
    sums = [sb(f"sums{s}", [128, 2], F, st) for s in range(2)]
    recip = [sb(f"recip{s}", [128, 2], F, st) for s in range(2)]
    coef = [sb(f"coef{s}", [128, 1], F, st) for s in range(2)]
    o_var = sb("o_var", [128, NQ], F, st)
    o_rstd = sb("o_rstd", [128, NQ], F, st)
    st.close()

    lam_step = sem("lam_step")
    qkv_loaded = [sem("qkv_loaded0"), sem("qkv_loaded1")]
    score_full = [sem("score_full0"), sem("score_full1")]
    score_max = [sem("score_max0"), sem("score_max1")]
    score_exp = [sem("score_exp0"), sem("score_exp1")]
    mix_ready = sem("mix_ready")
    tr_full = sem("tr_full")
    tr_free = sem("tr_free")
    out_full = sem("out_full")
    out_read = sem("out_read")
    var_ready = sem("var_ready")
    rstd_ready = sem("rstd_ready")
    head_normed = sem("head_normed")
    a_stored = sem("a_stored")
    copied = sem("copied")

    EXTRA = {4: ["K", "Q"], 10: ["O"], 12: ["K", "Q"], 15: ["O"]}

    def transposes_in_body(last):
        plan = []
        for n in range(STEPS):
            plan += [("W", n)] + [(kind, n) for kind in EXTRA.get(n, []) if not (last and n == 12 and kind != "O")]
        return plan

    def place(i, base, per, k):
        return base + k if i is None else i * per + (base + k)

    N_BODY = DH // 2
    TR_BODY = len(transposes_in_body(False))
    TR_LAST = 2 + TR_BODY * (N_BODY - 1)

    def bodies(eng, body):
        with eng.Fori(0, N_BODY - 1) as i:
            body(i, False)
        body(N_BODY - 1, True)

    def tr_index(i, last, what):
        return i * TR_BODY + (2 + transposes_in_body(last).index(what))

    def sp_attention(sp):
        sp.dma_start(causal[:, :], c_causal).then_inc(const_loaded, 16)
        for n, v in enumerate((lambda_q1, lambda_q2, lambda_k1, lambda_k2)):
            sp.dma_start(lam_in[:, n, :], v[0].partition_broadcast(128)).then_inc(const_loaded, 16)
        with nc.allow_non_contiguous_dma(reason="one gain a partition"):
            sp.dma_start(sub_gain[:, :], subln_g[0].rearrange("(p o) -> p o", o=1)).then_inc(const_loaded, 16)

        def load(h, s):
            for x, col in ((k_in, KA), (q_in, QA), (v_in, VA)):
                sp.dma_start(x[s][:, :, :], proj[0:TP, bass.ds(h * 128 + col, 128)].rearrange(
                    "(b p) d -> p b d", p=128)).then_inc(qkv_loaded[s], 16)

        load(0, 0)
        load(1, 1)
        for dst, dst_new, col in ((k_prompt[0, 0].rearrange("t h c d -> t (h c d)"),
                                   k_sample[0].rearrange("b t h c d -> (b t) (h c d)"), KA),
                                  (v_prompt[0, 0].rearrange("t h d -> t (h d)"),
                                   v_sample[0].rearrange("b t h d -> (b t) (h d)"), VA)):
            sp.dma_start(dst, proj[0:TP, col:col + D]).then_inc(copied, 16)
            sp.dma_start(dst_new, proj[TP:T, col:col + D]).then_inc(copied, 16)

        def body(i, last):
            for j in range(2):
                if not last:
                    sp.wait_ge(out_full, i * STEPS + NQ * (j + 1))
                    load(i * 2 + (2 + j), j)
                sp.wait_ge(a_ready, i * 2 + (j + 1))
                sp.dma_start(a_t[bass.ds(i * 256 + j * 128, 128), 0:TP], a_out[:, :]).then_inc(a_stored, 16)
        bodies(sp, body)
        sp.wait_ge(a_stored, 16 * DH)
        sp.wait_ge(copied, 64)

    a_ready = sem("a_ready")

    def pe_attention(pe):
        def transposes(tr, blocks, wait):
            pe.wait_ge(tr_free, tr)
            pe.wait_ge(*wait)
            for b, x in enumerate(blocks):
                last = nc.tensor.transpose(psum[:, 4 + b // 4, b % 4 * 128:b % 4 * 128 + 128], x, ident[:, :])
            last.then_inc(tr_full, 1)

        def scores(step, n, c):
            s, qb, r = n // NQ % 2, n % NQ, slice(c * DHD, (c + 1) * DHD)
            pe.wait_ge(score_exp[c], step)
            for a in range(0, (qb + 1) * 128, 512):
                width = min(512, (qb + 1) * 128 - a)
                last = nc.tensor.matmul(psum[:, 2 * c + a // 512, 0:width], q_t[s][r, qb * 128:(qb + 1) * 128],
                                        k_t[s][r, a:a + width], start=True, stop=True)
            last.then_inc(score_full[c], 1)

        def values(step, n):
            s, qb = n // NQ, n % NQ
            pe.wait_ge(mix_t_ready, step + 1)
            pe.wait_ge(out_read, step + 1)
            for b in range(qb + 1):
                last = nc.tensor.matmul(psum[:, 6 + n % 2, 0:DV], mix_t[n % 2][:, b * 128:(b + 1) * 128],
                                        v_in[s][:, b, :], start=b == 0, stop=b == qb)
            last.then_inc(out_full, 1)

        def heads_kq(tr, s, count):
            transposes(tr, [k_in[s][:, b, :] for b in range(NQ)], (qkv_loaded[s], count))
            transposes(tr + 1, [q_in[s][:, b, :] for b in range(NQ)], (qkv_loaded[s], count))
            return tr + 2

        heads_kq(0, 0, 48)
        pe.wait_ge(tr_free, 2)
        scores(0, 0, 0)
        scores(0, 0, 1)

        def body(i, last):
            for n in range(STEPS):
                step, final = i * STEPS + n, last and n == STEPS - 1
                if not final:
                    if n % NQ == NQ - 1:
                        pe.wait_ge(tr_free, tr_index(i, last, ("Q", n - 3)) + 1)
                    scores(step + 1, (n + 1) % STEPS, 0)
                tr = tr_index(i, last, ("W", n))
                transposes(tr, [mix[n % 2][:, b * 128:(b + 1) * 128] for b in range(n % NQ + 1)],
                           (mix_ready, step + 1))
                if not final:
                    scores(step + 1, (n + 1) % STEPS, 1)
                values(step, n)
                for kind in EXTRA.get(n, []):
                    if kind == "K" and not (last and n == 12):
                        s = 1 - n // NQ
                        heads_kq(tr + 1, s, i * 48 + (48 if s else 96))
                    if kind == "O":
                        s = n // NQ if n == 15 else 0
                        transposes(tr + 1, [o_head[s][:, b, :] for b in range(NQ)],
                                   (head_normed, i * 2 + (s + 1)))
        bodies(pe, body)
        pe.wait_ge(tr_free, TR_LAST + len(transposes_in_body(True)))

    mix_t_ready = sem("mix_t_ready")

    def act_attention(act):
        def exps(step, n, c, first=None):
            width = (n % NQ + 1) * 128
            act.wait_ge(score_max[c], step + 1)
            if first is None:
                act.wait_ge(mix_ready, step - 1)
            nc.scalar.activation(prob[n % 2][:, c, 0:width],
                                 psum[:, 2 * c:2 * c + 2, :].rearrange("p b n -> p (b n)")[:, 0:width],
                                 ACT.Exp, bias=neg_max[n % 2][:, c:c + 1],
                                 accum_out=sums[n % 2][:, c:c + 1]).then_inc(score_exp[c], 1)

        def evacuate(tr, out, width):
            act.wait_ge(tr_full, tr + 1)
            nc.scalar.copy(out[:, 0:width], psum[:, 4:6, :].rearrange("p b n -> p (b n)")[:, 0:width]).then_inc(tr_free, 1)

        act.sem_inc(out_read, 2)
        act.wait_ge(lam_step, 1)
        nc.scalar.activation(lam_exp[:, :], lam_sum[:, :], ACT.Exp).then_inc(lam_step, 1)
        evacuate(0, k_t[0], TP)
        exps(0, 0, 0, True)
        exps(0, 0, 1, True)

        def body(i, last):
            for n in range(STEPS):
                step, final = i * STEPS + n, last and n == STEPS - 1
                tr = tr_index(i, last, ("W", n))
                width = (n % NQ + 1) * 128
                act.wait_ge(tr_full, tr + 1)
                nc.scalar.copy(mix_t[n % 2][:, 0:width],
                               psum[:, 4:6, :].rearrange("p b n -> p (b n)")[:, 0:width]).then_inc(mix_t_ready, 1)
                act.wait_ge(mix_t_ready, step + 1)
                act.sem_inc(tr_free, 1)
                if not final:
                    exps(step + 1, n + 1, 0)
                    exps(step + 1, n + 1, 1)
                act.wait_ge(out_full, step + 1)
                if n % NQ == 0:
                    act.wait_ge(head_used, i * 2 + n // NQ)
                nc.scalar.activation(o_head[n // NQ][:, n % NQ, :], psum[:, 6 + n % 2, 0:DV], ACT.Copy,
                                     scale=recip[n % 2][:, 0:1]).then_inc(out_read, 1)
                if n == 4 or (n == 12 and not last):
                    evacuate(tr + 1, k_t[1 - n // NQ], TP)

        bodies(act, body)

    head_used = sem("head_used")

    def dve_attention(dve):
        dve.sem_inc(head_used, 1)
        dve.wait_ge(const_loaded, 64 + 16 * 6)
        dstep.done(nc.vector.tensor_tensor(lam_prod[:, :, :], lam_in[:, 0:2, :], lam_in[:, 2:4, :], ALU.mult))
        dstep.wait(dve)
        nc.vector.tensor_reduce(lam_sum[:, :], lam_prod[:, :, :], AX.X, ALU.add).then_inc(lam_step, 1)
        dve.wait_ge(lam_step, 2)
        dstep.done(nc.vector.tensor_tensor(neg_lam[:, :], lam_exp[:, 1:2], lam_exp[:, 0:1], ALU.subtract))
        dstep.wait(dve)
        dstep.done(nc.vector.tensor_scalar(neg_lam[:, :], neg_lam[:, :], -LAM_INIT, None, ALU.add))
        dstep.done(nc.vector.tensor_scalar(sub_gain[:, :], sub_gain[:, :], 1.0 - LAM_INIT, None, ALU.mult))
        dstep.wait(dve)

        def maxima(step, n, c):
            qb = n % NQ
            flat = psum[:, 2 * c:2 * c + 2, :].rearrange("p b n -> p (b n)")
            dve.wait_ge(score_full[c], step + 1)
            dstep.done(nc.vector.tensor_tensor(flat[:, qb * 128:(qb + 1) * 128], flat[:, qb * 128:(qb + 1) * 128],
                                               causal[:, :], ALU.add))
            dstep.wait(dve)
            nc.vector.tensor_reduce(neg_max[n % 2][:, c:c + 1], flat[:, 0:(qb + 1) * 128], AX.X, ALU.max,
                                    negate=True).then_inc(score_max[c], 1)

        def weights(step, n):
            s, width = n % 2, (n % NQ + 1) * 128
            for c in range(2):
                dve.wait_ge(score_exp[c], step + 1)
            dve.wait_ge(out_read, step + 1)
            dstep.done(nc.vector.reciprocal(recip[s][:, :], sums[s][:, :]))
            dstep.wait(dve)
            dstep.done(nc.vector.scalar_tensor_tensor(coef[s][:, :], sums[s][:, 0:1], recip[s][:, 1:2],
                                                      neg_lam[:, :], ALU.mult, ALU.mult))
            dstep.wait(dve)
            nc.vector.scalar_tensor_tensor(mix[s][:, 0:width], prob[s][:, 1, 0:width], coef[s][:, :],
                                           prob[s][:, 0, 0:width], ALU.mult, ALU.add).then_inc(mix_ready, 1)

        def queries(tr, s):
            dve.wait_ge(tr_full, tr + 1)
            nc.vector.tensor_scalar(q_t[s][:, :], psum[:, 4:6, :].rearrange("p b n -> p (b n)"), DHD ** -0.5, None,
                                    ALU.mult).then_inc(tr_free, 1)

        queries(1, 0)
        maxima(0, 0, 0)
        maxima(0, 0, 1)

        def one_body(i, last):
            for n in range(STEPS):
                step, final = i * STEPS + n, last and n == STEPS - 1
                tr = tr_index(i, last, ("W", n))
                weights(step, n)
                if not final:
                    maxima(step + 1, n + 1, 0)
                    maxima(step + 1, n + 1, 1)
                if n == 4 or (n == 12 and not last):
                    queries(tr + 2, 1 - n // NQ)
                if n in (8, 15):
                    variance(i, n // 15)
                if n in (9, 15):
                    normalise(i, n // 15)
                if n in (10, 15):
                    output(i, n // 15, tr + 1)

        def variance(i, j):
            dve.wait_ge(out_read, i * STEPS + (2 + NQ * (j + 1)))
            dve.wait_ge(a_stored, i * 32 + 16 * j)
            square = a_out[:, :].rearrange("p (b d) -> p b d", d=128)
            dstep.done(nc.vector.tensor_tensor(square, o_head[j][:, :, :], o_head[j][:, :, :], ALU.mult))
            dstep.wait(dve)
            dstep.done(nc.vector.tensor_reduce(o_var[:, :], square, AX.X, ALU.add))
            dstep.wait(dve)
            nc.vector.tensor_scalar(o_var[:, :], o_var[:, :], 1.0 / DV, EPS, ALU.mult, ALU.add).then_inc(var_ready, 1)

        def normalise(i, j):
            dve.wait_ge(rstd_ready, i * 2 + (j + 1))
            nc.vector.tensor_tensor(o_head[j][:, :, :], o_head[j][:, :, :],
                                    o_rstd[:, :].unsqueeze(2).to_broadcast([128, NQ, 128]),
                                    ALU.mult).then_inc(head_normed, 1)

        def output(i, j, tr):
            dve.wait_ge(tr_full, tr + 1)
            nc.vector.tensor_scalar(a_out[:, :], psum[:, 4:6, :].rearrange("p b n -> p (b n)"), sub_gain[:, :], None,
                                    ALU.mult).then_inc(head_used, 1)
            dve.wait_ge(head_used, i * 2 + (j + 2))
            dve.sem_inc(tr_free, 1)
            dve.sem_inc(a_ready, 1)

        with dve.Fori(0, N_BODY - 1) as i:
            dstep.loop(i, 4 * STEPS + 4)
            one_body(i, False)
            dstep.end(N_BODY - 1)
        one_body(N_BODY - 1, True)

    def pool_powers(pool):
        nc.gpsimd.memset(exponent[:, :], -0.5).then_inc(ones_set, 1)
        pool.wait_ge(ones_set, 2)
        with pool.Fori(0, DH) as i:
            pool.wait_ge(var_ready, i + 1)
            nc.gpsimd.tensor_tensor(o_rstd[:, :], o_var[:, :], exponent[:, 0:NQ], ALU.pow).then_inc(rstd_ready, 1)

    st = ExitStack()
    k_page = [sb(f"k_page{s}", [128, NPG, D], F, st) for s in range(2)]
    v_page = [sb(f"v_page{s}", [128, NPG, D], F, st) for s in range(2)]
    q_new = sb("q_new", [TS, D], F, st)
    k_new = sb("k_new", [TS, D], F, st)
    v_new = sb("v_new", [TS, D], F, st)
    q_new_t = sb("q_new_t", [128, DH, TS], F, st)
    k_new_t = sb("k_new_t", [128, DH, TS], F, st)
    q_wide = [sb(f"q_wide{s}", [128, DH * 144], F, st) for s in range(2)]
    page_t = [sb(f"page_t{s}", [128, PAST], F, st) for s in range(2)]
    s_prob = [sb(f"s_prob{s}", [128, PAST + TS], F, st) for s in range(2)]
    s_comb = [sb(f"s_comb{s}", [128, TS], F, st) for s in range(2)]
    s_mix_t = [sb(f"s_mix_t{s}", [128, NPG + 1, TS], F, st) for s in range(2)]
    s_neg_max = [sb(f"s_neg_max{s}", [128, 1], F, st) for s in range(2)]
    s_sum = [sb(f"s_sum{s}", [128, 1], F, st) for s in range(2)]
    s_recip = sb("s_recip", [128, 1], F, st)
    s_sign = sb("s_sign", [128, 1], F, st)
    comb = sb("comb", [128, TS + 2], F, st)
    new_mask = sb("new_mask", [128, DB, TS], F, st)
    o_new = sb("o_new", [128, DH, TS], F, st)
    o_square = sb("o_square", [128, DH, TS], F, st)
    ones_sq = sb("ones_sq", [128, 128], F, st)
    pages = sb("pages", [1, DB * NPG], I32, st)
    st.close()

    new_loaded = sem("new_loaded")
    kp_loaded = [sem("kp_loaded0"), sem("kp_loaded1")]
    vp_loaded = [sem("vp_loaded0"), sem("vp_loaded1")]
    new_full = sem("new_full")
    new_t_ready = [sem("new_k_ready"), sem("new_q_ready")]
    wide_ready = sem("wide_ready")
    page_full = sem("page_full")
    page_ready = [sem("page_ready0"), sem("page_ready1")]
    s_full = sem("s_full")
    s_max = sem("s_max")
    s_exp = sem("s_exp")
    s_comb_ready = sem("s_comb_ready")
    s_mix_full = sem("s_mix_full")
    s_mix_ready = sem("s_mix_ready")
    s_out_full = sem("s_out_full")
    s_out_read = sem("s_out_read")
    s_square = sem("s_square")
    s_total = sem("s_total")
    s_var = sem("s_var")
    s_rstd = sem("s_rstd")
    s_a_ready = sem("s_a_ready")
    s_a_stored = sem("s_a_stored")
    S_BODY = DB // 2

    def s_bodies(eng, body):
        with eng.Fori(0, S_BODY - 1) as i:
            body(i, False)
        body(S_BODY - 1, True)

    def sp_sampled(sp):
        sp.dma_start(pages[:, :], page_table.rearrange("(o b) n -> o (b n)", o=1)).then_inc(const_loaded, 16)
        for x, col in ((q_new, QA), (k_new, KA), (v_new, VA)):
            sp.dma_start(x[:, :], proj[TP:T, col:col + D]).then_inc(new_loaded, 16)
        sp.dma_start(comb[:, :], c_comb).then_inc(new_loaded, 16)
        sp.dma_start(new_mask[:, :, :], c_new_mask).then_inc(new_loaded, 16)
        sp.wait_ge(const_loaded, 64 + 16 * 7)

        def load(i, n):
            page = [sp.value_load(pages[0:1, bass.ds(i * (2 * NPG) + (n * NPG + p), 1)], min_val=0, max_val=N_PHYS - 1)
                    for p in range(NPG)]
            for x, cache, loaded, used in ((k_page, cache_k[0].rearrange("n p h c d -> n p (h c d)"), kp_loaded, s_full),
                                           (v_page, cache_v[0].rearrange("n p h d -> n p (h d)"), vp_loaded, s_out_full)):
                if n >= 2:
                    sp.wait_ge(used, i * 2 + (n - 1))
                for p in range(NPG):
                    sp.dma_start(x[n % 2][:, p, :], cache[bass.ds(page[p], 1), :, :].rearrange("o p d -> (o p) d")).then_inc(
                        loaded[n % 2], 16)

        load(0, 0)
        load(0, 1)
        with sp.Fori(0, S_BODY - 1) as i:
            load(i, 2)
            load(i, 3)
        sp.wait_ge(s_a_ready, 1)
        sp.dma_start(a_t.rearrange("(h e) n -> e h n", e=DV)[:, :, TP:T], o_square[:, :, :]).then_inc(s_a_stored, 16)
        sp.wait_ge(s_a_stored, 16)

    def pe_sampled(pe):
        pe.wait_ge(new_loaded, 80)
        for b, x in enumerate((k_new, q_new)):
            for h in range(DH):
                last = nc.tensor.transpose(psum[:, b, h * TS:(h + 1) * TS], x[:, h * 128:(h + 1) * 128], ident[0:TS, 0:TS])
            last.then_inc(new_full, 1)
        pe.wait_ge(new_t_ready[0], 1)
        pe.wait_ge(new_t_ready[1], 1)

        def scores(i, n):
            s, seq = n % 2, i * 2 + n
            pe.wait_ge(wide_ready, seq + 1)
            pe.wait_ge(kp_loaded[s], i * 64 + (64 * (n // 2 + 1)))
            pe.wait_ge(s_exp, seq)

            def transposes(h):
                if h >= 2:
                    pe.wait_ge(page_ready[h % 2], seq * 4 + (h // 2))
                for p in range(NPG):
                    last = nc.tensor.transpose(psum[:, 4 + h % 2, p * 128:(p + 1) * 128],
                                               k_page[s][:, p, h * 128:(h + 1) * 128], ident[:, :])
                last.then_inc(page_full, 1)

            transposes(0)
            for h in range(DH):
                if h + 1 < DH:
                    transposes(h + 1)
                pe.wait_ge(page_ready[h % 2], seq * 4 + (h // 2 + 1))
                nc.tensor.matmul(psum[:, 2 * s, :], q_wide[s][:, h * 128:(h + 1) * 128], page_t[h % 2][:, :],
                                 start=h == 0, stop=h == DH - 1)
                last = nc.tensor.matmul(psum[:, 2 * s + 1, 0:TS], q_wide[s][:, h * 128:(h + 1) * 128], k_new_t[:, h, :],
                                        start=h == 0, stop=h == DH - 1)
            last.then_inc(s_full, 1)

        def outputs(i, n):
            s, seq = n % 2, i * 2 + n
            pe.wait_ge(s_comb_ready, seq + 1)
            for b in range(NPG + 1):
                m = 128 if b < NPG else TS
                last = nc.tensor.matmul(psum[0:m, 6, b * TS:(b + 1) * TS], s_prob[s][:, b * 128:b * 128 + m],
                                        s_comb[s][:, :], start=True, stop=True)
            last.then_inc(s_mix_full, 1)
            pe.wait_ge(s_mix_ready, seq + 1)
            pe.wait_ge(s_out_read, seq)
            pe.wait_ge(vp_loaded[s], i * 64 + 64)
            for h in range(DH):
                out = psum[:, 7, h * DS:(h + 1) * DS]
                for p in range(NPG):
                    nc.tensor.matmul(out, v_page[s][:, p, h * DV:(h + 1) * DV], s_mix_t[s][:, p, h * DS:(h + 1) * DS],
                                     start=p == 0, stop=False)
                last = nc.tensor.matmul(out, v_new[:, h * DV:(h + 1) * DV], s_mix_t[s][0:TS, NPG, h * DS:(h + 1) * DS],
                                        start=False, stop=True)
            last.then_inc(s_out_full, 1)

        scores(0, 0)

        def body(i, last):
            for n in range(2):
                if not (last and n == 1):
                    scores(i, n + 1)
                outputs(i, n)
        s_bodies(pe, body)
        pe.wait_ge(s_square, 1)
        nc.tensor.matmul(psum[:, 0, :], ones_sq[:, :], o_square[:, :, :], start=True, stop=True).then_inc(s_total, 1)

    def pages_out(eng, copy, seq, h):
        eng.wait_ge(page_full, seq * DH + (h + 1))
        copy(page_t[h % 2][:, :], psum[:, 4 + h % 2, :]).then_inc(page_ready[h % 2], 1)

    def act_sampled(act):
        act.wait_ge(new_full, 1)
        nc.scalar.copy(k_new_t[:, :, :], psum[:, 0, :].rearrange("p (h t) -> p h t", h=DH)).then_inc(new_t_ready[0], 1)
        act.sem_inc(s_exp, 1)

        def pages_of(i, n):
            for h in range(0, DH, 2):
                pages_out(act, nc.scalar.copy, i * 2 + n, h)

        def exps(i, n):
            s, seq = n % 2, i * 2 + n
            act.wait_ge(s_max, seq + 1)
            nc.scalar.activation(s_prob[s][:, :], psum[:, 2 * s:2 * s + 2, :].rearrange("p b n -> p (b n)")[:, 0:PAST + TS],
                                 ACT.Exp, bias=s_neg_max[s][:, :], accum_out=s_sum[s][:, :]).then_inc(s_exp, 1)

        pages_of(0, 0)
        exps(0, 0)

        def body(i, last):
            for n in range(2):
                if not (last and n == 1):
                    pages_of(i, n + 1)
                s, seq = n % 2, i * 2 + n
                act.wait_ge(s_mix_full, seq + 1)
                nc.scalar.copy(s_mix_t[s][:, 0:NPG, :],
                               psum[:, 6, 0:NPG * TS].rearrange("p (b n) -> p b n", b=NPG))
                nc.scalar.copy(s_mix_t[s][0:TS, NPG, :], psum[0:TS, 6, NPG * TS:(NPG + 1) * TS]).then_inc(s_mix_ready, 1)
                if not (last and n == 1):
                    exps(i, n + 1)
        s_bodies(act, body)
        act.wait_ge(s_var, 1)
        nc.scalar.activation(o_square[:, :, :], o_square[:, :, :], ACT.Sqrt).then_inc(s_rstd, 1)

    def dve_sampled(dve):
        for s in range(2):
            dstep.done(nc.vector.memset(q_wide[s][:, :], 0.0))
        dstep.done(nc.vector.memset(ones_sq[:, :], 1.0))
        dve.wait_ge(new_loaded, 80)
        dstep.done(nc.vector.scalar_tensor_tensor(s_sign[:, :], comb[:, TS + 1:TS + 2], neg_lam[:, :], comb[:, TS:TS + 1],
                                                  ALU.mult, ALU.add))
        dve.wait_ge(new_full, 2)
        nc.vector.tensor_copy(q_new_t[:, :, :], psum[:, 1, :].rearrange("p (h t) -> p h t", h=DH)).then_inc(new_t_ready[1], 1)
        dve.wait_ge(new_t_ready[1], 1)
        dstep.wait(dve)

        def widen(i, n):
            s, seq = n % 2, i * 2 + n
            for c in range(2):
                r = slice(c * DHD, (c + 1) * DHD)
                last = nc.vector.tensor_scalar(
                    q_wide[s][r, :].rearrange("p (h x) -> p h x", x=144)[:, :, c * DS:(c + 1) * DS],
                    q_new_t[r, :, bass.ds(seq * DS, DS)], DHD ** -0.5, None, ALU.mult)
            last.then_inc(wide_ready, 1)

        def maxima(i, n):
            s, seq = n % 2, i * 2 + n
            for h in range(1, DH, 2):
                pages_out(dve, nc.vector.tensor_copy, seq, h)
            dve.wait_ge(s_full, seq + 1)
            dve.wait_ge(s_exp, seq + 1)
            dstep.done(nc.vector.tensor_tensor(psum[:, 2 * s + 1, 0:TS], psum[:, 2 * s + 1, 0:TS],
                                               new_mask[:, bass.ds(seq, 1), :].rearrange("p o n -> p (o n)"), ALU.add))
            dstep.wait(dve)
            nc.vector.tensor_reduce(s_neg_max[s][:, :],
                                    psum[:, 2 * s:2 * s + 2, :].rearrange("p b n -> p (b n)")[:, 0:PAST + TS],
                                    AX.X, ALU.max, negate=True).then_inc(s_max, 1)

        widen(0, 0)
        maxima(0, 0)

        def body(i, last):
            for n in range(2):
                s, seq = n % 2, i * 2 + n
                if not (last and n == 1):
                    widen(i, n + 1)
                dve.wait_ge(s_exp, seq + 2)
                dstep.done(nc.vector.reciprocal(s_recip[:, :], s_sum[s][:, :]))
                dstep.wait(dve)
                nc.vector.tensor_scalar(s_comb[s][:, :], comb[:, 0:TS], s_recip[:, :], s_sign[:, :], ALU.mult,
                                        ALU.mult).then_inc(s_comb_ready, 1)
                if not (last and n == 1):
                    maxima(i, n + 1)
                dve.wait_ge(s_out_full, seq + 1)
                nc.vector.tensor_scalar(o_new[:, :, bass.ds(seq * DS, DS)],
                                        psum[:, 7, 0:TS].rearrange("p (h t) -> p h t", h=DH), 1.0, None,
                                        ALU.mult).then_inc(s_out_read, 1)

        with dve.Fori(0, S_BODY - 1) as i:
            dstep.loop(i, 4)
            body(i, False)
            dstep.end(S_BODY - 1)
        body(S_BODY - 1, True)
        dve.wait_ge(s_out_read, DB)
        nc.vector.tensor_tensor(o_square[:, :, :], o_new[:, :, :], o_new[:, :, :], ALU.mult).then_inc(s_square, 1)
        dve.wait_ge(s_total, 1)
        nc.vector.tensor_scalar(o_square[:, :, :], psum[:, 0, :].rearrange("p (h t) -> p h t", h=DH), 1.0 / DV, EPS,
                                ALU.mult, ALU.add).then_inc(s_var, 1)
        dve.wait_ge(s_rstd, 1)
        dstep.done(nc.vector.reciprocal(o_square[:, :, :], o_square[:, :, :]))
        dstep.wait(dve)
        nc.vector.scalar_tensor_tensor(o_square[:, :, :], o_new[:, :, :], sub_gain[:, :], o_square[:, :, :], ALU.mult,
                                       ALU.mult).then_inc(s_a_ready, 1)


    KT = RK // 128
    VT = RV // 128
    st = ExitStack()
    rq_in = [sb(f"rq_in{s}", [128, NC, RK], F, st) for s in range(2)]
    rk_in = [sb(f"rk_in{s}", [128, NC, RK], F, st) for s in range(2)]
    rv_in = [sb(f"rv_in{s}", [128, NC, RV], F, st) for s in range(2)]
    decay = [sb(f"decay{s}", [128, 132], F, st) for s in range(2)]
    qk_t = [sb(f"qk_t{s}", [128, 2 * KT, 128], F, st) for s in range(2)]
    p_t = [sb(f"p_t{s}", [128, 128], F, st) for s in range(2)]
    k_dec = [sb(f"k_dec{s}", [128, RK], F, st) for s in range(2)]
    state = [sb(f"state{s}", [128, KT, RV], F, st) for s in range(2)]
    r_inter = sb("r_inter", [128, RV], F, st)
    r_rows = [sb(f"r_rows{s}", [128, RV], F, st) for s in range(2)]
    r_gate = [sb(f"r_gate{s}", [128, VT, 128], F, st) for s in range(4)]
    r_sq = [sb(f"r_sq{s}", [128, 1], F, st) for s in range(2)]
    r_var = sb("r_var", [128, 1], F, st)
    r_rstd = sb("r_rstd", [128, 1], F, st)
    st.close()

    r_loaded = [sem("r_loaded0"), sem("r_loaded1")]
    rg_loaded = [sem(f"rg_loaded{s}") for s in range(4)]
    rg_stored = [sem(f"rg_stored{s}") for s in range(4)]
    rt_full = sem("rt_full")
    rt_read = sem("rt_read")
    kd_ready = sem("kd_ready")
    qk_full = sem("qk_full")
    pt_ready = sem("pt_ready")
    intra_full = sem("intra_full")
    inter_full = sem("inter_full")
    inter_read = sem("inter_read")
    upd_full = sem("upd_full")
    state_ready = sem("state_ready")
    row_ready = sem("row_ready")
    rsq_ready = sem("rsq_ready")
    rvar_ready = sem("rvar_ready")
    rrstd_ready = sem("rrstd_ready")
    rnorm_ready = sem("rnorm_ready")
    rr_full = sem("rr_full")
    r_ready = sem("r_ready")
    state_stored = sem("state_stored")
    R_BODY = RH // 2

    def sp_retention(sp):
        def load(i, h):
            s = h % 2
            head = i * 2 + h
            for x, width, col in ((rq_in, RK, QR), (rk_in, RK, KR), (rv_in, RV, VR)):
                sp.dma_start(x[s][:, :, :], proj[0:TP, bass.ds(head * width + col, width)].rearrange(
                    "(c p) d -> p c d", p=128)).then_inc(r_loaded[s], 16)
            sp.dma_start(decay[s][:, :], c_ret[bass.ds(head, 1), :, :].rearrange("o p n -> (o p) n")).then_inc(r_loaded[s], 16)

        def gate_rows(x, i, j, n):
            return x[bass.ds(i * (2 * RV) + j * RV, RV), n * 128:(n + 1) * 128].rearrange("(b e) n -> e b n", e=128)

        for s in range(4):
            sp.sem_inc(rg_stored[s], 16)
        def body(i, last):
            for j in range(2):
                sp.wait_ge(r_ready, i * (2 * NC) + NC * j)
                if not (last and j == 1):
                    load(i, j + 1)
                for n in range(NC + 3):
                    if n < NC:
                        s = n % 4
                        sp.wait_ge(rg_stored[s], i * 64 + 16 * (2 * j + n // 4 + 1))
                        sp.dma_start(r_gate[s][:, :, :], gate_rows(gates, i, j, n)).then_inc(rg_loaded[s], 16)
                    if n >= 3:
                        m = n - 3
                        sp.wait_ge(r_ready, i * (2 * NC) + (NC * j + m + 1))
                        sp.dma_start(gate_rows(r_t, i, j, m), r_gate[m % 4][:, :, :]).then_inc(rg_stored[m % 4], 16)
                sp.wait_ge(state_ready, i * (2 * NC) + NC * (j + 1))
                sp.dma_start(ret_prompt[0, 0, bass.ds(i * 2 + j, 1), :, :].rearrange("o (k p) e -> p (o k) e", p=128),
                             state[0][:, :, :]).then_inc(state_stored, 16)

        load(0, 0)
        with sp.Fori(0, R_BODY - 1) as i:
            body(i, False)
        body(R_BODY - 1, True)
        for s in range(4):
            sp.wait_ge(rg_stored[s], 16 * (1 + RH * NC // 4))
        sp.wait_ge(state_stored, 16 * RH)

    def pe_retention(pe):
        with pe.Fori(0, R_BODY) as i:
            for j in range(2):
                def at(n):
                    return i * (2 * NC) + (NC * j + n)

                def transposes(n):
                    pe.wait_ge(rt_read, at(n))
                    for k in range(KT):
                        nc.tensor.transpose(psum[:, 0, k * 128:(k + 1) * 128], rq_in[j][:, n, k * 128:(k + 1) * 128],
                                            ident[:, :])
                    for k in range(KT):
                        last = nc.tensor.transpose(psum[:, 0, (KT + k) * 128:(KT + k + 1) * 128],
                                                   rk_in[j][:, n, k * 128:(k + 1) * 128], ident[:, :])
                    last.then_inc(rt_full, 1)

                def products(n):
                    pe.wait_ge(rt_read, at(n + 1))
                    pe.wait_ge(pt_ready, at(n))
                    for k in range(KT):
                        last = nc.tensor.matmul(psum[:, 1, 0:128], qk_t[n % 2][:, KT + k, :], qk_t[n % 2][:, k, :],
                                                start=k == 0, stop=k == KT - 1)
                    last.then_inc(qk_full, 1)

                def rows_out(n):
                    pe.wait_ge(rnorm_ready, at(n + 1))
                    pe.wait_ge(r_ready, at(n))
                    for b in range(VT):
                        last = nc.tensor.transpose(psum[:, 6, b * 128:(b + 1) * 128],
                                                   r_rows[n % 2][:, b * 128:(b + 1) * 128], ident[:, :])
                    last.then_inc(rr_full, 1)

                pe.wait_ge(r_loaded[j], i * 64 + 64)
                transposes(0)
                products(0)
                for n in range(NC):
                    pe.wait_ge(kd_ready, at(n + 1))
                    pe.wait_ge(state_ready, at(n))
                    for k in range(KT):
                        last = nc.tensor.matmul(psum[:, 4 + k, :], k_dec[n % 2][:, k * 128:(k + 1) * 128],
                                                rv_in[j][:, n, :], start=True, stop=True)
                    last.then_inc(upd_full, 1)
                    pe.wait_ge(pt_ready, at(n + 1))
                    pe.wait_ge(row_ready, at(n))
                    nc.tensor.matmul(psum[:, 2, :], p_t[n % 2][:, :], rv_in[j][:, n, :], start=True,
                                     stop=True).then_inc(intra_full, 1)
                    if n + 1 < NC:
                        transposes(n + 1)
                        products(n + 1)
                    if n:
                        pe.wait_ge(state_ready, at(n))
                        for k in range(KT):
                            last = nc.tensor.matmul(psum[:, 3, :], qk_t[n % 2][:, k, :], state[n % 2][:, k, :],
                                                    start=k == 0, stop=k == KT - 1)
                        last.then_inc(inter_full, 1)
                        rows_out(n - 1)
                rows_out(NC - 1)
        pe.wait_ge(rr_full, RH * NC)

    def act_retention(act):
        with act.Fori(0, R_BODY) as i:
            for j in range(2):
                def at(n):
                    return i * (2 * NC) + (NC * j + n)

                def chunk_in(n):
                    act.wait_ge(rt_full, at(n + 1))
                    nc.scalar.copy(qk_t[n % 2][:, :, :], psum[:, 0, :].rearrange("p (k n) -> p k n", n=128)).then_inc(rt_read, 1)
                    nc.scalar.activation(k_dec[n % 2][:, :], rk_in[j][:, n, :], ACT.Copy,
                                         scale=decay[j][:, 129:130]).then_inc(kd_ready, 1)

                chunk_in(0)
                for n in range(NC):
                    if n + 1 < NC:
                        if n:
                            act.wait_ge(upd_full, at(n))
                            if n >= 2:
                                act.wait_ge(inter_full, i * (2 * NC - 2) + ((NC - 1) * j + n - 1))
                        chunk_in(n + 1)
                    if n:
                        act.wait_ge(inter_full, i * (2 * NC - 2) + ((NC - 1) * j + n))
                        act.wait_ge(row_ready, at(n))
                        nc.scalar.activation(r_inter[:, :], psum[:, 3, :], ACT.Copy,
                                             scale=decay[j][:, 128:129]).then_inc(inter_read, 1)
                    act.wait_ge(row_ready, at(n + 1))
                    act.wait_ge(rvar_ready, at(n - 1) if n else at(n))
                    nc.scalar.activation(psum[:, 7, :], r_rows[n % 2][:, :], ACT.Square,
                                         accum_out=r_sq[n % 2][:, :]).then_inc(rsq_ready, 1)
                    act.wait_ge(rsq_ready, at(n + 1))

    def dve_retention(dve):
        with dve.Fori(0, R_BODY) as i:
            for j in range(2):
                def at(n):
                    return i * (2 * NC) + (NC * j + n)

                def weights(n):
                    dve.wait_ge(qk_full, at(n + 1))
                    if n >= 2:
                        dve.wait_ge(intra_full, at(n - 1))
                    nc.vector.tensor_tensor(p_t[n % 2][:, :], psum[:, 1, 0:128], decay[j][:, 0:128],
                                            ALU.mult).then_inc(pt_ready, 1)

                def variance(n):
                    dve.wait_ge(rsq_ready, at(n + 1))
                    dve.wait_ge(rrstd_ready, at(n))
                    nc.vector.tensor_scalar(r_var[:, :], r_sq[n % 2][:, :], 1.0 / RV, EPS, ALU.mult,
                                            ALU.add).then_inc(rvar_ready, 1)

                def normalise(n):
                    dve.wait_ge(rrstd_ready, at(n + 1))
                    nc.vector.tensor_scalar(r_rows[n % 2][:, :], r_rows[n % 2][:, :], r_rstd[:, :], None,
                                            ALU.mult).then_inc(rnorm_ready, 1)

                def gated(n):
                    dve.wait_ge(rr_full, at(n + 1))
                    dve.wait_ge(rg_loaded[n % 4], i * 64 + 16 * (2 * j + n // 4 + 1))
                    slot = r_gate[n % 4][:, :, :].rearrange("p b n -> p (b n)")
                    nc.vector.tensor_tensor(slot, psum[:, 6, :], slot, ALU.mult).then_inc(r_ready, 1)

                weights(0)
                for n in range(NC):
                    if n >= 2:
                        gated(n - 2)
                    if n + 1 < NC:
                        weights(n + 1)
                    if n:
                        variance(n - 1)
                    new, update = state[(n + 1) % 2], psum[:, 4:6, :]
                    dve.wait_ge(upd_full, at(n + 1))
                    if n == 1:
                        dve.wait_ge(state_stored, i * 32 + 16 * j)
                    if n:
                        dve.wait_ge(state_ready, at(n))
                        nc.vector.scalar_tensor_tensor(new[:, :, :], state[n % 2][:, :, :], decay[j][:, 130:131], update,
                                                       ALU.mult, ALU.add).then_inc(state_ready, 1)
                        normalise(n - 1)
                        dve.wait_ge(inter_read, i * (2 * NC - 2) + ((NC - 1) * j + n))
                        dve.wait_ge(intra_full, at(n + 1))
                        nc.vector.tensor_tensor(r_rows[n % 2][:, :], psum[:, 2, :], r_inter[:, :],
                                                ALU.add).then_inc(row_ready, 1)
                    else:
                        nc.vector.tensor_copy(new[:, :, :], update).then_inc(state_ready, 1)
                        dve.wait_ge(intra_full, at(n + 1))
                        nc.vector.tensor_copy(r_rows[0][:, :], psum[:, 2, :]).then_inc(row_ready, 1)
                variance(NC - 1)
                normalise(NC - 1)
                gated(NC - 2)
                gated(NC - 1)

    def pool_retention(pool):
        with pool.Fori(0, RH * NC) as i:
            pool.wait_ge(rvar_ready, i + 1)
            nc.gpsimd.tensor_tensor(r_rstd[:, :], r_var[:, :], exponent[:, 0:1], ALU.pow).then_inc(rrstd_ready, 1)

    n_at = [0]

    def n_view(p, *shape):
        width = math.prod(shape)
        x = acc1[0:p, n_at[0]:n_at[0] + width]
        n_at[0] += width
        assert n_at[0] <= NT * D
        return x.rearrange("p (a b) -> p a b", a=shape[0]) if len(shape) == 2 else x

    n_state = [n_view(128, KT, RV) for _ in range(4)]
    nq_in, nk_in, nv_in = n_view(TS, RK), n_view(TS, RK), n_view(TS, RV)
    n_decay = n_view(TS, TS + DB)
    n_qdec = n_view(128, TS)
    n_decay8 = n_view(128, 4)
    nqk_t = n_view(128, 2 * KT, TS)
    q_own = n_view(128, KT, DB * (TS + DS))
    np_t = n_view(TS, TS)
    nk_dec = [n_view(TS, RK) for _ in range(2)]
    nr_rows = n_view(TS, RV)
    nr_gate = n_view(128, VT, TS)
    nr_var, nr_rstd, nr_z = n_view(TS, 1), n_view(TS, 1), n_view(TS, 1)

    n_loaded = sem("n_loaded")
    nv_loaded = sem("nv_loaded")
    ng_loaded = sem("ng_loaded")
    n_stored = sem("n_stored")
    ns_loaded = [sem(f"ns_loaded{s}") for s in range(4)]
    ns_stored = [sem(f"ns_stored{s}") for s in range(4)]
    sp_step = sem("sp_step")
    pe_step = sem("pe_step")
    nt_full = sem("nt_full")
    nt_read = sem("nt_read")
    nq_ready = sem("nq_ready")
    nqk_full = sem("nqk_full")
    np_ready = sem("np_ready")
    nk_ready = sem("nk_ready")
    nu_full = sem("nu_full")
    ns_ready = sem("ns_ready")
    nr_full = sem("nr_full")
    nr_read = sem("nr_read")
    nr_step = sem("nr_step")
    nn_ready = sem("nn_ready")
    nrr_full = sem("nrr_full")
    n_ready = sem("n_ready")

    def state_rows(x, i, b):
        return x[0, b, bass.ds(i, 1), :, :].rearrange("o (k p) e -> p (o k) e", p=128)

    def sp_n_inputs(sp, i, d):
        sp.wait_ge(nk_ready, i * DB + DB * d)
        sp.wait_ge(np_ready, i + d)
        sp.wait_ge(nq_ready, i + d)
        for x, col in ((nq_in, QR), (nk_in, KR)):
            sp.dma_start(x, proj[TP:T, bass.ds(i * RK + (d * RK + col), RK)]).then_inc(n_loaded, 16)
        sp.dma_start(n_decay, c_ret_new[bass.ds(i + d, 1), :, :].rearrange("o p n -> (o p) n")).then_inc(n_loaded, 16)
        sp.dma_start(n_qdec, c_ret_qdec[bass.ds(i + d, 1), :, :].rearrange("o p n -> (o p) n")).then_inc(n_loaded, 16)
        sp.wait_ge(ns_ready, i * (2 * DB) + 2 * DB * d)
        sp.dma_start(nv_in, proj[TP:T, bass.ds(i * RV + (d * RV + VR), RV)]).then_inc(nv_loaded, 16)
        sp.dma_start(n_decay8, c_ret[bass.ds(i + d, 1), :, 128:132].rearrange("o p n -> (o p) n")).then_inc(nv_loaded, 16)

    def sp_n_load_state(sp, i, b):
        sp.wait_ge(ns_stored[b % 4], i * 32 + 16 * (b // 4 + 1))
        sp.dma_start(n_state[b % 4], state_rows(state_ret, i + b // DB, b % DB)).then_inc(ns_loaded[b % 4], 16)

    def sp_n_begin(sp):
        for s in range(4):
            sp.sem_inc(ns_stored[s], 16)
        sp.sem_inc(n_stored, 16)
        sp_n_inputs(sp, 0, 0)
        for b in range(2):
            sp_n_load_state(sp, 0, b)

    def sp_n_unit(sp, i, m, last):
        if m:
            sp.wait_ge(ns_ready, i * (2 * DB) + 2 * m)
            sp.sem_inc(sp_step, 1)
            sp.dma_start(state_rows(ret_sample, i, m - 1), n_state[(m - 1) % 4]).then_inc(ns_stored[(m - 1) % 4], 16)
        if not (last and m + 2 >= DB):
            sp_n_load_state(sp, i, m + 2)
        if m == 5:
            sp.wait_ge(n_stored, i * 16 + 16)
            sp.sem_inc(sp_step, 1)
            for s in range(2):
                sp.wait_ge(gate_stored[s], i * 32 + 48)
                sp.sem_inc(sp_step, 1)
            sp.dma_start(nr_gate, gates[bass.ds(i * RV, RV), TP:T].rearrange("(b e) n -> e b n", e=128)).then_inc(
                ng_loaded, 16)
        if m == DB - 1:
            if not last:
                sp_n_inputs(sp, i, 1)
            sp.wait_ge(ns_ready, i * (2 * DB) + 2 * DB)
            sp.dma_start(state_rows(ret_sample, i, m), n_state[m % 4]).then_inc(ns_stored[m % 4], 16)

    def sp_n_end(sp, i):
        sp.wait_ge(n_ready, i + 1)
        sp.dma_start(r_t[bass.ds(i * RV, RV), TP:T].rearrange("(b e) n -> e b n", e=128), nr_gate).then_inc(n_stored, 16)

    def pe_n_piece(pe, i, m, k):
        first = m == 0
        if first and k == 0:
            pe.wait_ge(n_loaded, i * 64 + 64)
            pe.wait_ge(n_ready, i)
            pe.sem_inc(pe_step, 1)
            for x, a in ((nq_in, 0), (nk_in, KT)):
                for b in range(KT):
                    last = nc.tensor.transpose(psum[:, 6, (a + b) * TS:(a + b + 1) * TS], x[:, b * 128:(b + 1) * 128],
                                               ident[0:TS, 0:TS])
            last.then_inc(nt_full, 1)
        if first and k == 2:
            pe.wait_ge(nt_read, i + 1)
            for b in range(KT):
                last = nc.tensor.matmul(psum[0:TS, 6, 0:TS], nqk_t[:, KT + b, :], nqk_t[:, b, :], start=b == 0,
                                        stop=b == KT - 1)
            last.then_inc(nqk_full, 1)
        if k == (4 if first else 0):
            if first:
                pe.wait_ge(np_ready, i + 1)
                pe.wait_ge(nq_ready, i + 1)
                pe.wait_ge(nr_read, i * 2)
                pe.wait_ge(nv_loaded, i * 32 + 32)
            pe.wait_ge(ns_loaded[m % 4], i * 32 + 16 * (m // 4 + 1))
            for b in range(KT):
                last = nc.tensor.matmul(psum[0:TS, 7, :], q_own[:, b, m * TS:(m + 1) * TS], n_state[m % 4][:, b, :],
                                        start=first and b == 0, stop=m == DB - 1 and b == KT - 1)
            if first:
                nc.tensor.matmul(psum[0:TS, 7, :], np_t, nv_in, start=False, stop=False)
            if m == DB - 1:
                last.then_inc(nr_full, 1)
        if k in ((5, 7) if first else (2, 4)):
            b = 1 if k in (7, 4) else 0
            pe.wait_ge(nk_ready, i * DB + (m + 1))
            pe.wait_ge(ns_ready, i * (2 * DB) + (2 * m + b))
            pe.sem_inc(pe_step, 1)
            nc.tensor.matmul(psum[:, 6, :], nk_dec[m % 2][:, b * 128:(b + 1) * 128], nv_in, start=True,
                             stop=True).then_inc(nu_full, 1)

    def pe_n_end(pe, i):
        pe.wait_ge(nn_ready, i + 1)
        pe.wait_ge(ns_ready, i * (2 * DB) + 2 * DB)
        pe.sem_inc(pe_step, 1)
        for v in range(VT):
            last = nc.tensor.transpose(psum[:, 6, v * TS:(v + 1) * TS], nr_rows[:, v * 128:(v + 1) * 128], ident[0:TS, 0:TS])
        last.then_inc(nrr_full, 1)

    def act_n_unit(act, i, m):
        if m == 0:
            act.wait_ge(nt_full, i + 1)
            nc.scalar.copy(nqk_t, psum[:, 6, 0:2 * KT * TS].rearrange("p (k n) -> p k n", n=TS)).then_inc(nt_read, 1)
        for b in ((0, 1) if m == 0 else (m + 1,) if m + 1 < DB else ()):
            act.wait_ge(nu_full, i * (2 * DB) + (2 * (b - 1) if b > 1 else 0))
            nc.scalar.activation(nk_dec[b % 2], nk_in, ACT.Copy, scale=n_decay[:, TS + b:TS + b + 1]).then_inc(nk_ready, 1)
        if m == DB - 1:
            act.wait_ge(nr_full, i + 1)
            nc.scalar.copy(nr_rows, psum[0:TS, 7, :]).then_inc(nr_read, 1)
            act.wait_ge(nr_read, i * 2 + 1)
            nc.scalar.activation(psum[0:TS, 7, :], nr_rows, ACT.Square, accum_out=nr_var).then_inc(nr_read, 1)
            act.wait_ge(nr_step, i * 6 + 1)
            nc.scalar.activation(nr_rstd, nr_var, ACT.Sqrt).then_inc(nr_step, 1)

    def dve_n_unit(dve, i, m):
        if m == 0:
            dve.wait_ge(nt_read, i + 1)
            for b in range(KT):
                last = nc.vector.tensor_tensor(q_own[:, b, :].rearrange("p (b x) -> p b x", x=TS + DS)[:, :, 0:DS],
                                               nqk_t[:, b, :].rearrange("p (b t) -> p b t", t=DS),
                                               n_qdec.rearrange("p (b t) -> p b t", t=DS), ALU.mult)
            last.then_inc(nq_ready, 1)
            dve.wait_ge(nqk_full, i + 1)
            nc.vector.tensor_tensor(np_t, psum[0:TS, 6, 0:TS], n_decay[:, 0:TS], ALU.mult).then_inc(np_ready, 1)
        for b in range(KT):
            dve.wait_ge(nu_full, i * (2 * DB) + (2 * m + b + 1))
            s = n_state[m % 4][:, b, :]
            nc.vector.scalar_tensor_tensor(s, s, n_decay8[:, 3:4], psum[:, 6, :], ALU.mult, ALU.add).then_inc(ns_ready, 1)
        if m == DB - 1:
            v, y, z = nr_var, nr_rstd, nr_z
            dve.wait_ge(nr_read, i * 2 + 2)
            nc.vector.tensor_scalar(v, v, 1.0 / RV, EPS, ALU.mult, ALU.add).then_inc(nr_step, 1)
            dve.wait_ge(nr_step, i * 6 + 2)
            nc.vector.reciprocal(y, y).then_inc(nr_step, 1)
            dve.wait_ge(nr_step, i * 6 + 3)
            nc.vector.scalar_tensor_tensor(z, y, v, y, ALU.mult, ALU.mult).then_inc(nr_step, 1)
            dve.wait_ge(nr_step, i * 6 + 4)
            nc.vector.tensor_scalar(z, z, -0.5, 1.5, ALU.mult, ALU.add).then_inc(nr_step, 1)
            dve.wait_ge(nr_step, i * 6 + 5)
            nc.vector.tensor_tensor(y, y, z, ALU.mult).then_inc(nr_step, 1)
            dve.wait_ge(nr_step, i * 6 + 6)
            nc.vector.tensor_scalar(nr_rows, nr_rows, y, None, ALU.mult).then_inc(nn_ready, 1)

    def dve_n_end(dve, i):
        dve.wait_ge(nrr_full, i + 1)
        dve.wait_ge(ng_loaded, i * 16 + 16)
        nc.vector.tensor_tensor(nr_gate, psum[:, 6, 0:VT * TS].rearrange("p (b n) -> p b n", n=TS), nr_gate,
                                ALU.mult).then_inc(n_ready, 1)

    XIN = [0, T]
    SG = 2 * T
    G_M, G_O, G_O1 = banks_before(W_PA), banks_before(W_O), banks_before(W_O) + NT
    G_GU, G_DN = banks_before(W_GU), banks_before(W_DN)
    N_MERGE = 3
    UNITS = D // 128
    O1_ORDER = []
    for t in range(NT + 2):
        O1_ORDER += [("O", t)] * (t < NT) + [("N", t - 2, b) for b in range(2) if t >= 2]

    def o1_place(*what):
        return G_O1 + O1_ORDER.index(what)

    xin_loaded = [sem("xin_loaded0"), sem("xin_loaded1")]
    xh_ready = sem("xh_ready")
    xt_ready = sem("xt_ready")
    xt_free = sem("xt_free")
    sg_loaded = sem("sg_loaded")
    merged = sem("merged")
    ff_gate = sem("ff_gate")
    ff_mul = sem("ff_mul")
    h_ready = sem("h_ready")
    h_stored = [sem("h_stored0"), sem("h_stored1")]
    y_stored = sem("y_stored")

    def sp_finish(sp):
        sources = [a_t, r_t[0:D, :], r_t[D:2 * D, :]]

        def load_x(q, k):
            n = q * KD + k
            if n >= 2:
                sp.wait_ge(xt_ready, n - 1)
            sp.dma_start(edge[:, XIN[k % 2]:XIN[k % 2] + T], sources[q][k * 128:(k + 1) * 128, :]).then_inc(
                xin_loaded[k % 2], 16)

        load_x(0, 0)
        load_x(0, 1)
        load_w(sp, W_PB)
        sp_load_gain(sp, norm_ffn_g[0])
        for q in range(N_MERGE):
            for f in range(UNITS):
                n = q * UNITS + f
                if n:
                    sp.wait_ge(merged, n)
                row = (G_B if q else G_A) + f * 128
                sp.dma_start(edge[:, SG:SG + T], gates[row:row + 128, :]).then_inc(sg_loaded, 16)
                if n == 0:
                    for k in range(2, KD):
                        load_x(0, k)
                if f == 2 and q:
                    load_w(sp, W_PB + 2 * q)
                if f == 4 and q + 1 < N_MERGE:
                    load_x(q + 1, 0)
                    load_x(q + 1, 1)
                if f == 6:
                    load_w(sp, W_PB + 2 * q + 1)
            if q + 1 < N_MERGE:
                for k in range(2, KD):
                    load_x(q + 1, k)
        sp.wait_ge(xt_ready, (N_MERGE + 1) * KD)
        for t in range(NT):
            sp.dma_start(h_rows[0:rows(t), t, :], token_rows(x_prompt, x_sample, t)).then_inc(x_loaded[t // 3], 16)
        load_w_gu(sp, 0)
        load_w_gu(sp, 1)
        sp.wait_ge(norm_sems["ffn"]["scaled"], NT)
        sp_load_gain(sp, norm_final_g)

        for s in range(2):
            sp.sem_inc(h_stored[s], 16)

        def store_h(i, j):
            sp.wait_ge(h_ready, i * 4 + (j + 1))
            sp.dma_start(h_t[bass.ds(i * 512 + j * 128, 128), :], edge[:, XIN[j % 2]:XIN[j % 2] + T]).then_inc(
                h_stored[j % 2], 16)

        with sp.Fori(0, N_GU // 2 - 1) as i:
            for j in range(4):
                if j % 2 == 0:
                    load_w_gu(sp, i * 2 + (2 + j // 2))
                store_h(i, j)
        i = N_GU // 2 - 1
        for j in range(4):
            if j == 0:
                load_w_gu(sp, N_GU - 1)
            if j == 2:
                load_w(sp, W_DN)
            store_h(i, j)
        load_w(sp, W_DN + 1)
        store_h(N_GU // 2, 0)

        def load_h(c, t):
            n, nk, k0 = c * NT + t, DOWN_K[c], sum(DOWN_K[:c])
            if n >= 2:
                sp.wait_ge(xt_ready, (N_MERGE + 1) * KD + n - 1)
            sp.dma_start(edge[:, XIN[n % 2]:XIN[n % 2] + nk * rows(t)].rearrange("p (k n) -> p k n", k=nk),
                         h_t[k0 * 128:(k0 + nk) * 128, t * 128:t * 128 + rows(t)].rearrange(
                             "(k p) n -> p k n", p=128)).then_inc(xin_loaded[n % 2], 16)

        n_block = 2 * N_GU
        sp.wait_ge(h_stored[0], 16 * (1 + n_block // 2))
        load_h(0, 0)
        store_h(N_GU // 2, 1)
        sp.wait_ge(h_stored[1], 16 * (1 + n_block // 2))
        for t in range(1, NT):
            load_h(0, t)
        load_w(sp, W_DN + 2)
        load_w(sp, W_DN + 3)
        for c in range(1, len(DOWN_K)):
            for t in range(NT):
                load_h(c, t)
                if c + 1 < len(DOWN_K) and t == 4:
                    load_w(sp, W_DN + 2 * c + 2)
            if c + 1 < len(DOWN_K):
                load_w(sp, W_DN + 2 * c + 3)
        for t in range(NT):
            sp.wait_ge(norm_sems["final"]["scaled"], t + 1)
            sp.dma_start(token_rows(y_prompt, y_sample, t), h_rows[0:rows(t), t, :]).then_inc(y_stored, 16)
        sp.wait_ge(y_stored, 16 * NT)

    def pe_finish(pe):
        with pe.Fori(0, N_MERGE) as i:
            for j in range(2):
                pe_feature_tile(pe, xt_h2, xt_l2, j, i * 4 + (2 * (W_PA + j) + 1),
                                lambda c: (i * 24 + (G_M + 12 * j + c), (G_M + 12 * j + c) % RING),
                                free=xt_free if j else None,
                                ready=None if j else lambda k: (xt_ready, i * KD + (k + 1)))
        pe_token_tile(pe, xt_h2, xt_l2, xs_hl2, 0, 2 * W_O + 1, lambda t: (G_O + t, (G_O + t) % RING),
                      ready=lambda t, k: (xt_ready, N_MERGE * KD + k + 1) if t == 0 else None)

        def behind(t):
            if t >= 2:
                pe_norm_tile(pe, "ffn", t - 2, lambda b: o1_place("N", t - 2, b))

        pe_token_tile(pe, xt_h2, xt_l2, xs_hl2, 1, 2 * (W_O + 1) + 1, lambda t: (o1_place("O", t), o1_place("O", t) % RING),
                      behind=behind)
        behind(NT)
        behind(NT + 1)
        pe.wait_ge(bank_free, RING + G_GU)

        def gate_up(i, j, free=None):
            pe_feature_tile(pe, xt_h2, xt_l2, j, i * 4 + (2 * (W_GU + j) + 1),
                            lambda c: (i * 24 + (G_GU + 12 * j + c), (G_GU + 12 * j + c) % RING), order=(0, 2, 1, 3))

        with pe.Fori(0, N_GU // 2) as i:
            gate_up(i, 0)
            gate_up(i, 1)
        gate_up(N_GU // 2, 0)
        for w in range(W_DN, N_W):
            c, n = divmod(w - W_DN, 2)
            g = banks_before(w)
            pe_token_tile(pe, xt_h2, xt_l2, xs_hl2, w % 2, 2 * w + 1, lambda t: (g + t, (g + t) % RING), DOWN_K[c],
                          ready=lambda t, k: (xt_ready, (N_MERGE + 1) * KD + c * NT + t + 1) if k == 0 and n == 0 else None)

    def act_half(act, g, n):
        act.wait_ge(bank_full, g + 1)
        nc.scalar.copy(edge[0:TS, 2560:3072], psum[TS:2 * TS, g % RING, :]).then_inc(half_ready, 1)
        act.wait_ge(half_ready, n)

    def act_finish(act):
        for q in range(N_MERGE + 1):
            for k in range(KD):
                n = q * KD + k
                if q:
                    if k < KD - 1:
                        act.wait_ge(xt_free, (q - 1) * (KD - 1) + k + 1)
                    else:
                        act.wait_ge(bank_full, G_M + q * 24)
                if q < N_MERGE:
                    act.wait_ge(xin_loaded[k % 2], q * 64 + 16 * (k // 2 + 1))
                    nc.scalar.copy(xt_h2[:, k, :], edge[:, XIN[k % 2]:XIN[k % 2] + T]).then_inc(xh_ready, 1)
                else:
                    act.wait_ge(merged, (N_MERGE - 1) * UNITS + k + 1)
                    nc.scalar.copy(xs_hl2[:, k, 0:TS], m_t[:, k, TP:T])
                    nc.scalar.copy(xt_h2[:, k, 0:TP], m_t[:, k, 0:TP]).then_inc(xh_ready, 1)
        act_half(act, G_O + SAMPLE, N_TM + 1)
        for t in range(NT + 2):
            if t == SAMPLE:
                act.wait_ge(norm_sems["ffn"]["squares"], t)
                act_half(act, o1_place("O", t), N_TM + 2)
            if 1 <= t <= NT:
                act_deviation(act, "ffn", t - 1)
            if t < NT:
                act.wait_ge(bank_free, RING + o1_place("O", t) + 1)
                act_square(act, "ffn", h_rows, t)
            if t >= 2:
                act_high_tile(act, "ffn", t - 2, lambda b: o1_place("N", t - 2, b), xt_h2, xs_hl2)

        def gate_unit(i, u):
            for c, (a, width) in enumerate(CHUNKS):
                g = G_GU + 6 * u + c
                act.wait_ge(bank_full, i * 24 + (g + 1))
                act.wait_ge(ff_mul, i * 24 + (6 * u))
                nc.scalar.activation(edge[:, SG + a:SG + a + width], psum[:, g % RING, 0:width],
                                     ACT.Sigmoid).then_inc(ff_gate, 1)

        with act.Fori(0, N_GU // 2) as i:
            for u in range(4):
                gate_unit(i, u)
        gate_unit(N_GU // 2, 0)
        gate_unit(N_GU // 2, 1)

        def high(c, t):
            n, nk = c * NT + t, DOWN_K[c]
            if c == 0:
                act.wait_ge(bank_full, G_DN)
            else:
                act.wait_ge(bank_full, banks_before(W_DN + 2 * c - 1) + t + 1)
            act.wait_ge(xin_loaded[n % 2], 16 * (N_MERGE * KD // 2 + n // 2 + 1))
            dst = xs_hl2[:, 0:nk, 0:TS] if t == SAMPLE else xt_h2[:, 0:nk, t * 128:(t + 1) * 128]
            nc.scalar.copy(dst, edge[:, XIN[n % 2]:XIN[n % 2] + nk * rows(t)].rearrange("p (k n) -> p k n", k=nk)).then_inc(
                xh_ready, 1)

        for t in range(NT):
            high(0, t)
        for w in range(W_DN, N_W):
            c, n = divmod(w - W_DN, 2)
            g = banks_before(w)
            if n and c + 1 < len(DOWN_K):
                for t in range(NT - 1):
                    high(c + 1, t)
            if w == N_W - 1:
                for t in range(NT - 1):
                    act.wait_ge(bank_free, RING + g + t + 1)
                    act_square(act, "final", h_rows, t)
                    if t:
                        act_deviation(act, "final", t - 1)
                act.wait_ge(norm_sems["final"]["squares"], NT - 1)
            act_half(act, g + SAMPLE, N_TM + 3 + w - W_DN)
            if n and c + 1 < len(DOWN_K):
                high(c + 1, SAMPLE)
        act_deviation(act, "final", SAMPLE - 1)
        act.wait_ge(bank_free, RING + banks_before(N_W))
        act_square(act, "final", h_rows, SAMPLE)
        act_deviation(act, "final", SAMPLE)

    def dve_finish(dve):
        def refill(q, k):
            n = q * KD + k
            dve.wait_ge(xh_ready, n + 1)
            if q < N_MERGE:
                nc.vector.tensor_tensor(xt_l2[:, k, :], edge[:, XIN[k % 2]:XIN[k % 2] + T], xt_h2[:, k, :].bitcast(F),
                                        ALU.subtract).then_inc(xt_ready, 1)
            else:
                nc.vector.tensor_tensor(xs_hl2[:, k, TS:2 * TS], m_t[:, k, TP:T], xs_hl2[:, k, 0:TS].bitcast(F), ALU.subtract)
                nc.vector.tensor_tensor(xt_l2[:, k, 0:TP], m_t[:, k, 0:TP], xt_h2[:, k, 0:TP].bitcast(F),
                                        ALU.subtract).then_inc(xt_ready, 1)

        for k in range(KD):
            refill(0, k)
        for q in range(N_MERGE):
            for f in range(UNITS):
                n = q * UNITS + f
                if f == UNITS - 1:
                    for k in range(KD - 1):
                        refill(q + 1, k)
                dve.wait_ge(sg_loaded, 16 * (n + 1))
                for c, (a, width) in enumerate(CHUNKS):
                    g = G_M + 3 * n + c
                    dve.wait_ge(bank_full, g + 1)
                    gate = edge[:, SG + a:SG + a + width]
                    nc.vector.tensor_tensor(gate if q else m_t[:, f, a:a + width], psum[:, g % RING, 0:width], gate,
                                            ALU.mult).then_inc(bank_free, 1)
                dve.wait_ge(bank_free, RING + G_M + 3 * (n + 1))
                if q:
                    nc.vector.tensor_tensor(m_t[:, f, :], m_t[:, f, :], edge[:, SG:SG + T], ALU.add).then_inc(merged, 1)
                else:
                    dve.sem_inc(merged, 1)
                if f == UNITS - 1:
                    refill(q + 1, KD - 1)

        def add_rows(t, n, g, half):
            h = h_rows[0:rows(t), t, n * WN:(n + 1) * WN]
            dve.wait_ge(bank_full, g + 1)
            if t == SAMPLE:
                dve.wait_ge(half_ready, half)
                dstep.done(nc.vector.tensor_tensor(h, h, edge[0:TS, 2560:3072], ALU.add))
                dstep.wait(dve)
            nc.vector.tensor_tensor(h, h, psum[0:rows(t), g % RING, :], ALU.add).then_inc(bank_free, 1)

        for t in range(NT):
            dve.wait_ge(x_loaded[t // 3], 96)
            add_rows(t, 0, G_O + t, N_TM + 1)
        dve.wait_ge(gain_loaded, 32)
        for t in range(NT + 2):
            if t < NT:
                add_rows(t, 1, o1_place("O", t), N_TM + 2)
            if 1 <= t <= NT:
                dve_rstd(dve, "ffn", t - 1)
                dve_scale_tile(dve, "ffn", h_rows, t - 1, lambda b: o1_place("N", t - 3, b))
            if t >= 2:
                dve_low_tile(dve, "ffn", t - 2, lambda b: o1_place("N", t - 2, b), xt_h2, xt_l2, xs_hl2)

        def gated_unit(i, u):
            for c, (a, width) in enumerate(CHUNKS):
                g = G_GU + 6 * u + c
                sg = edge[:, SG + a:SG + a + width]
                dve.wait_ge(ff_gate, i * 12 + (3 * u + c + 1))
                nc.vector.tensor_tensor(sg, psum[:, g % RING, 0:width], sg, ALU.mult).then_inc(ff_mul, 1)
                dve.wait_ge(ff_mul, i * 24 + (6 * u + c + 1))
                dve.sem_inc(bank_free, 1)
            dve.wait_ge(h_stored[u % 2], i * 32 + 16 * (u // 2 + 1))
            for c, (a, width) in enumerate(CHUNKS):
                g = G_GU + 6 * u + 3 + c
                dve.wait_ge(bank_full, i * 24 + (g + 1))
                nc.vector.tensor_tensor(edge[:, XIN[u % 2] + a:XIN[u % 2] + a + width], psum[:, g % RING, 0:width],
                                        edge[:, SG + a:SG + a + width], ALU.mult).then_inc(ff_mul, 1)
                dve.wait_ge(ff_mul, i * 24 + (6 * u + 3 + c + 1))
                dve.sem_inc(bank_free, 1)
            dve.sem_inc(h_ready, 1)

        with dve.Fori(0, N_GU // 2) as i:
            for u in range(4):
                gated_unit(i, u)
        gated_unit(N_GU // 2, 0)
        gated_unit(N_GU // 2, 1)

        def low(c, t):
            n, nk = c * NT + t, DOWN_K[c]
            dve.wait_ge(xh_ready, (N_MERGE + 1) * KD + n + 1)
            src = edge[:, XIN[n % 2]:XIN[n % 2] + nk * rows(t)].rearrange("p (k n) -> p k n", k=nk)
            if t == SAMPLE:
                dst, high = xs_hl2[:, 0:nk, TS:2 * TS], xs_hl2[:, 0:nk, 0:TS]
            else:
                dst, high = xt_l2[:, 0:nk, t * 128:(t + 1) * 128], xt_h2[:, 0:nk, t * 128:(t + 1) * 128]
            nc.vector.tensor_tensor(dst, src, high.bitcast(F), ALU.subtract).then_inc(xt_ready, 1)

        for t in range(3):
            low(0, t)
        for w in range(W_DN, N_W):
            c, n = divmod(w - W_DN, 2)
            for t in range(NT):
                if c == 0 and n == 0 and t + 3 < NT:
                    low(0, t + 3)
                add_rows(t, n, banks_before(w) + t, N_TM + 3 + w - W_DN)
                if n and c + 1 < len(DOWN_K):
                    low(c + 1, t)
                if w == N_W - 1:
                    if t == 0:
                        dve.wait_ge(gain_loaded, 48)
                    if t:
                        finish_rows(dve, t - 1)
        finish_rows(dve, SAMPLE)

    def finish_rows(dve, t):
        dve_rstd(dve, "final", t)
        h = h_rows[0:rows(t), t, :]
        nc.vector.scalar_tensor_tensor(h, h, rstd[0:rows(t), t:t + 1], gain[0:rows(t), :], ALU.mult,
                                       ALU.mult).then_inc(norm_sems["final"]["scaled"], 1)

    @block.gpsimd
    def _(pool):
        gpsimd_program(pool)

    @block.sync
    def _(sp):
        sp_project(sp)
        end_stage(sp, 1)
        sp_attention(sp)
        end_stage(sp, 2)
        sp_sampled(sp)
        end_stage(sp, 3)
        sp_retention(sp)
        end_stage(sp, 4)
        sp_finish(sp)

    @block.tensor
    def _(pe):
        pe_project(pe)
        end_stage(pe, 1)
        pe_attention(pe)
        end_stage(pe, 2)
        pe_sampled(pe)
        end_stage(pe, 3)
        pe_retention(pe)
        end_stage(pe, 4)
        pe_finish(pe)

    @block.scalar
    def _(act):
        act_project(act)
        act.wait_ge(bank_free, RING + banks_before(W_PA))
        end_stage(act, 1)
        act_attention(act)
        end_stage(act, 2)
        act_sampled(act)
        end_stage(act, 3)
        act_retention(act)
        end_stage(act, 4)
        act_finish(act)

    @block.vector
    def _(dve):
        dve_project(dve)
        dve.wait_ge(bank_free, RING + G_FM + 48)
        end_stage(dve, 1)
        dve_attention(dve)
        end_stage(dve, 2)
        dve_sampled(dve)
        end_stage(dve, 3)
        dve_retention(dve)
        end_stage(dve, 4)
        dve_finish(dve)

    ctx.close()


def tables():
    f = np.float32
    pos = np.concatenate([np.arange(TP), np.tile(np.arange(DS) + PAST, DB)]).astype(f)
    pad = np.concatenate([pos, np.zeros(NT * 128 - T, f)])

    def tiles(x):
        return np.ascontiguousarray(x.reshape(NT, 128, *x.shape[1:]).swapaxes(0, 1))

    def exp(arg):
        return np.exp(arg.astype(f).astype(np.float64)).astype(f)

    freq = exp(f(-math.log(500000.0)) * np.arange(8, dtype=f) * f(2.0 / 16))
    ang = (pad[:, None] * freq[None, :]).astype(f).astype(np.float64)
    cos, sin = np.cos(ang).astype(f), np.sin(ang).astype(f)
    rope_diff = tiles(np.stack([np.concatenate([cos, cos], 1), np.concatenate([-sin, sin], 1)], 1))
    freq = exp(f(-math.log(10000.0)) * (np.arange(RK // 2, dtype=f) * (f(1) / f(RK // 2 - 1))))
    ang = (pad[:, None] * freq[None, :]).astype(f).astype(np.float64)
    cos, sin = np.cos(ang).astype(f), np.sin(ang).astype(f)
    rope_ret = tiles(np.stack([np.repeat(cos, 2, 1), np.stack([-sin, sin], 2).reshape(-1, RK)], 1))

    i = np.arange(128)
    causal = np.where(i[:, None] >= i[None, :], 0.0, NEG).astype(f)
    tok = i % DS
    new = np.arange(TS)
    new_mask = np.stack([np.where((new[None, :] // DS == b) & (new[None, :] % DS <= tok[:, None]), 0.0, NEG)
                         for b in range(DB)], 1).astype(f)
    comb = (np.arange(TS)[None, :] == (i // 16 * DS + tok)[:, None]).astype(f)
    comb = np.concatenate([comb, (i // DS % 2 == 0)[:, None], (i // DS % 2 == 1)[:, None]], 1).astype(f)

    lg = np.log(f(1) - np.exp2(f(-5) - np.arange(RH, dtype=f)).astype(f)).astype(f).astype(np.float64)
    k_scale = RK ** -0.5
    ret = np.zeros((RH, 128, 132), f)
    ret_new = np.zeros((RH, TS, TS + DB), f)
    qdec = np.zeros((RH, 128, TS), f)
    rel = i[None, :] - i[:, None]
    nrel = new[None, :] % DS - new[:, None] % DS
    same = new[None, :] // DS == new[:, None] // DS
    for h in range(RH):
        ret[h, :, 0:128] = np.where(rel >= 0, np.exp(lg[h] * np.maximum(rel, 0)), 0) * k_scale
        ret[h, :, 128] = np.exp((i + 1) * lg[h])
        ret[h, :, 129] = np.exp((CH - 1 - i) * lg[h]) * k_scale
        ret[h, :, 130] = np.exp(CH * lg[h])
        ret[h, :, 131] = np.exp(DS * lg[h])
        ret_new[h, :, 0:TS] = np.where(same & (nrel >= 0), np.exp(lg[h] * np.maximum(nrel, 0)), 0) * k_scale
        ret_new[h, :, TS:] = np.where(new[:, None] // DS == np.arange(DB)[None, :],
                                      np.exp((DS - 1 - new % DS) * lg[h])[:, None] * k_scale, 0)
        qdec[h] = np.exp((new % DS + 1) * lg[h])[None, :]
    return {"c_ident": np.eye(128, dtype=f), "c_rope_diff": rope_diff, "c_rope_ret": rope_ret,
            "c_causal": causal, "c_new_mask": np.ascontiguousarray(new_mask), "c_comb": comb,
            "c_ret": ret, "c_ret_new": ret_new, "c_ret_qdec": qdec}


_INS = ["x_prompt", "x_sample", "cache_k", "cache_v", "state_ret", "page_table", "norm_mix_g", "w_in", "b_gate",
        "lambda_q1", "lambda_k1", "lambda_q2", "lambda_k2", "subln_g", "w_pa", "w_pb", "w_o", "norm_ffn_g",
        "w_gu", "w_down", "norm_final_g"]
_OUTS = [(1, TP, D), (DB, DS, D), (1, 1, TP, DH, 2, DHD), (1, 1, TP, DH, DV), (1, 1, RH, RK, RV),
         (1, DB, DS, DH, 2, DHD), (1, DB, DS, DH, DV), (1, DB, RH, RK, RV)]


def kernel(**inputs):
    import concourse.bacc as bacc
    from concourse.bass_utils import run_bass_kernel_spmd

    nc = bacc.Bacc("TRN2", target_bir_lowering=False, num_devices=1)
    arrays, args = {}, []
    for name, a in [*((n, inputs[n]) for n in _INS), *tables().items()]:
        a = np.ascontiguousarray(a)
        arrays[f"in_{name}_dram"] = a
        args.append(nc.dram_tensor(f"in_{name}_dram", a.shape, mybir.dt.from_np(a.dtype), kind="ExternalInput").ap())
    for i, shape in enumerate(_OUTS):
        args.append(nc.dram_tensor(f"out_{i}_dram", shape, F, kind="ExternalOutput").ap())
    hybrid_layer(nc, *args)
    r = run_bass_kernel_spmd(nc, [arrays], core_ids=[0])
    return tuple(r.results[0][f"out_{i}_dram"] for i in range(len(_OUTS)))
```

```python
import math
from contextlib import ExitStack

import numpy as np
import concourse.bass as bass
from concourse import mybir

F = mybir.dt.float32
R = mybir.dt.float32r
I32 = mybir.dt.int32
ALU = mybir.AluOpType
ACT = mybir.ActivationFunctionType
AX = mybir.AxisListType

D = 1024
TP = 1024
DB, DS = 8, 8
TS = DB * DS
T = TP + TS
NT = TP // 128 + 1
SAMPLE = NT - 1
KD = D // 128
PAST, PAGE = 512, 128
NPG = PAST // PAGE
N_PHYS = 40
DH, DHD, DV = 8, 64, 128
RH, RK, RV = 4, 256, 512
CH = 128
NC = TP // CH
FFN = 2816
NEG = -1e30
EPS = 1e-5
LAM_INIT = 0.8 - 0.6 * math.exp(-0.3 * 0)
WN = 512
N_TM = 14
N_FM = 8
N_GU = FFN // 256
DOWN_K = [8, 8, 6]
CHUNKS = [(0, 384), (384, 384), (768, 320)]
RING = 6
QA, KA, VA, QR, KR, VR = 0, 1024, 2048, 3072, 4096, 5120
PW = N_TM * WN
G_R, G_A, G_B = 0, 2048, 3072

W_TM, W_FM = 0, N_TM
W_PA = W_FM + N_FM
W_PB = W_PA + 2
W_O = W_PB + 4
W_GU = W_O + 2
W_DN = W_GU + N_GU
N_W = W_DN + 2 * len(DOWN_K)
W_NK = [KD] * W_DN + [k for k in DOWN_K for _ in range(2)]


def rows(t):
    return TS if t == SAMPLE else 128


def banks_before(w):
    n = 0
    for v in range(w):
        if v == W_GU:
            n += 2 * NT
        n += NT if v < W_FM or W_O <= v < W_GU or v >= W_DN else 12
    return n + (2 * NT if w == W_GU else 0)


class Count:

    def __init__(self, sem):
        self.sem, self.n, self.i, self.per = sem, 0, None, 0

    def loop(self, i, per):
        self.i, self.per, self.at = i, per, self.n

    def end(self, rounds):
        assert self.n - self.at == self.per, (self.n - self.at, self.per)
        self.n = self.at + self.per * rounds
        self.i = None

    def value(self):
        return self.n if self.i is None else self.i * self.per + self.n

    def done(self, ins):
        ins.then_inc(self.sem, 1)
        self.n += 1

    def wait(self, eng):
        eng.wait_ge(self.sem, self.value())


def hybrid_layer(nc, x_prompt, x_sample, cache_k, cache_v, state_ret, page_table, norm_mix_g, w_in, b_gate,
                 lambda_q1, lambda_k1, lambda_q2, lambda_k2, subln_g, w_pa, w_pb, w_o, norm_ffn_g, w_gu,
                 w_down, norm_final_g, c_ident, c_rope_diff, c_rope_ret, c_causal, c_new_mask, c_comb,
                 c_ret, c_ret_new, c_ret_qdec,
                 y_prompt, y_sample, k_prompt, v_prompt, ret_prompt, k_sample, v_sample, ret_sample):
    ctx = ExitStack()
    sb = lambda name, shape, dt=F, st=ctx: st.enter_context(nc.sbuf_tensor(name, shape, dt))
    sem = lambda name: ctx.enter_context(nc.semaphore(name))

    proj = nc.dram_tensor("proj", [T, PW], F).ap()
    gates = nc.dram_tensor("gates", [4 * D, T], F).ap()
    a_t = nc.dram_tensor("a_t", [D, T], F).ap()
    r_t = nc.dram_tensor("r_t", [2 * D, T], F).ap()
    h_t = nc.dram_tensor("h_t", [FFN, T], F).ap()

    ident = sb("ident", [128, 128])
    gain = sb("gain", [128, D])
    rope_diff = sb("rope_diff", [128, NT, 2, 16])
    stage = [sb(f"stage{h}", [128, KD // 2, WN]) for h in range(2)]
    w_h = [sb(f"w_h{s}", [128, KD, WN], R) for s in range(2)]
    w_l = [sb(f"w_l{s}", [128, KD, WN], R) for s in range(2)]
    edge = sb("edge", [128, 3328])
    bias = sb("bias", [128, 16])
    ss = sb("ss", [128, NT])
    rstd = sb("rstd", [128, NT])
    newton = sb("newton", [128, NT])
    ones = sb("ones", [128, 1])
    one = ones[:, :]
    exponent = sb("exponent", [128, NT])
    neg_lam = sb("neg_lam", [128, 1])
    sub_gain = sb("sub_gain", [128, 1])

    def activations(n, st):
        return (sb(f"xt_h{n}", [128, KD, T], R, st), sb(f"xt_l{n}", [128, KD, T], R, st),
                sb(f"xs_hl{n}", [128, KD, 128], R, st), sb(f"acc{n}", [128, NT * D], F, st))

    st = ExitStack()
    xt_h1, xt_l1, xs_hl1, acc1 = activations(1, st)
    st.close()
    st = ExitStack()
    xt_h2, xt_l2, xs_hl2, acc2 = activations(2, st)
    st.close()
    x_rows = acc1[:, :].rearrange("p (t d) -> p t d", d=D)
    rope_ret = acc1[:, 0:NT * 512].rearrange("p (t s d) -> p t s d", s=2, d=256)
    h_rows = acc2[:, :].rearrange("p (t d) -> p t d", d=D)
    m_t = acc2[:, 0:KD * T].rearrange("p (k n) -> p k n", n=T)

    psum = ctx.enter_context(nc.psum_tensor("psum", [128, 8, 512], F))

    stage_loaded = [sem("stage_loaded0"), sem("stage_loaded1")]
    ones_set = sem("ones_set")
    w_high = sem("w_high")
    w_split = sem("w_split")
    bank_full = sem("bank_full")
    mix_full, mix_free = sem("mix_full"), sem("mix_free")
    bank_free = sem("bank_free")
    x_loaded = [sem(f"x_loaded{i}") for i in range(3)]
    const_loaded = sem("const_loaded")
    gain_loaded = sem("gain_loaded")
    dve_step = sem("dve_step")
    stage_end = sem("stage_end")
    norm_sems = {n: {k: sem(f"{k}_{n}") for k in ("squares", "variance", "deviation", "scaled", "high")
                     if (n, k) != ("final", "high")} for n in ("mix", "ffn", "final")}
    raw_ready = sem("raw_ready")
    roped = sem("roped")
    stored = [sem(f"stored{s}") for s in range(3)]
    sg_ready = sem("sg_ready")
    gate_ready = sem("gate_ready")
    gate_stored = [sem("gate_stored0"), sem("gate_stored1")]
    passed = [0]

    def end_stage(eng, n):
        eng.sem_inc(stage_end, 1)
        eng.wait_ge(stage_end, 4 * n)

    block = ctx.enter_context(nc.Block())

    def w_source(w):
        if w < W_PA:
            return w_in[0].rearrange("(k p) n -> p k n", p=128)[:, :, w * WN:(w + 1) * WN]
        if w < W_PB:
            return w_pa[0].rearrange("(k p) n -> p k n", p=128)[:, :, (w - W_PA) * WN:(w - W_PA + 1) * WN]
        if w < W_O:
            half, n = divmod(w - W_PB, 2)
            return w_pb[0].rearrange("(k p) n -> p k n", p=128)[:, half * KD:(half + 1) * KD, n * WN:(n + 1) * WN]
        if w < W_GU:
            return w_o[0].rearrange("(k p) n -> p k n", p=128)[:, :, (w - W_O) * WN:(w - W_O + 1) * WN]
        chunk, n = divmod(w - W_DN, 2)
        k0 = sum(DOWN_K[:chunk])
        return w_down[0].rearrange("(k p) n -> p k n", p=128)[:, k0:k0 + DOWN_K[chunk], n * WN:(n + 1) * WN]

    def load_half(sp, src, h, nk=KD):
        lo, hi = 4 * h, min(4 * h + 4, nk)
        mid = (lo + hi) // 2
        for a, b in ((lo, mid), (mid, hi)):
            sp.dma_start(stage[h][:, a - lo:b - lo, :], src[:, a:b, :]).then_inc(stage_loaded[h], 16)

    def load_w(sp, w):
        for h in range(2):
            if w >= 1:
                sp.wait_ge(w_split, 2 * (w - 1) + h + 1)
            load_half(sp, w_source(w), h, W_NK[w])

    def load_w_in(sp, i, w):
        col = i * (2 * WN) + w * WN
        src = w_in[0].rearrange("(k p) n -> p k n", p=128)[:, :, bass.ds(col, WN)]
        for h in range(2):
            sp.wait_ge(w_split, i * 4 + (2 * (w - 1) + h + 1))
            load_half(sp, src, h)

    def load_w_gu(sp, n):
        src = w_gu[0].rearrange("(k p) n -> p k n", p=128)
        for h in range(2):
            sp.wait_ge(w_split, n * 2 + (2 * (W_GU - 1) + h + 1))
            for u in range(2):
                sp.dma_start(stage[h][:, :, 256 * u:256 * u + 256],
                             src[:, 4 * h:4 * h + 4, bass.ds(n * 256 + u * FFN, 256)]).then_inc(stage_loaded[h], 16)

    def gpsimd_program(pool):
        def split(w, s, nk=KD, used=None):
            if used is not None:
                pool.wait_ge(bank_full, used)
            for h in range(2):
                lo, hi = 4 * h, min(4 * h + 4, nk)
                pairs = [(k, k + 2) for k in range(lo, hi, 2)]
                pool.wait_ge(stage_loaded[h], w * 32 + 32)
                for a, b in pairs:
                    src = stage[h][:, a - lo:b - lo, :]
                    last = nc.gpsimd.tensor_tensor(w_h[s][:, a:b, :], src, one.unsqueeze(1).to_broadcast([128, b - a, WN]),
                                                   ALU.mult)
                last.then_inc(w_high, 1)
                pool.wait_ge(w_high, w * 2 + (h + 1))
                for a, b in pairs:
                    last = nc.gpsimd.tensor_tensor(w_l[s][:, a:b, :], stage[h][:, a - lo:b - lo, :],
                                                   w_h[s][:, a:b, :].bitcast(F), ALU.subtract)
                last.then_inc(w_split, 1)

        nc.gpsimd.memset(ones[:, :], 1.0).then_inc(ones_set, 1)
        pool.wait_ge(ones_set, 1)
        split(0, 0)
        split(1, 1)

        def split_loop(w0, n):
            step = banks_before(w0 + 1) - banks_before(w0 - 1)
            for v in range(w0, w0 + 2 * n, 2):
                assert banks_before(v + 1) - banks_before(v - 1) == step or v + 2 >= w0 + 2 * n
                assert banks_before(v - 1) == banks_before(w0 - 1) + (v - w0) // 2 * step
                assert banks_before(v) == banks_before(w0) + (v - w0) // 2 * step
            with pool.Fori(0, n) as i:
                split(i * 2 + w0, w0 % 2, used=i * step + banks_before(w0 - 1))
                split(i * 2 + (w0 + 1), (w0 + 1) % 2, used=i * step + banks_before(w0))

        split_loop(2, 7)
        split_loop(16, 4)
        pool_powers(pool)
        pool_retention(pool)
        for w in range(W_PB, W_GU + 2):
            split(w, w % 2, used=banks_before(w - 1) if w - 2 != W_O + 1 else o1_place("O", SAMPLE) + 1)
        n_even = (N_GU - 2) // 2
        split_loop(W_GU + 2, n_even)
        for w in range(W_GU + 2 + 2 * n_even, N_W):
            split(w, w % 2, W_NK[w], used=banks_before(w - 1))

    def act_square(act, tag, src, t):
        p, squares = rows(t), norm_sems[tag]["squares"]
        if t:
            act.wait_ge(squares, t)
        nc.scalar.activation(edge[0:p, 2176:3200], src[0:p, t, :], ACT.Square,
                             accum_out=ss[0:p, t:t + 1]).then_inc(squares, 1)

    def act_deviation(act, tag, t):
        p, s = rows(t), norm_sems[tag]
        act.wait_ge(s["variance"], t + 1)
        nc.scalar.activation(rstd[0:p, t:t + 1], ss[0:p, t:t + 1], ACT.Sqrt).then_inc(s["deviation"], 1)

    def dve_rstd(dve, tag, t):
        p, s = rows(t), norm_sems[tag]
        v, y, z = ss[0:p, t:t + 1], rstd[0:p, t:t + 1], newton[0:p, t:t + 1]
        dve.wait_ge(s["squares"], t + 1)
        nc.vector.tensor_scalar(v, v, 1.0 / D, EPS, ALU.mult, ALU.add).then_inc(s["variance"], 1)
        dve.wait_ge(s["deviation"], t + 1)
        dstep.done(nc.vector.reciprocal(y, y))
        dstep.wait(dve)
        dstep.done(nc.vector.scalar_tensor_tensor(z, y, v, y, ALU.mult, ALU.mult))
        dstep.wait(dve)
        dstep.done(nc.vector.tensor_scalar(z, z, -0.5, 1.5, ALU.mult, ALU.add))
        dstep.wait(dve)
        dstep.done(nc.vector.tensor_tensor(y, y, z, ALU.mult))
        dstep.wait(dve)

    norm_banks = {"mix": (mix_full, mix_free, lambda g: RING + g % 2), "ffn": (bank_full, bank_free, lambda g: g % RING)}

    def scaled_rows(tag, t):
        p = rows(t)
        return x_rows[0:p, t, :] if tag == "mix" else edge[0:p, t % 2 * D:(t % 2 + 1) * D]

    def dve_scale_tile(dve, tag, src, t, place=None):
        p, s = rows(t), norm_sems[tag]
        if place is not None and t >= 2:
            dve.wait_ge(bank_full, place(1) + 1)
        nc.vector.scalar_tensor_tensor(scaled_rows(tag, t), src[0:p, t, :], rstd[0:p, t:t + 1], gain[0:p, :], ALU.mult,
                                       ALU.mult).then_inc(s["scaled"], 1)

    def pe_norm_tile(pe, tag, t, place):
        p, (full, free, bank) = rows(t), norm_banks[tag]
        pe.wait_ge(norm_sems[tag]["scaled"], t + 1)
        for b in range(2):
            g = place(b)
            pe.wait_ge(free, g + 1)
            for k in range(4):
                last = nc.tensor.transpose(psum[:, bank(g), 128 * k:128 * k + p],
                                           scaled_rows(tag, t)[:, (4 * b + k) * 128:(4 * b + k + 1) * 128], ident[0:p, 0:p])
            last.then_inc(full, 1)

    def transposed(tag, g, t):
        return psum[:, norm_banks[tag][2](g), :].rearrange("p (k n) -> p k n", k=4)[:, :, 0:rows(t)]

    def act_high_tile(act, tag, t, place, xh, xs):
        for b in range(2):
            g = place(b)
            act.wait_ge(norm_banks[tag][0], g + 1)
            if t == SAMPLE:
                nc.scalar.copy(xs[:, 4 * b:4 * b + 4, 0:TS], transposed(tag, g, t))
            nc.scalar.copy(xh[:, 4 * b:4 * b + 4, t * 128:t * 128 + rows(t)],
                           transposed(tag, g, t)).then_inc(norm_sems[tag]["high"], 1)

    def dve_low_tile(dve, tag, t, place, xh, xl, xs):
        for b in range(2):
            g = place(b)
            dve.wait_ge(norm_sems[tag]["high"], 2 * t + b + 1)
            ks = slice(4 * b, 4 * b + 4)
            high = xh[:, ks, t * 128:t * 128 + rows(t)].bitcast(F)
            if t == SAMPLE:
                nc.vector.tensor_tensor(xs[:, ks, TS:2 * TS], transposed(tag, g, t), high, ALU.subtract)
            nc.vector.tensor_tensor(xl[:, ks, t * 128:t * 128 + rows(t)], transposed(tag, g, t), high,
                                    ALU.subtract).then_inc(norm_banks[tag][1], 1)

    def pe_token_tile(pe, xh, xl, xs, s, split, g, nk=KD, ready=None, ahead=None, behind=None):
        for t in range(NT):
            if ahead is not None:
                ahead(t)
            count, bank = g(t)
            pe.wait_ge(bank_free, count + 1)
            for k in range(nk):
                if t == 0 and k % 4 == 0:
                    pe.wait_ge(w_split, split + k // 4)
                state = ready(t, k) if ready is not None else None
                if state is not None:
                    pe.wait_ge(*state)
                at = slice(t * 128, t * 128 + 128)
                if t == SAMPLE:
                    passes = ((xs[:, k, :], w_h), (xs[:, k, :], w_l))
                else:
                    passes = ((xh[:, k, at], w_h), (xl[:, k, at], w_h), (xh[:, k, at], w_l))
                for n, (x, w) in enumerate(passes):
                    last = nc.tensor.matmul(psum[:, bank, :], x, w[s][:, k, :], start=k == 0 and n == 0,
                                            stop=k == nk - 1 and n == len(passes) - 1)
            last.then_inc(bank_full, 1)
            if behind is not None:
                behind(t)

    def pe_feature_tile(pe, xh, xl, s, split, g, order=range(4), free=None, ready=None, beside=None):
        for j, m in enumerate(order):
            for c in range(3):
                count, bank = g(3 * j + c)
                if c == 0:
                    pe.wait_ge(bank_free, count + 3)
            for k in range(KD):
                if beside is not None:
                    beside(j, k)
                if j == 0 and k % 4 == 0:
                    pe.wait_ge(w_split, split + k // 4)
                if j == 0 and ready is not None:
                    pe.wait_ge(*ready(k))
                for n, (w, x) in enumerate(((w_h, xh), (w_h, xl), (w_l, xh))):
                    for c, (a, width) in enumerate(CHUNKS):
                        ins = nc.tensor.matmul(psum[:, g(3 * j + c)[1], 0:width], w[s][:, k, m * 128:(m + 1) * 128],
                                               x[:, k, a:a + width], start=k == 0 and n == 0,
                                               stop=k == KD - 1 and n == 2)
                        if k == KD - 1 and n == 2:
                            ins.then_inc(bank_full, 1)
                if free is not None and j == 3 and k < KD - 1:
                    ins.then_inc(free, 1)

    def sp_load_gain(sp, g):
        sp.dma_start(gain[:, :], g.partition_broadcast(128)).then_inc(gain_loaded, 16)

    def token_rows(x, xs, t):
        return x[0, t * 128:(t + 1) * 128, :] if t < SAMPLE else xs.rearrange("b t d -> (b t) d")

    def sp_project(sp):
        for t in range(NT):
            sp.dma_start(x_rows[0:rows(t), t, :], token_rows(x_prompt, x_sample, t)).then_inc(x_loaded[t // 3], 16)
        sp_load_gain(sp, norm_mix_g[0])
        sp.dma_start(ident[:, :], c_ident).then_inc(const_loaded, 16)
        sp.dma_start(rope_diff[:, :, :, :], c_rope_diff).then_inc(const_loaded, 16)
        with nc.allow_non_contiguous_dma(reason="16 biases a partition"):
            sp.dma_start(bias[:, :], b_gate[0].rearrange("(m p) -> p m", p=128)).then_inc(const_loaded, 16)
        load_w(sp, 0)
        load_w(sp, 1)
        for s in range(3):
            sp.sem_inc(stored[s], 16)
        sp.wait_ge(mix_full, 2 * NT)
        sp.dma_start(rope_ret, c_rope_ret).then_inc(const_loaded, 16)

        def store(i, j, t, n_roped, n_raw):
            u = NT * j + t
            if n_roped is not None:
                sp.wait_ge(roped, n_roped)
            if n_raw is not None:
                sp.wait_ge(raw_ready, n_raw)
            col = i * (2 * WN) + j * WN
            sp.dma_start(proj[t * 128:t * 128 + rows(t), bass.ds(col, WN)],
                         edge[0:rows(t), u % 3 * WN:(u % 3 + 1) * WN]).then_inc(stored[u % 3], 16)

        def tiles(first, n, rotate, roped_before):
            with sp.Fori(first, first + n) as i:
                for j in range(2):
                    for t in range(NT):
                        if rotate:
                            store(i, j, t, (i - first) * (2 * NT) + (roped_before + NT * j + t + 1), None)
                        elif t == SAMPLE:
                            store(i, j, t, (i - first) * 2 + (roped_before + j + 1), None)
                        else:
                            store(i, j, t, None, i * (2 * NT) + (NT * j + t + 1))
                        if t == 4:
                            load_w_in(sp, i, j + 2)

        tiles(0, 2, True, 0)
        tiles(2, 1, False, 4 * NT)
        tiles(3, 2, True, 4 * NT + 2)
        tiles(5, 2, False, 8 * NT + 2)
        for s in range(3):
            sp.wait_ge(stored[s], 16 * (1 + N_TM * NT // 3))

        for s in range(2):
            sp.sem_inc(gate_stored[s], 16)
        sp_n_begin(sp)
        with sp.Fori(0, N_FM // 2 - 1) as i:
            for m in range(8):
                sp_n_unit(sp, i, m, False)
                sp_store_gate(sp, i, m)
                if m % 4 == 1:
                    load_w_in(sp, i, N_TM + m // 4 + 2)
            sp_n_end(sp, i)
        i = N_FM // 2 - 1
        for m in range(8):
            sp_n_unit(sp, i, m, True)
            sp_store_gate(sp, i, m)
            if m % 4 == 1:
                load_w(sp, W_PA + m // 4)
        sp_n_end(sp, i)
        for s in range(4):
            sp.wait_ge(ns_stored[s], 16 * (1 + RH * 2))
        sp.wait_ge(n_stored, 16 * (1 + RH))
        for s in range(2):
            sp.wait_ge(gate_stored[s], 16 * (1 + 4 * N_FM // 2))

    def sp_store_gate(sp, i, m):
        s = m % 2
        sp.wait_ge(gate_ready, i * 8 + (m + 1))
        sp.dma_start(gates[bass.ds(i * D + m * 128, 128), :], edge[:, s * T:(s + 1) * T]).then_inc(gate_stored[s], 16)

    G_TM = 0
    G_FM = banks_before(W_FM)

    def pe_project(pe):
        pe.wait_ge(const_loaded, 48)
        pe_norm_tile(pe, "mix", 0, lambda b: b)

        def token_tiles(i, **more):
            for j in range(2):
                pe_token_tile(pe, xt_h1, xt_l1, xs_hl1, j, i * 4 + (2 * j + 1),
                              lambda t: (i * (2 * NT) + (G_TM + NT * j + t), (G_TM + NT * j + t) % RING),
                              **(more if j == 0 else {}))

        ahead_of = {0: [1], 1: [2, 3], 2: [4], 3: [5, 6], 4: [7], 5: [8]}

        def ahead(t):
            for u in ahead_of.get(t, []):
                pe_norm_tile(pe, "mix", u, lambda b: 2 * u + b)

        token_tiles(0, ahead=ahead, ready=lambda t, k: (mix_free, 2 + 2 * (t + 1)) if k == 0 else None)
        with pe.Fori(1, N_TM // 2) as i:
            token_tiles(i)
        with pe.Fori(0, N_FM // 2) as i:
            for j in range(2):
                pe_feature_tile(pe, xt_h1, xt_l1, j, i * 4 + (2 * (W_FM + j) + 1),
                                lambda c: (i * 24 + (G_FM + 12 * j + c), (G_FM + 12 * j + c) % RING),
                                beside=lambda m, k: pe_n_piece(pe, i, 4 * j + m, k))
            pe_n_end(pe, i)
        pe.wait_ge(bank_full, banks_before(W_PA))

    def act_project(act):
        for t in range(NT + 2):
            if 1 <= t <= NT:
                act_deviation(act, "mix", t - 1)
            if t < NT:
                act.wait_ge(x_loaded[t // 3], 48)
                act_square(act, "mix", x_rows, t)
            if t >= 2:
                act_high_tile(act, "mix", t - 2, lambda b: 2 * (t - 2) + b, xt_h1, xs_hl1)
        with act.Fori(0, N_TM // 2) as i:
            for u in range(2 * NT):
                t, g = u % NT, G_TM + u
                act.wait_ge(bank_full, i * (2 * NT) + (g + 1))
                act.wait_ge(stored[u % 3], i * (16 * 6) + 16 * (u // 3 + 1))
                slot = edge[0:rows(t), u % 3 * WN:(u % 3 + 1) * WN]
                nc.scalar.copy(slot, psum[0:rows(t), g % RING, :]).then_inc(raw_ready, 1)
                if t == SAMPLE:
                    act.wait_ge(raw_ready, i * (2 * NT) + (u + 1))
                    nc.scalar.copy(edge[0:TS, 2560:3072], psum[TS:2 * TS, g % RING, :]).then_inc(half_ready, 1)
                    act.wait_ge(half_ready, i * 2 + (u // NT + 1))
                else:
                    act.wait_ge(raw_ready, i * (2 * NT) + (u + 1))
                act.sem_inc(bank_free, 1)
        act.wait_ge(roped, 8 * NT + 6)
        with act.Fori(0, N_FM // 4) as i:
            for c in range(24):
                g = G_FM + c
                if c % 3 == 0:
                    act_n_unit(act, i, c // 3)
                act.wait_ge(bank_full, i * 24 + (g + 1))
                act.wait_ge(bank_free, i * 24 + (RING + g - 2))
                nc.scalar.activation(edge[:, 2176 + 384 * (c % 3):2176 + 384 * (c % 3) + CHUNKS[c % 3][1]],
                                     psum[:, g % RING, 0:CHUNKS[c % 3][1]], ACT.Sigmoid).then_inc(sg_ready, 1)
        act.wait_ge(bank_free, RING + G_FM + 48)
        act.wait_ge(gate_stored[1], 16 * 9)
        for m in range(16):
            act_n_unit(act, 2 + m // 8, m % 8)
            act.wait_ge(gate_stored[m % 2], 16 * (8 + m // 2 + 1))
            for c, (a, width) in enumerate(CHUNKS):
                g = G_FM + 48 + 3 * m + c
                act.wait_ge(bank_full, g + 1)
                nc.scalar.activation(edge[:, m % 2 * T + a:m % 2 * T + a + width], psum[:, g % RING, 0:width],
                                     ACT.Sigmoid, bias=bias[:, m:m + 1]).then_inc(bank_free, 1)
            act.wait_ge(bank_free, RING + G_FM + 48 + 3 * m + 3)
            act.sem_inc(gate_ready, 1)

    half_ready = sem("half_ready")
    dstep = Count(dve_step)

    def dve_project(dve):
        dve.sem_inc(bank_free, RING)
        dve.sem_inc(mix_free, 2)
        dve.wait_ge(gain_loaded, 16)
        for t in range(NT + 1):
            if t < NT:
                dve_rstd(dve, "mix", t)
                dve_scale_tile(dve, "mix", x_rows, t)
            if t:
                dve_low_tile(dve, "mix", t - 1, lambda b: 2 * (t - 1) + b, xt_h1, xt_l1, xs_hl1)
        dve.wait_ge(const_loaded, 48)

        def combine(i, u, n_half):
            p = edge[0:TS, u % 3 * WN:(u % 3 + 1) * WN]
            dve.wait_ge(half_ready, n_half)
            return nc.vector.tensor_tensor(p, p, edge[0:TS, 2560:3072], ALU.add)

        def rotate_diff(u):
            p, t = rows(u % NT), u % NT
            slot = edge[0:p, u % 3 * WN:(u % 3 + 1) * WN].rearrange("p (g d) -> p g d", d=DHD)
            by_cos = edge[0:p, 1536:1664].rearrange("p (g d) -> p g d", d=16)
            by_sin = edge[0:p, 2048:2176].rearrange("p (g d) -> p g d", d=16)
            cos = rope_diff[0:p, t, 0, :].unsqueeze(1).to_broadcast([p, 8, 16])
            sin = rope_diff[0:p, t, 1, :].unsqueeze(1).to_broadcast([p, 8, 16])
            nc.vector.tensor_tensor(by_cos, slot[:, :, 0:16], cos, ALU.mult)
            nc.vector.tensor_tensor(by_sin[:, :, 0:8], slot[:, :, 8:16], sin[:, :, 0:8], ALU.mult)
            dstep.done(nc.vector.tensor_tensor(by_sin[:, :, 8:16], slot[:, :, 0:8], sin[:, :, 8:16], ALU.mult))
            dstep.wait(dve)
            nc.vector.tensor_tensor(slot[:, :, 0:16], by_cos, by_sin, ALU.add).then_inc(roped, 1)

        def rotate_ret(u):
            p, t = rows(u % NT), u % NT
            flat = edge[0:p, u % 3 * WN:(u % 3 + 1) * WN]
            slot = flat.rearrange("p (h d) -> p h d", d=RK)
            pair = flat.rearrange("p (h j c) -> p h j c", c=2, j=RK // 2)
            by_cos = edge[0:p, 1536:2048].rearrange("p (h d) -> p h d", d=RK)
            by_sin = edge[0:p, 2048:2560].rearrange("p (h j c) -> p h j c", c=2, j=RK // 2)
            cos = rope_ret[0:p, t, 0, :].unsqueeze(1).to_broadcast([p, 2, RK])
            sin = rope_ret[0:p, t, 1, :].rearrange("p (j c) -> p j c", c=2).unsqueeze(1)
            nc.vector.tensor_tensor(by_cos, slot, cos, ALU.mult)
            for c in range(2):
                last = nc.vector.tensor_tensor(by_sin[:, :, :, c], pair[:, :, :, 1 - c],
                                               sin[:, :, :, c].to_broadcast([p, 2, RK // 2]), ALU.mult)
            dstep.done(last)
            dstep.wait(dve)
            nc.vector.tensor_tensor(flat, edge[0:p, 1536:2048], edge[0:p, 2048:2560], ALU.add).then_inc(roped, 1)

        def rotations(first, n, rotate, roped_before):
            with dve.Fori(first, first + n) as i:
                dstep.loop(i - first, 2 * NT + 2)
                for u in range(2 * NT):
                    dve.wait_ge(raw_ready, i * (2 * NT) + (u + 1))
                    dve.wait_ge(roped, (i - first) * (2 * NT) + (roped_before + u))
                    if u % NT == SAMPLE:
                        dstep.done(combine(i, u, i * 2 + (u // NT + 1)))
                        dstep.wait(dve)
                    rotate(u)
                dstep.end(n)

        def copies(first, n):
            with dve.Fori(first, first + n) as i:
                for j in range(2):
                    combine(i, NT * j + SAMPLE, i * 2 + (j + 1)).then_inc(roped, 1)

        rotations(0, 2, rotate_diff, 0)
        copies(2, 1)
        dve.wait_ge(const_loaded, 64)
        rotations(3, 2, rotate_ret, 4 * NT + 2)
        copies(5, 2)
        dve.wait_ge(roped, 8 * NT + 6)
        dstep.done(nc.vector.memset(q_own, 0.0))
        dstep.wait(dve)
        with dve.Fori(0, N_FM // 4) as i:
            for c in range(24):
                g, m = G_FM + c, c // 3
                if c % 3 == 0:
                    dve_n_unit(dve, i, m)
                    dve.wait_ge(gate_stored[m % 2], i * 64 + 16 * (m // 2 + 1))
                dve.wait_ge(sg_ready, i * 24 + (c + 1))
                a, width = CHUNKS[c % 3]
                nc.vector.tensor_tensor(edge[:, m % 2 * T + a:m % 2 * T + a + width], psum[:, g % RING, 0:width],
                                        edge[:, 2176 + 384 * (c % 3):2176 + 384 * (c % 3) + width],
                                        ALU.mult).then_inc(bank_free, 1)
                if c % 3 == 2:
                    dve.wait_ge(bank_free, i * 24 + (RING + g + 1))
                    dve.sem_inc(gate_ready, 1)
            dve_n_end(dve, i)
        for i in range(2, RH):
            for m in range(DB):
                dve_n_unit(dve, i, m)
            dve_n_end(dve, i)

    NQ = TP // 128
    STEPS = 2 * NQ
    st = ExitStack()
    q_in = [sb(f"q_in{s}", [128, NQ, 128], F, st) for s in range(2)]
    k_in = [sb(f"k_in{s}", [128, NQ, 128], F, st) for s in range(2)]
    v_in = [sb(f"v_in{s}", [128, NQ, 128], F, st) for s in range(2)]
    q_t = [sb(f"q_t{s}", [128, TP], F, st) for s in range(2)]
    k_t = [sb(f"k_t{s}", [128, TP], F, st) for s in range(2)]
    prob = [sb(f"prob{s}", [128, 2, TP], F, st) for s in range(2)]
    mix = [sb(f"mix{s}", [128, TP], F, st) for s in range(2)]
    mix_t = [sb(f"mix_t{s}", [128, TP], F, st) for s in range(2)]
    o_head = [sb(f"o_head{s}", [128, NQ, 128], F, st) for s in range(2)]
    a_out = sb("a_out", [128, TP], F, st)
    causal = sb("causal", [128, 128], F, st)
    lam_in = sb("lam_in", [128, 4, DHD], F, st)
    lam_prod = sb("lam_prod", [128, 2, DHD], F, st)
    lam_sum = sb("lam_sum", [128, 2], F, st)
    lam_exp = sb("lam_exp", [128, 2], F, st)
    neg_max = [sb(f"neg_max{s}", [128, 2], F, st) for s in range(2)]
    sums = [sb(f"sums{s}", [128, 2], F, st) for s in range(2)]
    recip = [sb(f"recip{s}", [128, 2], F, st) for s in range(2)]
    coef = [sb(f"coef{s}", [128, 1], F, st) for s in range(2)]
    o_var = sb("o_var", [128, NQ], F, st)
    o_rstd = sb("o_rstd", [128, NQ], F, st)
    st.close()

    lam_step = sem("lam_step")
    qkv_loaded = [sem("qkv_loaded0"), sem("qkv_loaded1")]
    score_full = [sem("score_full0"), sem("score_full1")]
    score_max = [sem("score_max0"), sem("score_max1")]
    score_exp = [sem("score_exp0"), sem("score_exp1")]
    mix_ready = sem("mix_ready")
    tr_full = sem("tr_full")
    tr_free = sem("tr_free")
    out_full = sem("out_full")
    out_read = sem("out_read")
    var_ready = sem("var_ready")
    rstd_ready = sem("rstd_ready")
    head_normed = sem("head_normed")
    a_stored = sem("a_stored")
    copied = sem("copied")

    EXTRA = {4: ["K", "Q"], 10: ["O"], 12: ["K", "Q"], 15: ["O"]}

    def transposes_in_body(last):
        plan = []
        for n in range(STEPS):
            plan += [("W", n)] + [(kind, n) for kind in EXTRA.get(n, []) if not (last and n == 12 and kind != "O")]
        return plan

    def place(i, base, per, k):
        return base + k if i is None else i * per + (base + k)

    N_BODY = DH // 2
    TR_BODY = len(transposes_in_body(False))
    TR_LAST = 2 + TR_BODY * (N_BODY - 1)

    def bodies(eng, body):
        with eng.Fori(0, N_BODY - 1) as i:
            body(i, False)
        body(N_BODY - 1, True)

    def tr_index(i, last, what):
        return i * TR_BODY + (2 + transposes_in_body(last).index(what))

    def sp_attention(sp):
        sp.dma_start(causal[:, :], c_causal).then_inc(const_loaded, 16)
        for n, v in enumerate((lambda_q1, lambda_q2, lambda_k1, lambda_k2)):
            sp.dma_start(lam_in[:, n, :], v[0].partition_broadcast(128)).then_inc(const_loaded, 16)
        with nc.allow_non_contiguous_dma(reason="one gain a partition"):
            sp.dma_start(sub_gain[:, :], subln_g[0].rearrange("(p o) -> p o", o=1)).then_inc(const_loaded, 16)

        def load(h, s):
            for x, col in ((k_in, KA), (q_in, QA), (v_in, VA)):
                sp.dma_start(x[s][:, :, :], proj[0:TP, bass.ds(h * 128 + col, 128)].rearrange(
                    "(b p) d -> p b d", p=128)).then_inc(qkv_loaded[s], 16)

        load(0, 0)
        load(1, 1)
        for dst, dst_new, col in ((k_prompt[0, 0].rearrange("t h c d -> t (h c d)"),
                                   k_sample[0].rearrange("b t h c d -> (b t) (h c d)"), KA),
                                  (v_prompt[0, 0].rearrange("t h d -> t (h d)"),
                                   v_sample[0].rearrange("b t h d -> (b t) (h d)"), VA)):
            sp.dma_start(dst, proj[0:TP, col:col + D]).then_inc(copied, 16)
            sp.dma_start(dst_new, proj[TP:T, col:col + D]).then_inc(copied, 16)

        def body(i, last):
            for j in range(2):
                if not last:
                    sp.wait_ge(out_full, i * STEPS + NQ * (j + 1))
                    load(i * 2 + (2 + j), j)
                sp.wait_ge(a_ready, i * 2 + (j + 1))
                sp.dma_start(a_t[bass.ds(i * 256 + j * 128, 128), 0:TP], a_out[:, :]).then_inc(a_stored, 16)
        bodies(sp, body)
        sp.wait_ge(a_stored, 16 * DH)
        sp.wait_ge(copied, 64)

    a_ready = sem("a_ready")

    def pe_attention(pe):
        def transposes(tr, blocks, wait):
            pe.wait_ge(tr_free, tr)
            pe.wait_ge(*wait)
            for b, x in enumerate(blocks):
                last = nc.tensor.transpose(psum[:, 4 + b // 4, b % 4 * 128:b % 4 * 128 + 128], x, ident[:, :])
            last.then_inc(tr_full, 1)

        def scores(step, n, c):
            s, qb, r = n // NQ % 2, n % NQ, slice(c * DHD, (c + 1) * DHD)
            pe.wait_ge(score_exp[c], step)
            for a in range(0, (qb + 1) * 128, 512):
                width = min(512, (qb + 1) * 128 - a)
                nc.tensor.matmul(psum[:, 2 * c + a // 512, 0:width], q_t[s][r, qb * 128:(qb + 1) * 128],
                                 k_t[s][r, a:a + width], start=True, stop=qb * 128 >= a + width)
            a = qb % 4 * 128
            last = nc.tensor.matmul(psum[:, 2 * c + qb // 4, a:a + 128], ident[:, :], causal[:, :], start=False, stop=True)
            last.then_inc(score_full[c], 1)

        def values(step, n):
            s, qb = n // NQ, n % NQ
            pe.wait_ge(mix_t_ready, step + 1)
            pe.wait_ge(out_read, step + 1)
            for b in range(qb + 1):
                last = nc.tensor.matmul(psum[:, 6 + n % 2, 0:DV], mix_t[n % 2][:, b * 128:(b + 1) * 128],
                                        v_in[s][:, b, :], start=b == 0, stop=b == qb)
            last.then_inc(out_full, 1)

        def heads_kq(tr, s, count):
            transposes(tr, [k_in[s][:, b, :] for b in range(NQ)], (qkv_loaded[s], count))
            transposes(tr + 1, [q_in[s][:, b, :] for b in range(NQ)], (qkv_loaded[s], count))
            return tr + 2

        pe.wait_ge(const_loaded, 64 + 16 * 6)
        heads_kq(0, 0, 48)
        pe.wait_ge(tr_free, 2)
        scores(0, 0, 0)
        scores(0, 0, 1)

        def body(i, last):
            for n in range(STEPS):
                step, final = i * STEPS + n, last and n == STEPS - 1
                if not final:
                    if n % NQ == NQ - 1:
                        pe.wait_ge(tr_free, tr_index(i, last, ("Q", n - 3)) + 1)
                    scores(step + 1, (n + 1) % STEPS, 0)
                tr = tr_index(i, last, ("W", n))
                transposes(tr, [mix[n % 2][:, b * 128:(b + 1) * 128] for b in range(n % NQ + 1)],
                           (mix_ready, step + 1))
                if not final:
                    scores(step + 1, (n + 1) % STEPS, 1)
                values(step, n)
                for kind in EXTRA.get(n, []):
                    if kind == "K" and not (last and n == 12):
                        s = 1 - n // NQ
                        heads_kq(tr + 1, s, i * 48 + (48 if s else 96))
                    if kind == "O":
                        s = n // NQ if n == 15 else 0
                        transposes(tr + 1, [o_head[s][:, b, :] for b in range(NQ)],
                                   (head_normed, i * 2 + (s + 1)))
        bodies(pe, body)
        pe.wait_ge(tr_free, TR_LAST + len(transposes_in_body(True)))

    mix_t_ready = sem("mix_t_ready")

    def act_attention(act):
        def exps(step, n, c, first=None):
            width = (n % NQ + 1) * 128
            act.wait_ge(score_max[c], step + 1)
            if first is None:
                act.wait_ge(mix_ready, step - 1)
            nc.scalar.activation(prob[n % 2][:, c, 0:width],
                                 psum[:, 2 * c:2 * c + 2, :].rearrange("p b n -> p (b n)")[:, 0:width],
                                 ACT.Exp, bias=neg_max[n % 2][:, c:c + 1],
                                 accum_out=sums[n % 2][:, c:c + 1]).then_inc(score_exp[c], 1)

        def evacuate(tr, out, width):
            act.wait_ge(tr_full, tr + 1)
            nc.scalar.copy(out[:, 0:width], psum[:, 4:6, :].rearrange("p b n -> p (b n)")[:, 0:width]).then_inc(tr_free, 1)

        act.sem_inc(out_read, 2)
        act.wait_ge(lam_step, 1)
        nc.scalar.activation(lam_exp[:, :], lam_sum[:, :], ACT.Exp).then_inc(lam_step, 1)
        evacuate(0, k_t[0], TP)
        exps(0, 0, 0, True)
        exps(0, 0, 1, True)

        def body(i, last):
            for n in range(STEPS):
                step, final = i * STEPS + n, last and n == STEPS - 1
                tr = tr_index(i, last, ("W", n))
                width = (n % NQ + 1) * 128
                act.wait_ge(tr_full, tr + 1)
                nc.scalar.copy(mix_t[n % 2][:, 0:width],
                               psum[:, 4:6, :].rearrange("p b n -> p (b n)")[:, 0:width]).then_inc(mix_t_ready, 1)
                act.wait_ge(mix_t_ready, step + 1)
                act.sem_inc(tr_free, 1)
                if not final:
                    exps(step + 1, n + 1, 0)
                    exps(step + 1, n + 1, 1)
                act.wait_ge(out_full, step + 1)
                if n % NQ == 0:
                    act.wait_ge(head_used, i * 2 + n // NQ)
                nc.scalar.activation(o_head[n // NQ][:, n % NQ, :], psum[:, 6 + n % 2, 0:DV], ACT.Copy,
                                     scale=recip[n % 2][:, 0:1]).then_inc(out_read, 1)
                if n == 4 or (n == 12 and not last):
                    evacuate(tr + 1, k_t[1 - n // NQ], TP)

        bodies(act, body)

    head_used = sem("head_used")

    def dve_attention(dve):
        dve.sem_inc(head_used, 1)
        dve.wait_ge(const_loaded, 64 + 16 * 6)
        dstep.done(nc.vector.tensor_tensor(lam_prod[:, :, :], lam_in[:, 0:2, :], lam_in[:, 2:4, :], ALU.mult))
        dstep.wait(dve)
        nc.vector.tensor_reduce(lam_sum[:, :], lam_prod[:, :, :], AX.X, ALU.add).then_inc(lam_step, 1)
        dve.wait_ge(lam_step, 2)
        dstep.done(nc.vector.tensor_tensor(neg_lam[:, :], lam_exp[:, 1:2], lam_exp[:, 0:1], ALU.subtract))
        dstep.wait(dve)
        dstep.done(nc.vector.tensor_scalar(neg_lam[:, :], neg_lam[:, :], -LAM_INIT, None, ALU.add))
        dstep.done(nc.vector.tensor_scalar(sub_gain[:, :], sub_gain[:, :], 1.0 - LAM_INIT, None, ALU.mult))
        dstep.wait(dve)

        def maxima(step, n, c):
            qb = n % NQ
            flat = psum[:, 2 * c:2 * c + 2, :].rearrange("p b n -> p (b n)")
            dve.wait_ge(score_full[c], step + 1)
            nc.vector.tensor_reduce(neg_max[n % 2][:, c:c + 1], flat[:, 0:(qb + 1) * 128], AX.X, ALU.max,
                                    negate=True).then_inc(score_max[c], 1)

        def weights(step, n):
            s, width = n % 2, (n % NQ + 1) * 128
            for c in range(2):
                dve.wait_ge(score_exp[c], step + 1)
            dve.wait_ge(out_read, step + 1)
            dstep.done(nc.vector.reciprocal(recip[s][:, :], sums[s][:, :]))
            dstep.wait(dve)
            dstep.done(nc.vector.scalar_tensor_tensor(coef[s][:, :], sums[s][:, 0:1], recip[s][:, 1:2],
                                                      neg_lam[:, :], ALU.mult, ALU.mult))
            dstep.wait(dve)
            nc.vector.scalar_tensor_tensor(mix[s][:, 0:width], prob[s][:, 1, 0:width], coef[s][:, :],
                                           prob[s][:, 0, 0:width], ALU.mult, ALU.add).then_inc(mix_ready, 1)

        def queries(tr, s):
            dve.wait_ge(tr_full, tr + 1)
            nc.vector.tensor_scalar(q_t[s][:, :], psum[:, 4:6, :].rearrange("p b n -> p (b n)"), DHD ** -0.5, None,
                                    ALU.mult).then_inc(tr_free, 1)

        queries(1, 0)
        maxima(0, 0, 0)
        maxima(0, 0, 1)

        def one_body(i, last):
            for n in range(STEPS):
                step, final = i * STEPS + n, last and n == STEPS - 1
                tr = tr_index(i, last, ("W", n))
                weights(step, n)
                if not final:
                    maxima(step + 1, n + 1, 0)
                    maxima(step + 1, n + 1, 1)
                if n == 4 or (n == 12 and not last):
                    queries(tr + 2, 1 - n // NQ)
                if n in (8, 15):
                    variance(i, n // 15)
                if n in (9, 15):
                    normalise(i, n // 15)
                if n in (10, 15):
                    output(i, n // 15, tr + 1)

        def variance(i, j):
            dve.wait_ge(out_read, i * STEPS + (2 + NQ * (j + 1)))
            dve.wait_ge(a_stored, i * 32 + 16 * j)
            square = a_out[:, :].rearrange("p (b d) -> p b d", d=128)
            dstep.done(nc.vector.tensor_tensor(square, o_head[j][:, :, :], o_head[j][:, :, :], ALU.mult))
            dstep.wait(dve)
            dstep.done(nc.vector.tensor_reduce(o_var[:, :], square, AX.X, ALU.add))
            dstep.wait(dve)
            nc.vector.tensor_scalar(o_var[:, :], o_var[:, :], 1.0 / DV, EPS, ALU.mult, ALU.add).then_inc(var_ready, 1)

        def normalise(i, j):
            dve.wait_ge(rstd_ready, i * 2 + (j + 1))
            nc.vector.tensor_tensor(o_head[j][:, :, :], o_head[j][:, :, :],
                                    o_rstd[:, :].unsqueeze(2).to_broadcast([128, NQ, 128]),
                                    ALU.mult).then_inc(head_normed, 1)

        def output(i, j, tr):
            dve.wait_ge(tr_full, tr + 1)
            nc.vector.tensor_scalar(a_out[:, :], psum[:, 4:6, :].rearrange("p b n -> p (b n)"), sub_gain[:, :], None,
                                    ALU.mult).then_inc(head_used, 1)
            dve.wait_ge(head_used, i * 2 + (j + 2))
            dve.sem_inc(tr_free, 1)
            dve.sem_inc(a_ready, 1)

        with dve.Fori(0, N_BODY - 1) as i:
            dstep.loop(i, 2 * STEPS + 4)
            one_body(i, False)
            dstep.end(N_BODY - 1)
        one_body(N_BODY - 1, True)

    def pool_powers(pool):
        nc.gpsimd.memset(exponent[:, :], -0.5).then_inc(ones_set, 1)
        pool.wait_ge(ones_set, 2)
        with pool.Fori(0, DH) as i:
            pool.wait_ge(var_ready, i + 1)
            nc.gpsimd.tensor_tensor(o_rstd[:, :], o_var[:, :], exponent[:, 0:NQ], ALU.pow).then_inc(rstd_ready, 1)

    KT = RK // 128
    VT = RV // 128
    CHB = 2 * NC
    N_BODY3 = RH // 2
    SQB = DB // N_BODY3
    PER = CHB // SQB
    BT, BO, BU, BR = 0, 1, 2, 3
    BS, BP, BM = 4, 6, 7
    assert PER == 4
    st = ExitStack()
    rq_in = [sb(f"rq_in{s}", [128, RK], F, st) for s in range(4)]
    rk_in = [sb(f"rk_in{s}", [128, RK], F, st) for s in range(4)]
    rv_in = [sb(f"rv_in{s}", [128, RV], F, st) for s in range(4)]
    decay = [sb(f"decay{s}", [128, 132], F, st) for s in range(2)]
    qk_t = [sb(f"qk_t{s}", [128, 2 * KT, 128], F, st) for s in range(2)]
    p_t = [sb(f"p_t{s}", [128, 128], F, st) for s in range(2)]
    k_dec = [sb(f"k_dec{s}", [128, RK], F, st) for s in range(2)]
    state = [sb(f"state{s}", [128, KT, RV], F, st) for s in range(2)]
    r_rows = [sb(f"r_rows{s}", [128, RV], F, st) for s in range(2)]
    r_square = sb("r_square", [128, RV], F, st)
    r_gate = [sb(f"r_gate{s}", [128, VT, 128], F, st) for s in range(4)]
    r_sq = [sb(f"r_sq{s}", [128, 1], F, st) for s in range(2)]
    r_var = sb("r_var", [128, 1], F, st)
    r_rstd = sb("r_rstd", [128, 1], F, st)
    k_page = sb("k_page", [128, NPG, D], F, st)
    v_page = sb("v_page", [128, NPG, D], F, st)
    q_new, k_new, v_new = (edge[0:TS, a * D:(a + 1) * D] for a in range(3))
    q_new_t = sb("q_new_t", [128, DH, TS], F, st)
    k_new_t = sb("k_new_t", [128, DH, TS], F, st)
    q_wide = sb("q_wide", [128, DH * 144], F, st)
    page_t = [sb(f"page_t{s}", [128, PAST], F, st) for s in range(2)]
    s_prob = sb("s_prob", [128, PAST + TS], F, st)
    s_comb = sb("s_comb", [128, TS], F, st)
    s_mix_t = sb("s_mix_t", [128, NPG + 1, TS], F, st)
    s_neg_max = sb("s_neg_max", [128, 1], F, st)
    s_sum = sb("s_sum", [128, 1], F, st)
    s_recip = sb("s_recip", [128, 1], F, st)
    s_sign = sb("s_sign", [128, 1], F, st)
    comb = sb("comb", [128, TS + 2], F, st)
    new_mask = sb("new_mask", [128, DB, TS], F, st)
    o_new = sb("o_new", [128, DH, TS], F, st)
    o_square = sb("o_square", [128, DH, TS], F, st)
    ones_sq = sb("ones_sq", [128, 128], F, st)
    pages = sb("pages", [1, DB * NPG], I32, st)
    st.close()

    rc_loaded = [sem(f"rc_loaded{s}") for s in range(4)]
    rd_loaded = [sem("rd_loaded0"), sem("rd_loaded1")]
    rg_loaded = [sem(f"rg_loaded{s}") for s in range(4)]
    rg_stored = [sem(f"rg_stored{s}") for s in range(4)]
    rt_full = sem("rt_full")
    rt_read = sem("rt_read")
    kd_ready = sem("kd_ready")
    qk_full = sem("qk_full")
    pt_ready = sem("pt_ready")
    upd_full = sem("upd_full")
    state_ready = sem("state_ready")
    ro_full = sem("ro_full")
    rsq_ready = sem("rsq_ready")
    rvar_ready = sem("rvar_ready")
    rrstd_ready = sem("rrstd_ready")
    rnorm_ready = sem("rnorm_ready")
    rr_full = sem("rr_full")
    r_ready = sem("r_ready")
    state_stored = sem("state_stored")
    new_loaded = sem("new_loaded")
    kp_loaded = sem("kp_loaded")
    vp_loaded = sem("vp_loaded")
    new_full = sem("new_full")
    new_t_ready = [sem("new_k_ready"), sem("new_q_ready")]
    wide_ready = sem("wide_ready")
    page_full = sem("page_full")
    page_ready = sem("page_ready")
    s_full = sem("s_full")
    s_max = sem("s_max")
    s_exp = sem("s_exp")
    s_comb_ready = sem("s_comb_ready")
    s_mix_full = sem("s_mix_full")
    s_mix_ready = sem("s_mix_ready")
    s_out_full = sem("s_out_full")
    s_out_read = sem("s_out_read")
    s_norm = sem("s_norm")
    s_a_stored = sem("s_a_stored")

    def sp_mixers(sp):
        sp.dma_start(pages[:, :], page_table.rearrange("(o b) n -> o (b n)", o=1)).then_inc(const_loaded, 16)
        for x, col in ((q_new, QA), (k_new, KA), (v_new, VA)):
            sp.dma_start(x, proj[TP:T, col:col + D]).then_inc(new_loaded, 16)
        sp.dma_start(comb[:, :], c_comb).then_inc(new_loaded, 16)
        sp.dma_start(new_mask[:, :, :], c_new_mask).then_inc(new_loaded, 16)
        for s in range(4):
            sp.sem_inc(rg_stored[s], 16)

        def load_chunk(i, c):
            for x, width, col in ((rq_in, RK, QR), (rk_in, RK, KR), (rv_in, RV, VR)):
                sp.dma_start(x[c % 4][:, :], proj[c % NC * 128:(c % NC + 1) * 128,
                                                  bass.ds(i * (2 * width) + (c // NC * width + col), width)]).then_inc(
                    rc_loaded[c % 4], 16)

        def load_decay(i, j):
            sp.dma_start(decay[j][:, :], c_ret[bass.ds(i * 2 + j, 1), :, :].rearrange("o p n -> (o p) n")).then_inc(
                rd_loaded[j], 16)

        def gate_rows(x, i, c):
            return x[bass.ds(i * (2 * RV) + c // NC * RV, RV), c % NC * 128:(c % NC + 1) * 128].rearrange(
                "(b e) n -> e b n", e=128)

        def page_numbers(i, s):
            return [sp.value_load(pages[0:1, bass.ds(i * (SQB * NPG) + (s * NPG + p), 1)], min_val=0, max_val=N_PHYS - 1)
                    for p in range(NPG)]

        def load_pages(numbers, x, cache, loaded):
            for p in range(NPG):
                sp.dma_start(x[:, p, :], cache[bass.ds(numbers[p], 1), :, :].rearrange("o p d -> (o p) d")).then_inc(loaded, 16)

        keys = (k_page, cache_k[0].rearrange("n p h c d -> n p (h c d)"), kp_loaded)
        vals = (v_page, cache_v[0].rearrange("n p h d -> n p (h d)"), vp_loaded)
        load_decay(0, 0)
        load_chunk(0, 0)
        sp.wait_ge(const_loaded, 64 + 16 * 7)
        numbers = page_numbers(0, 0)
        load_pages(numbers, *keys)
        for c in (1, 2):
            load_chunk(0, c)
        load_decay(0, 1)
        load_pages(numbers, *vals)

        def body(i, last):
            numbers = None
            for c in range(CHB):
                if not (last and c + 3 >= CHB):
                    sp.wait_ge(upd_full, i * (2 * CHB) + 2 * c)
                    load_chunk(i, c + 3)
                if c == NC:
                    sp.wait_ge(state_ready, i * (2 * CHB) + 2 * NC)
                    store_state(i, 0)
                s = c % 4
                sp.wait_ge(rg_stored[s], i * (CHB * 4) + 16 * (c // 4 + 1))
                sp.dma_start(r_gate[s][:, :, :], gate_rows(gates, i, c)).then_inc(rg_loaded[s], 16)
                if c % PER == 2 and not (last and c // PER == SQB - 1):
                    numbers = page_numbers(i, c // PER + 1)
                    sp.wait_ge(s_full, i * SQB + (c // PER + 1))
                    load_pages(numbers, *keys)
                for m in ((c - 3,) if c >= 3 else ()) + ((c - 2, c - 1, c) if c == CHB - 1 else ()):
                    sp.wait_ge(r_ready, i * CHB + (m + 1))
                    sp.dma_start(gate_rows(r_t, i, m), r_gate[m % 4][:, :, :]).then_inc(rg_stored[m % 4], 16)
                if c % PER == PER - 1 and not (last and c // PER == SQB - 1):
                    sp.wait_ge(s_out_full, i * SQB + (c // PER + 1))
                    load_pages(numbers, *vals)
            sp.wait_ge(state_ready, i * (2 * CHB) + 2 * CHB)
            store_state(i, 1)
            if not last:
                for j in range(2):
                    load_decay(i + 1, j)

        def store_state(i, j):
            sp.dma_start(ret_prompt[0, 0, bass.ds(i * 2 + j, 1), :, :].rearrange("o (k p) e -> p (o k) e", p=128),
                         state[0][:, :, :]).then_inc(state_stored, 16)

        with sp.Fori(0, N_BODY3 - 1) as i:
            body(i, False)
        body(N_BODY3 - 1, True)
        for s in range(4):
            sp.wait_ge(rg_stored[s], 16 * (1 + RH * NC // 4))
        sp.wait_ge(state_stored, 16 * RH)
        sp.wait_ge(s_norm, 5)
        sp.dma_start(a_t.rearrange("(h e) n -> e h n", e=DV)[:, :, TP:T], o_square[:, :, :]).then_inc(s_a_stored, 16)
        sp.wait_ge(s_a_stored, 16)

    def pe_mixers(pe):
        pe.wait_ge(new_loaded, 80)
        for b, x in enumerate((k_new, q_new)):
            for h in range(DH):
                last = nc.tensor.transpose(psum[:, BS + b, h * TS:(h + 1) * TS], x[:, h * 128:(h + 1) * 128], ident[0:TS, 0:TS])
            last.then_inc(new_full, 1)
        pe.wait_ge(new_t_ready[0], 1)
        pe.wait_ge(new_t_ready[1], 1)

        with pe.Fori(0, N_BODY3) as i:
            def at(c):
                return i * CHB + c

            def transposes(c):
                pe.wait_ge(rc_loaded[c % 4], i * (48 * 4) + 48 * (c // 4 + 1))
                pe.wait_ge(pt_ready, at(c))
                for x, a in ((rq_in, 0), (rk_in, KT)):
                    for k in range(KT):
                        last = nc.tensor.transpose(psum[:, BT, (a + k) * 128:(a + k + 1) * 128],
                                                   x[c % 4][:, k * 128:(k + 1) * 128], ident[:, :])
                last.then_inc(rt_full, 1)

            def products(c):
                pe.wait_ge(rt_read, at(c + 1))
                for k in range(KT):
                    last = nc.tensor.matmul(psum[:, BT, 0:128], qk_t[c % 2][:, KT + k, :], qk_t[c % 2][:, k, :],
                                            start=k == 0, stop=k == KT - 1)
                last.then_inc(qk_full, 1)

            def update(c, k):
                pe.wait_ge(kd_ready, at(c + 1))
                pe.wait_ge(state_ready, i * (2 * CHB) + (2 * c + k))
                nc.tensor.matmul(psum[:, BU, :], k_dec[c % 2][:, k * 128:(k + 1) * 128], rv_in[c % 4][:, :], start=True,
                                 stop=True).then_inc(upd_full, 1)

            def rows_out(c):
                pe.wait_ge(rnorm_ready, at(c + 1))
                pe.wait_ge(r_ready, at(c))
                for b in range(VT):
                    last = nc.tensor.transpose(psum[:, BR, b * 128:(b + 1) * 128], r_rows[c % 2][:, b * 128:(b + 1) * 128],
                                               ident[:, :])
                last.then_inc(rr_full, 1)

            def page(s, h):
                if h == 0:
                    pe.wait_ge(kp_loaded, i * (64 * SQB) + 64 * (s + 1))
                pe.wait_ge(page_ready, i * (SQB * DH) + (s * DH + h))
                for p in range(NPG):
                    last = nc.tensor.transpose(psum[:, BP, p * 128:(p + 1) * 128], k_page[:, p, h * 128:(h + 1) * 128],
                                               ident[:, :])
                last.then_inc(page_full, 1)

            def scores(s, h):
                if h == 0:
                    pe.wait_ge(wide_ready, i * SQB + (s + 1))
                    pe.wait_ge(s_exp, i * SQB + s)
                pe.wait_ge(page_ready, i * (SQB * DH) + (s * DH + h + 1))
                q = q_wide[:, h * 128:(h + 1) * 128]
                nc.tensor.matmul(psum[:, BS, :], q, page_t[h % 2][:, :], start=h == 0, stop=h == DH - 1)
                last = nc.tensor.matmul(psum[:, BS + 1, 0:TS], q, k_new_t[:, h, :], start=h == 0, stop=h == DH - 1)
                if h == DH - 1:
                    last.then_inc(s_full, 1)

            def weights(s):
                pe.wait_ge(s_comb_ready, i * SQB + (s + 1))
                pe.wait_ge(s_out_read, i * SQB + s)
                for b in range(NPG + 1):
                    m = 128 if b < NPG else TS
                    last = nc.tensor.matmul(psum[0:m, BM, b * TS:(b + 1) * TS], s_prob[:, b * 128:b * 128 + m],
                                            s_comb[:, :], start=True, stop=True)
                last.then_inc(s_mix_full, 1)

            def outputs(s, place):
                if place == 0:
                    pe.wait_ge(vp_loaded, i * (64 * SQB) + 64 * (s + 1))
                    pe.wait_ge(s_mix_ready, i * SQB + (s + 1))
                for h in range(2 * place, 2 * place + 2):
                    out = psum[:, BM, 384 + h * DS:384 + (h + 1) * DS]
                    for p in range(NPG):
                        nc.tensor.matmul(out, v_page[:, p, h * DV:(h + 1) * DV], s_mix_t[:, p, h * DS:(h + 1) * DS],
                                         start=p == 0, stop=False)
                    last = nc.tensor.matmul(out, v_new[:, h * DV:(h + 1) * DV], s_mix_t[0:TS, NPG, h * DS:(h + 1) * DS],
                                            start=False, stop=True)
                if place == 3:
                    last.then_inc(s_out_full, 1)

            def beside(c, place):
                s, h = c // PER, 4 * (c % PER) + place
                if h <= DH:
                    if h:
                        scores(s, h - 1)
                    if h < DH:
                        page(s, h)
                elif c % PER == 2 and place == 3:
                    weights(s)
                elif c % PER == 3:
                    outputs(s, place)

            transposes(0)
            products(0)
            for c in range(CHB):
                update(c, 0)
                pe.wait_ge(pt_ready, at(c + 1))
                pe.wait_ge(rnorm_ready, at(c))
                first = nc.tensor.matmul(psum[:, BO, :], p_t[c % 2][:, :], rv_in[c % 4][:, :], start=True, stop=c % NC == 0)
                if c % NC == 0:
                    first.then_inc(ro_full, 1)
                beside(c, 0)
                if c % NC:
                    for k in range(KT):
                        last = nc.tensor.matmul(psum[:, BO, :], qk_t[c % 2][:, k, :], state[c % 2][:, k, :], start=False,
                                                stop=k == KT - 1)
                    last.then_inc(ro_full, 1)
                update(c, 1)
                if c + 1 < CHB:
                    transposes(c + 1)
                beside(c, 1)
                if c + 1 < CHB:
                    products(c + 1)
                beside(c, 2)
                if c:
                    rows_out(c - 1)
                beside(c, 3)
            rows_out(CHB - 1)
        pe.wait_ge(s_norm, 1)
        nc.tensor.matmul(psum[:, BS, :], ones_sq[:, :], o_square[:, :, :], start=True, stop=True).then_inc(s_norm, 1)

    def act_mixers(act):
        act.wait_ge(new_full, 1)
        nc.scalar.copy(k_new_t[:, :, :], psum[:, BS, :].rearrange("p (h t) -> p h t", h=DH)).then_inc(new_t_ready[0], 1)

        with act.Fori(0, N_BODY3) as i:
            def at(c):
                return i * CHB + c

            def chunk_t(c):
                act.wait_ge(rt_full, at(c + 1))
                act.wait_ge(ro_full, at(c - 1 if c else c))
                nc.scalar.copy(qk_t[c % 2][:, :, :], psum[:, BT, :].rearrange("p (k n) -> p k n", n=128)).then_inc(rt_read, 1)

            def chunk_decay(c):
                act.wait_ge(rd_loaded[c // NC], i * 16 + 16)
                act.wait_ge(upd_full, i * (2 * CHB) + 2 * (c - 1 if c else c))
                nc.scalar.activation(k_dec[c % 2][:, :], rk_in[c % 4][:, :], ACT.Copy,
                                     scale=decay[c // NC][:, 129:130]).then_inc(kd_ready, 1)

            def page(c, place):
                s, h = c // PER, 4 * (c % PER) + place
                if h < DH:
                    act.wait_ge(page_full, i * (SQB * DH) + (s * DH + h + 1))
                    nc.scalar.copy(page_t[h % 2][:, :], psum[:, BP, :]).then_inc(page_ready, 1)

            chunk_t(0)
            chunk_decay(0)
            for c in range(CHB):
                s = c // PER
                page(c, 0)
                if c % PER == 2:
                    act.wait_ge(s_max, i * SQB + (s + 1))
                    nc.scalar.activation(s_prob[:, :], psum[:, BS:BS + 2, :].rearrange("p b n -> p (b n)")[:, 0:PAST + TS],
                                         ACT.Exp, bias=s_neg_max[:, :], accum_out=s_sum[:, :]).then_inc(s_exp, 1)
                act.wait_ge(ro_full, at(c + 1))
                act.wait_ge(rsq_ready, at(c))
                act.wait_ge(rvar_ready, at(c - 1) if c else at(c))
                nc.scalar.activation(r_square[:, :], psum[:, BO, :], ACT.Square, scale=decay[c // NC][:, 128:129],
                                     accum_out=r_sq[c % 2][:, :]).then_inc(rsq_ready, 1)
                if c + 1 < CHB:
                    chunk_t(c + 1)
                page(c, 1)
                if c + 1 < CHB:
                    chunk_decay(c + 1)
                page(c, 2)
                page(c, 3)
                if c % PER == 2:
                    act.wait_ge(s_mix_full, i * SQB + (s + 1))
                    nc.scalar.copy(s_mix_t[:, 0:NPG, :], psum[:, BM, 0:NPG * TS].rearrange("p (b n) -> p b n", b=NPG))
                    nc.scalar.copy(s_mix_t[0:TS, NPG, :], psum[0:TS, BM, NPG * TS:(NPG + 1) * TS]).then_inc(s_mix_ready, 1)
        act.wait_ge(s_norm, 3)
        nc.scalar.activation(o_square[:, :, :], o_square[:, :, :], ACT.Sqrt).then_inc(s_norm, 1)

    def dve_mixers(dve):
        dstep.done(nc.vector.memset(q_wide[:, :], 0.0))
        dstep.done(nc.vector.memset(ones_sq[:, :], 1.0))
        dve.wait_ge(new_loaded, 80)
        dstep.done(nc.vector.scalar_tensor_tensor(s_sign[:, :], comb[:, TS + 1:TS + 2], neg_lam[:, :], comb[:, TS:TS + 1],
                                                  ALU.mult, ALU.add))
        dve.wait_ge(new_full, 2)
        nc.vector.tensor_copy(q_new_t[:, :, :], psum[:, BS + 1, :].rearrange("p (h t) -> p h t", h=DH)).then_inc(
            new_t_ready[1], 1)
        dve.wait_ge(new_t_ready[1], 1)
        dstep.wait(dve)

        with dve.Fori(0, N_BODY3) as i:
            def at(c):
                return i * CHB + c

            dstep.loop(i, 2 * SQB)

            def between(c):
                dve.wait_ge(rd_loaded[c // NC], i * 16 + 16)
                dve.wait_ge(qk_full, at(c + 1))
                nc.vector.tensor_tensor(p_t[c % 2][:, :], psum[:, BT, 0:128], decay[c // NC][:, 0:128],
                                        ALU.mult).then_inc(pt_ready, 1)

            def new_state(c, k):
                new, n = state[(c + 1) % 2][:, k, :], c % NC
                dve.wait_ge(upd_full, i * (2 * CHB) + (2 * c + k + 1))
                if n == 1:
                    dve.wait_ge(state_stored, i * 32 + 16 * (c // NC))
                if n:
                    dve.wait_ge(state_ready, i * (2 * CHB) + (2 * c))
                    last = nc.vector.scalar_tensor_tensor(new, state[c % 2][:, k, :], decay[c // NC][:, 130:131],
                                                          psum[:, BU, :], ALU.mult, ALU.add)
                else:
                    last = nc.vector.tensor_copy(new, psum[:, BU, :])
                last.then_inc(state_ready, 1)

            def variance(c):
                dve.wait_ge(rsq_ready, at(c + 1))
                dve.wait_ge(rrstd_ready, at(c))
                nc.vector.tensor_scalar(r_var[:, :], r_sq[c % 2][:, :], 1.0 / RV, EPS, ALU.mult, ALU.add).then_inc(rvar_ready, 1)

            def normalise(c):
                dve.wait_ge(rrstd_ready, at(c + 1))
                dve.wait_ge(rr_full, at(c - 1 if c else c))
                nc.vector.tensor_scalar(r_rows[c % 2][:, :], psum[:, BO, :], decay[c // NC][:, 128:129], r_rstd[:, :],
                                        ALU.mult, ALU.mult).then_inc(rnorm_ready, 1)

            def gated(c):
                dve.wait_ge(rr_full, at(c + 1))
                dve.wait_ge(rg_loaded[c % 4], i * (CHB * 4) + 16 * (c // 4 + 1))
                slot = r_gate[c % 4][:, :, :].rearrange("p b n -> p (b n)")
                nc.vector.tensor_tensor(slot, psum[:, BR, :], slot, ALU.mult).then_inc(r_ready, 1)

            def widen(s):
                for c in range(2):
                    r = slice(c * DHD, (c + 1) * DHD)
                    last = nc.vector.tensor_scalar(
                        q_wide[r, :].rearrange("p (h x) -> p h x", x=144)[:, :, c * DS:(c + 1) * DS],
                        q_new_t[r, :, bass.ds(i * (SQB * DS) + s * DS, DS)], DHD ** -0.5, None, ALU.mult)
                last.then_inc(wide_ready, 1)

            def maximum(s):
                dve.wait_ge(s_full, i * SQB + (s + 1))
                dstep.done(nc.vector.tensor_tensor(psum[:, BS + 1, 0:TS], psum[:, BS + 1, 0:TS],
                                                   new_mask[:, bass.ds(i * SQB + s, 1), :].rearrange("p o n -> p (o n)"), ALU.add))
                dstep.wait(dve)
                nc.vector.tensor_reduce(s_neg_max[:, :], psum[:, BS:BS + 2, :].rearrange("p b n -> p (b n)")[:, 0:PAST + TS],
                                        AX.X, ALU.max, negate=True).then_inc(s_max, 1)

            def combination(s):
                dve.wait_ge(s_exp, i * SQB + (s + 1))
                dstep.done(nc.vector.reciprocal(s_recip[:, :], s_sum[:, :]))
                dstep.wait(dve)
                nc.vector.tensor_scalar(s_comb[:, :], comb[:, 0:TS], s_recip[:, :], s_sign[:, :], ALU.mult,
                                        ALU.mult).then_inc(s_comb_ready, 1)

            between(0)
            for c in range(CHB):
                s = c // PER
                if c % PER == 0:
                    widen(s)
                new_state(c, 0)
                if c % PER == 2:
                    maximum(s)
                new_state(c, 1)
                variance(c)
                if c % PER == 2:
                    combination(s)
                if c + 1 < CHB:
                    between(c + 1)
                normalise(c)
                if c:
                    gated(c - 1)
                if c % PER == PER - 1:
                    dve.wait_ge(s_out_full, i * SQB + (s + 1))
                    nc.vector.tensor_scalar(o_new[:, :, bass.ds(i * (SQB * DS) + s * DS, DS)],
                                            psum[:, BM, 384:384 + TS].rearrange("p (h t) -> p h t", h=DH), 1.0, None,
                                            ALU.mult).then_inc(s_out_read, 1)
            gated(CHB - 1)
            dstep.end(N_BODY3)
        dve.wait_ge(s_out_read, DB)
        nc.vector.tensor_tensor(o_square[:, :, :], o_new[:, :, :], o_new[:, :, :], ALU.mult).then_inc(s_norm, 1)
        dve.wait_ge(s_norm, 2)
        nc.vector.tensor_scalar(o_square[:, :, :], psum[:, BS, :].rearrange("p (h t) -> p h t", h=DH), 1.0 / DV, EPS,
                                ALU.mult, ALU.add).then_inc(s_norm, 1)
        dve.wait_ge(s_norm, 4)
        dstep.done(nc.vector.reciprocal(o_square[:, :, :], o_square[:, :, :]))
        dstep.wait(dve)
        nc.vector.scalar_tensor_tensor(o_square[:, :, :], o_new[:, :, :], sub_gain[:, :], o_square[:, :, :], ALU.mult,
                                       ALU.mult).then_inc(s_norm, 1)

    def pool_retention(pool):
        with pool.Fori(0, RH * NC) as i:
            pool.wait_ge(rvar_ready, i + 1)
            nc.gpsimd.tensor_tensor(r_rstd[:, :], r_var[:, :], exponent[:, 0:1], ALU.pow).then_inc(rrstd_ready, 1)

    n_at = [0]

    def n_view(p, *shape):
        width = math.prod(shape)
        x = acc1[0:p, n_at[0]:n_at[0] + width]
        n_at[0] += width
        assert n_at[0] <= NT * D
        return x.rearrange("p (a b) -> p a b", a=shape[0]) if len(shape) == 2 else x

    n_state = [n_view(128, KT, RV) for _ in range(4)]
    nq_in, nk_in, nv_in = n_view(TS, RK), n_view(TS, RK), n_view(TS, RV)
    n_decay = n_view(TS, TS + DB)
    n_qdec = n_view(128, TS)
    n_decay8 = n_view(128, 4)
    nqk_t = n_view(128, 2 * KT, TS)
    q_own = n_view(128, KT, DB * (TS + DS))
    np_t = n_view(TS, TS)
    nk_dec = [n_view(TS, RK) for _ in range(2)]
    nr_rows = n_view(TS, RV)
    nr_gate = n_view(128, VT, TS)
    nr_var, nr_rstd, nr_z = n_view(TS, 1), n_view(TS, 1), n_view(TS, 1)

    n_loaded = sem("n_loaded")
    nv_loaded = sem("nv_loaded")
    ng_loaded = sem("ng_loaded")
    n_stored = sem("n_stored")
    ns_loaded = [sem(f"ns_loaded{s}") for s in range(4)]
    ns_stored = [sem(f"ns_stored{s}") for s in range(4)]
    sp_step = sem("sp_step")
    pe_step = sem("pe_step")
    nt_full = sem("nt_full")
    nt_read = sem("nt_read")
    nq_ready = sem("nq_ready")
    nqk_full = sem("nqk_full")
    np_ready = sem("np_ready")
    nk_ready = sem("nk_ready")
    nu_full = sem("nu_full")
    ns_ready = sem("ns_ready")
    nr_full = sem("nr_full")
    nr_read = sem("nr_read")
    nr_step = sem("nr_step")
    nn_ready = sem("nn_ready")
    nrr_full = sem("nrr_full")
    n_ready = sem("n_ready")

    def state_rows(x, i, b):
        return x[0, b, bass.ds(i, 1), :, :].rearrange("o (k p) e -> p (o k) e", p=128)

    def sp_n_inputs(sp, i, d):
        sp.wait_ge(nk_ready, i * DB + DB * d)
        sp.wait_ge(np_ready, i + d)
        sp.wait_ge(nq_ready, i + d)
        for x, col in ((nq_in, QR), (nk_in, KR)):
            sp.dma_start(x, proj[TP:T, bass.ds(i * RK + (d * RK + col), RK)]).then_inc(n_loaded, 16)
        sp.dma_start(n_decay, c_ret_new[bass.ds(i + d, 1), :, :].rearrange("o p n -> (o p) n")).then_inc(n_loaded, 16)
        sp.dma_start(n_qdec, c_ret_qdec[bass.ds(i + d, 1), :, :].rearrange("o p n -> (o p) n")).then_inc(n_loaded, 16)
        sp.wait_ge(ns_ready, i * (2 * DB) + 2 * DB * d)
        sp.dma_start(nv_in, proj[TP:T, bass.ds(i * RV + (d * RV + VR), RV)]).then_inc(nv_loaded, 16)
        sp.dma_start(n_decay8, c_ret[bass.ds(i + d, 1), :, 128:132].rearrange("o p n -> (o p) n")).then_inc(nv_loaded, 16)

    def sp_n_load_state(sp, i, b):
        sp.wait_ge(ns_stored[b % 4], i * 32 + 16 * (b // 4 + 1))
        sp.dma_start(n_state[b % 4], state_rows(state_ret, i + b // DB, b % DB)).then_inc(ns_loaded[b % 4], 16)

    def sp_n_begin(sp):
        for s in range(4):
            sp.sem_inc(ns_stored[s], 16)
        sp.sem_inc(n_stored, 16)
        sp_n_inputs(sp, 0, 0)
        for b in range(2):
            sp_n_load_state(sp, 0, b)

    def sp_n_unit(sp, i, m, last):
        if m:
            sp.wait_ge(ns_ready, i * (2 * DB) + 2 * m)
            sp.sem_inc(sp_step, 1)
            sp.dma_start(state_rows(ret_sample, i, m - 1), n_state[(m - 1) % 4]).then_inc(ns_stored[(m - 1) % 4], 16)
        if not (last and m + 2 >= DB):
            sp_n_load_state(sp, i, m + 2)
        if m == 5:
            sp.wait_ge(n_stored, i * 16 + 16)
            sp.sem_inc(sp_step, 1)
            for s in range(2):
                sp.wait_ge(gate_stored[s], i * 32 + 48)
                sp.sem_inc(sp_step, 1)
            sp.dma_start(nr_gate, gates[bass.ds(i * RV, RV), TP:T].rearrange("(b e) n -> e b n", e=128)).then_inc(
                ng_loaded, 16)
        if m == DB - 1:
            if not last:
                sp_n_inputs(sp, i, 1)
            sp.wait_ge(ns_ready, i * (2 * DB) + 2 * DB)
            sp.dma_start(state_rows(ret_sample, i, m), n_state[m % 4]).then_inc(ns_stored[m % 4], 16)

    def sp_n_end(sp, i):
        sp.wait_ge(n_ready, i + 1)
        sp.dma_start(r_t[bass.ds(i * RV, RV), TP:T].rearrange("(b e) n -> e b n", e=128), nr_gate).then_inc(n_stored, 16)

    def pe_n_piece(pe, i, m, k):
        first = m == 0
        if first and k == 0:
            pe.wait_ge(n_loaded, i * 64 + 64)
            pe.wait_ge(n_ready, i)
            pe.sem_inc(pe_step, 1)
            for x, a in ((nq_in, 0), (nk_in, KT)):
                for b in range(KT):
                    last = nc.tensor.transpose(psum[:, 6, (a + b) * TS:(a + b + 1) * TS], x[:, b * 128:(b + 1) * 128],
                                               ident[0:TS, 0:TS])
            last.then_inc(nt_full, 1)
        if first and k == 2:
            pe.wait_ge(nt_read, i + 1)
            for b in range(KT):
                last = nc.tensor.matmul(psum[0:TS, 6, 0:TS], nqk_t[:, KT + b, :], nqk_t[:, b, :], start=b == 0,
                                        stop=b == KT - 1)
            last.then_inc(nqk_full, 1)
        if k == (4 if first else 0):
            if first:
                pe.wait_ge(np_ready, i + 1)
                pe.wait_ge(nq_ready, i + 1)
                pe.wait_ge(nr_read, i * 2)
                pe.wait_ge(nv_loaded, i * 32 + 32)
            pe.wait_ge(ns_loaded[m % 4], i * 32 + 16 * (m // 4 + 1))
            for b in range(KT):
                last = nc.tensor.matmul(psum[0:TS, 7, :], q_own[:, b, m * TS:(m + 1) * TS], n_state[m % 4][:, b, :],
                                        start=first and b == 0, stop=m == DB - 1 and b == KT - 1)
            if first:
                nc.tensor.matmul(psum[0:TS, 7, :], np_t, nv_in, start=False, stop=False)
            if m == DB - 1:
                last.then_inc(nr_full, 1)
        if k in ((5, 7) if first else (2, 4)):
            b = 1 if k in (7, 4) else 0
            pe.wait_ge(nk_ready, i * DB + (m + 1))
            pe.wait_ge(ns_ready, i * (2 * DB) + (2 * m + b))
            pe.sem_inc(pe_step, 1)
            nc.tensor.matmul(psum[:, 6, :], nk_dec[m % 2][:, b * 128:(b + 1) * 128], nv_in, start=True,
                             stop=True).then_inc(nu_full, 1)

    def pe_n_end(pe, i):
        pe.wait_ge(nn_ready, i + 1)
        pe.wait_ge(ns_ready, i * (2 * DB) + 2 * DB)
        pe.sem_inc(pe_step, 1)
        for v in range(VT):
            last = nc.tensor.transpose(psum[:, 6, v * TS:(v + 1) * TS], nr_rows[:, v * 128:(v + 1) * 128], ident[0:TS, 0:TS])
        last.then_inc(nrr_full, 1)

    def act_n_unit(act, i, m):
        if m == 0:
            act.wait_ge(nt_full, i + 1)
            nc.scalar.copy(nqk_t, psum[:, 6, 0:2 * KT * TS].rearrange("p (k n) -> p k n", n=TS)).then_inc(nt_read, 1)
        for b in ((0, 1) if m == 0 else (m + 1,) if m + 1 < DB else ()):
            act.wait_ge(nu_full, i * (2 * DB) + (2 * (b - 1) if b > 1 else 0))
            nc.scalar.activation(nk_dec[b % 2], nk_in, ACT.Copy, scale=n_decay[:, TS + b:TS + b + 1]).then_inc(nk_ready, 1)
        if m == DB - 1:
            act.wait_ge(nr_full, i + 1)
            nc.scalar.copy(nr_rows, psum[0:TS, 7, :]).then_inc(nr_read, 1)
            act.wait_ge(nr_read, i * 2 + 1)
            nc.scalar.activation(psum[0:TS, 7, :], nr_rows, ACT.Square, accum_out=nr_var).then_inc(nr_read, 1)
            act.wait_ge(nr_step, i * 6 + 1)
            nc.scalar.activation(nr_rstd, nr_var, ACT.Sqrt).then_inc(nr_step, 1)

    def dve_n_unit(dve, i, m):
        if m == 0:
            dve.wait_ge(nt_read, i + 1)
            for b in range(KT):
                last = nc.vector.tensor_tensor(q_own[:, b, :].rearrange("p (b x) -> p b x", x=TS + DS)[:, :, 0:DS],
                                               nqk_t[:, b, :].rearrange("p (b t) -> p b t", t=DS),
                                               n_qdec.rearrange("p (b t) -> p b t", t=DS), ALU.mult)
            last.then_inc(nq_ready, 1)
            dve.wait_ge(nqk_full, i + 1)
            nc.vector.tensor_tensor(np_t, psum[0:TS, 6, 0:TS], n_decay[:, 0:TS], ALU.mult).then_inc(np_ready, 1)
        for b in range(KT):
            dve.wait_ge(nu_full, i * (2 * DB) + (2 * m + b + 1))
            s = n_state[m % 4][:, b, :]
            nc.vector.scalar_tensor_tensor(s, s, n_decay8[:, 3:4], psum[:, 6, :], ALU.mult, ALU.add).then_inc(ns_ready, 1)
        if m == DB - 1:
            v, y, z = nr_var, nr_rstd, nr_z
            dve.wait_ge(nr_read, i * 2 + 2)
            nc.vector.tensor_scalar(v, v, 1.0 / RV, EPS, ALU.mult, ALU.add).then_inc(nr_step, 1)
            dve.wait_ge(nr_step, i * 6 + 2)
            nc.vector.reciprocal(y, y).then_inc(nr_step, 1)
            dve.wait_ge(nr_step, i * 6 + 3)
            nc.vector.scalar_tensor_tensor(z, y, v, y, ALU.mult, ALU.mult).then_inc(nr_step, 1)
            dve.wait_ge(nr_step, i * 6 + 4)
            nc.vector.tensor_scalar(z, z, -0.5, 1.5, ALU.mult, ALU.add).then_inc(nr_step, 1)
            dve.wait_ge(nr_step, i * 6 + 5)
            nc.vector.tensor_tensor(y, y, z, ALU.mult).then_inc(nr_step, 1)
            dve.wait_ge(nr_step, i * 6 + 6)
            nc.vector.tensor_scalar(nr_rows, nr_rows, y, None, ALU.mult).then_inc(nn_ready, 1)

    def dve_n_end(dve, i):
        dve.wait_ge(nrr_full, i + 1)
        dve.wait_ge(ng_loaded, i * 16 + 16)
        nc.vector.tensor_tensor(nr_gate, psum[:, 6, 0:VT * TS].rearrange("p (b n) -> p b n", n=TS), nr_gate,
                                ALU.mult).then_inc(n_ready, 1)

    XIN = [0, T]
    SG = 2 * T
    G_M, G_O, G_O1 = banks_before(W_PA), banks_before(W_O), banks_before(W_O) + NT
    G_GU, G_DN = banks_before(W_GU), banks_before(W_DN)
    N_MERGE = 3
    UNITS = D // 128
    O1_ORDER = []
    for t in range(NT + 2):
        O1_ORDER += [("O", t)] * (t < NT) + [("N", t - 2, b) for b in range(2) if t >= 2]

    def o1_place(*what):
        return G_O1 + O1_ORDER.index(what)

    xin_loaded = [sem("xin_loaded0"), sem("xin_loaded1")]
    xh_ready = sem("xh_ready")
    xt_ready = sem("xt_ready")
    xt_free = sem("xt_free")
    sg_loaded = sem("sg_loaded")
    merged = sem("merged")
    ff_gate = sem("ff_gate")
    ff_mul = sem("ff_mul")
    h_ready = sem("h_ready")
    h_stored = [sem("h_stored0"), sem("h_stored1")]
    y_stored = sem("y_stored")

    def sp_finish(sp):
        sources = [a_t, r_t[0:D, :], r_t[D:2 * D, :]]

        def load_x(q, k):
            n = q * KD + k
            if n >= 2:
                sp.wait_ge(xt_ready, n - 1)
            sp.dma_start(edge[:, XIN[k % 2]:XIN[k % 2] + T], sources[q][k * 128:(k + 1) * 128, :]).then_inc(
                xin_loaded[k % 2], 16)

        load_x(0, 0)
        load_x(0, 1)
        load_w(sp, W_PB)
        sp_load_gain(sp, norm_ffn_g[0])
        for q in range(N_MERGE):
            for f in range(UNITS):
                n = q * UNITS + f
                if n:
                    sp.wait_ge(merged, n)
                row = (G_B if q else G_A) + f * 128
                sp.dma_start(edge[:, SG:SG + T], gates[row:row + 128, :]).then_inc(sg_loaded, 16)
                if n == 0:
                    for k in range(2, KD):
                        load_x(0, k)
                if f == 2 and q:
                    load_w(sp, W_PB + 2 * q)
                if f == 4 and q + 1 < N_MERGE:
                    load_x(q + 1, 0)
                    load_x(q + 1, 1)
                if f == 6:
                    load_w(sp, W_PB + 2 * q + 1)
            if q + 1 < N_MERGE:
                for k in range(2, KD):
                    load_x(q + 1, k)
        sp.wait_ge(xt_ready, (N_MERGE + 1) * KD)
        for t in range(NT):
            sp.dma_start(h_rows[0:rows(t), t, :], token_rows(x_prompt, x_sample, t)).then_inc(x_loaded[t // 3], 16)
        load_w_gu(sp, 0)
        load_w_gu(sp, 1)
        sp.wait_ge(norm_sems["ffn"]["scaled"], NT)
        sp_load_gain(sp, norm_final_g)

        for s in range(2):
            sp.sem_inc(h_stored[s], 16)

        def store_h(i, j):
            sp.wait_ge(h_ready, i * 4 + (j + 1))
            sp.dma_start(h_t[bass.ds(i * 512 + j * 128, 128), :], edge[:, XIN[j % 2]:XIN[j % 2] + T]).then_inc(
                h_stored[j % 2], 16)

        with sp.Fori(0, N_GU // 2 - 1) as i:
            for j in range(4):
                if j % 2 == 0:
                    load_w_gu(sp, i * 2 + (2 + j // 2))
                store_h(i, j)
        i = N_GU // 2 - 1
        for j in range(4):
            if j == 0:
                load_w_gu(sp, N_GU - 1)
            if j == 2:
                load_w(sp, W_DN)
            store_h(i, j)
        load_w(sp, W_DN + 1)
        store_h(N_GU // 2, 0)

        def load_h(c, t):
            n, nk, k0 = c * NT + t, DOWN_K[c], sum(DOWN_K[:c])
            if n >= 2:
                sp.wait_ge(xt_ready, (N_MERGE + 1) * KD + n - 1)
            sp.dma_start(edge[:, XIN[n % 2]:XIN[n % 2] + nk * rows(t)].rearrange("p (k n) -> p k n", k=nk),
                         h_t[k0 * 128:(k0 + nk) * 128, t * 128:t * 128 + rows(t)].rearrange(
                             "(k p) n -> p k n", p=128)).then_inc(xin_loaded[n % 2], 16)

        n_block = 2 * N_GU
        sp.wait_ge(h_stored[0], 16 * (1 + n_block // 2))
        load_h(0, 0)
        store_h(N_GU // 2, 1)
        sp.wait_ge(h_stored[1], 16 * (1 + n_block // 2))
        for t in range(1, NT):
            load_h(0, t)
        load_w(sp, W_DN + 2)
        load_w(sp, W_DN + 3)
        for c in range(1, len(DOWN_K)):
            for t in range(NT):
                load_h(c, t)
                if c + 1 < len(DOWN_K) and t == 4:
                    load_w(sp, W_DN + 2 * c + 2)
            if c + 1 < len(DOWN_K):
                load_w(sp, W_DN + 2 * c + 3)
        for t in range(NT):
            sp.wait_ge(norm_sems["final"]["scaled"], t + 1)
            sp.dma_start(token_rows(y_prompt, y_sample, t), h_rows[0:rows(t), t, :]).then_inc(y_stored, 16)
        sp.wait_ge(y_stored, 16 * NT)

    def pe_finish(pe):
        with pe.Fori(0, N_MERGE) as i:
            for j in range(2):
                pe_feature_tile(pe, xt_h2, xt_l2, j, i * 4 + (2 * (W_PA + j) + 1),
                                lambda c: (i * 24 + (G_M + 12 * j + c), (G_M + 12 * j + c) % RING),
                                free=xt_free if j else None,
                                ready=None if j else lambda k: (xt_ready, i * KD + (k + 1)))
        pe_token_tile(pe, xt_h2, xt_l2, xs_hl2, 0, 2 * W_O + 1, lambda t: (G_O + t, (G_O + t) % RING),
                      ready=lambda t, k: (xt_ready, N_MERGE * KD + k + 1) if t == 0 else None)

        def behind(t):
            if t >= 2:
                pe_norm_tile(pe, "ffn", t - 2, lambda b: o1_place("N", t - 2, b))

        pe_token_tile(pe, xt_h2, xt_l2, xs_hl2, 1, 2 * (W_O + 1) + 1, lambda t: (o1_place("O", t), o1_place("O", t) % RING),
                      behind=behind)
        behind(NT)
        behind(NT + 1)
        pe.wait_ge(bank_free, RING + G_GU)

        def gate_up(i, j, free=None):
            pe_feature_tile(pe, xt_h2, xt_l2, j, i * 4 + (2 * (W_GU + j) + 1),
                            lambda c: (i * 24 + (G_GU + 12 * j + c), (G_GU + 12 * j + c) % RING), order=(0, 2, 1, 3))

        with pe.Fori(0, N_GU // 2) as i:
            gate_up(i, 0)
            gate_up(i, 1)
        gate_up(N_GU // 2, 0)
        for w in range(W_DN, N_W):
            c, n = divmod(w - W_DN, 2)
            g = banks_before(w)
            pe_token_tile(pe, xt_h2, xt_l2, xs_hl2, w % 2, 2 * w + 1, lambda t: (g + t, (g + t) % RING), DOWN_K[c],
                          ready=lambda t, k: (xt_ready, (N_MERGE + 1) * KD + c * NT + t + 1) if k == 0 and n == 0 else None)

    def act_half(act, g, n):
        act.wait_ge(bank_full, g + 1)
        nc.scalar.copy(edge[0:TS, 2560:3072], psum[TS:2 * TS, g % RING, :]).then_inc(half_ready, 1)
        act.wait_ge(half_ready, n)

    def act_finish(act):
        for q in range(N_MERGE + 1):
            for k in range(KD):
                n = q * KD + k
                if q:
                    if k < KD - 1:
                        act.wait_ge(xt_free, (q - 1) * (KD - 1) + k + 1)
                    else:
                        act.wait_ge(bank_full, G_M + q * 24)
                if q < N_MERGE:
                    act.wait_ge(xin_loaded[k % 2], q * 64 + 16 * (k // 2 + 1))
                    nc.scalar.copy(xt_h2[:, k, :], edge[:, XIN[k % 2]:XIN[k % 2] + T]).then_inc(xh_ready, 1)
                else:
                    act.wait_ge(merged, (N_MERGE - 1) * UNITS + k + 1)
                    nc.scalar.copy(xs_hl2[:, k, 0:TS], m_t[:, k, TP:T])
                    nc.scalar.copy(xt_h2[:, k, 0:TP], m_t[:, k, 0:TP]).then_inc(xh_ready, 1)
        act_half(act, G_O + SAMPLE, N_TM + 1)
        for t in range(NT + 2):
            if t == SAMPLE:
                act.wait_ge(norm_sems["ffn"]["squares"], t)
                act_half(act, o1_place("O", t), N_TM + 2)
            if 1 <= t <= NT:
                act_deviation(act, "ffn", t - 1)
            if t < NT:
                act.wait_ge(bank_free, RING + o1_place("O", t) + 1)
                act_square(act, "ffn", h_rows, t)
            if t >= 2:
                act_high_tile(act, "ffn", t - 2, lambda b: o1_place("N", t - 2, b), xt_h2, xs_hl2)

        def gate_unit(i, u):
            for c, (a, width) in enumerate(CHUNKS):
                g = G_GU + 6 * u + c
                act.wait_ge(bank_full, i * 24 + (g + 1))
                act.wait_ge(ff_mul, i * 24 + (6 * u))
                nc.scalar.activation(edge[:, SG + a:SG + a + width], psum[:, g % RING, 0:width],
                                     ACT.Sigmoid).then_inc(ff_gate, 1)

        with act.Fori(0, N_GU // 2) as i:
            for u in range(4):
                gate_unit(i, u)
        gate_unit(N_GU // 2, 0)
        gate_unit(N_GU // 2, 1)

        def high(c, t):
            n, nk = c * NT + t, DOWN_K[c]
            if c == 0:
                act.wait_ge(bank_full, G_DN)
            else:
                act.wait_ge(bank_full, banks_before(W_DN + 2 * c - 1) + t + 1)
            act.wait_ge(xin_loaded[n % 2], 16 * (N_MERGE * KD // 2 + n // 2 + 1))
            dst = xs_hl2[:, 0:nk, 0:TS] if t == SAMPLE else xt_h2[:, 0:nk, t * 128:(t + 1) * 128]
            nc.scalar.copy(dst, edge[:, XIN[n % 2]:XIN[n % 2] + nk * rows(t)].rearrange("p (k n) -> p k n", k=nk)).then_inc(
                xh_ready, 1)

        for t in range(NT):
            high(0, t)
        for w in range(W_DN, N_W):
            c, n = divmod(w - W_DN, 2)
            g = banks_before(w)
            if n and c + 1 < len(DOWN_K):
                for t in range(NT - 1):
                    high(c + 1, t)
            if w == N_W - 1:
                for t in range(NT - 1):
                    act.wait_ge(bank_free, RING + g + t + 1)
                    act_square(act, "final", h_rows, t)
                    if t:
                        act_deviation(act, "final", t - 1)
                act.wait_ge(norm_sems["final"]["squares"], NT - 1)
            act_half(act, g + SAMPLE, N_TM + 3 + w - W_DN)
            if n and c + 1 < len(DOWN_K):
                high(c + 1, SAMPLE)
        act_deviation(act, "final", SAMPLE - 1)
        act.wait_ge(bank_free, RING + banks_before(N_W))
        act_square(act, "final", h_rows, SAMPLE)
        act_deviation(act, "final", SAMPLE)

    def dve_finish(dve):
        def refill(q, k):
            n = q * KD + k
            dve.wait_ge(xh_ready, n + 1)
            if q < N_MERGE:
                nc.vector.tensor_tensor(xt_l2[:, k, :], edge[:, XIN[k % 2]:XIN[k % 2] + T], xt_h2[:, k, :].bitcast(F),
                                        ALU.subtract).then_inc(xt_ready, 1)
            else:
                nc.vector.tensor_tensor(xs_hl2[:, k, TS:2 * TS], m_t[:, k, TP:T], xs_hl2[:, k, 0:TS].bitcast(F), ALU.subtract)
                nc.vector.tensor_tensor(xt_l2[:, k, 0:TP], m_t[:, k, 0:TP], xt_h2[:, k, 0:TP].bitcast(F),
                                        ALU.subtract).then_inc(xt_ready, 1)

        for k in range(KD):
            refill(0, k)
        for q in range(N_MERGE):
            for f in range(UNITS):
                n = q * UNITS + f
                if f == UNITS - 1:
                    for k in range(KD - 1):
                        refill(q + 1, k)
                dve.wait_ge(sg_loaded, 16 * (n + 1))
                for c, (a, width) in enumerate(CHUNKS):
                    g = G_M + 3 * n + c
                    dve.wait_ge(bank_full, g + 1)
                    gate = edge[:, SG + a:SG + a + width]
                    nc.vector.tensor_tensor(gate if q else m_t[:, f, a:a + width], psum[:, g % RING, 0:width], gate,
                                            ALU.mult).then_inc(bank_free, 1)
                dve.wait_ge(bank_free, RING + G_M + 3 * (n + 1))
                if q:
                    nc.vector.tensor_tensor(m_t[:, f, :], m_t[:, f, :], edge[:, SG:SG + T], ALU.add).then_inc(merged, 1)
                else:
                    dve.sem_inc(merged, 1)
                if f == UNITS - 1:
                    refill(q + 1, KD - 1)

        def add_rows(t, n, g, half):
            h = h_rows[0:rows(t), t, n * WN:(n + 1) * WN]
            dve.wait_ge(bank_full, g + 1)
            if t == SAMPLE:
                dve.wait_ge(half_ready, half)
                dstep.done(nc.vector.tensor_tensor(h, h, edge[0:TS, 2560:3072], ALU.add))
                dstep.wait(dve)
            nc.vector.tensor_tensor(h, h, psum[0:rows(t), g % RING, :], ALU.add).then_inc(bank_free, 1)

        for t in range(NT):
            dve.wait_ge(x_loaded[t // 3], 96)
            add_rows(t, 0, G_O + t, N_TM + 1)
        dve.wait_ge(gain_loaded, 32)
        for t in range(NT + 2):
            if t < NT:
                add_rows(t, 1, o1_place("O", t), N_TM + 2)
            if 1 <= t <= NT:
                dve_rstd(dve, "ffn", t - 1)
                dve_scale_tile(dve, "ffn", h_rows, t - 1, lambda b: o1_place("N", t - 3, b))
            if t >= 2:
                dve_low_tile(dve, "ffn", t - 2, lambda b: o1_place("N", t - 2, b), xt_h2, xt_l2, xs_hl2)

        def gated_unit(i, u):
            for c, (a, width) in enumerate(CHUNKS):
                g = G_GU + 6 * u + c
                sg = edge[:, SG + a:SG + a + width]
                dve.wait_ge(ff_gate, i * 12 + (3 * u + c + 1))
                nc.vector.tensor_tensor(sg, psum[:, g % RING, 0:width], sg, ALU.mult).then_inc(ff_mul, 1)
                dve.wait_ge(ff_mul, i * 24 + (6 * u + c + 1))
                dve.sem_inc(bank_free, 1)
            dve.wait_ge(h_stored[u % 2], i * 32 + 16 * (u // 2 + 1))
            for c, (a, width) in enumerate(CHUNKS):
                g = G_GU + 6 * u + 3 + c
                dve.wait_ge(bank_full, i * 24 + (g + 1))
                nc.vector.tensor_tensor(edge[:, XIN[u % 2] + a:XIN[u % 2] + a + width], psum[:, g % RING, 0:width],
                                        edge[:, SG + a:SG + a + width], ALU.mult).then_inc(ff_mul, 1)
                dve.wait_ge(ff_mul, i * 24 + (6 * u + 3 + c + 1))
                dve.sem_inc(bank_free, 1)
            dve.sem_inc(h_ready, 1)

        with dve.Fori(0, N_GU // 2) as i:
            for u in range(4):
                gated_unit(i, u)
        gated_unit(N_GU // 2, 0)
        gated_unit(N_GU // 2, 1)

        def low(c, t):
            n, nk = c * NT + t, DOWN_K[c]
            dve.wait_ge(xh_ready, (N_MERGE + 1) * KD + n + 1)
            src = edge[:, XIN[n % 2]:XIN[n % 2] + nk * rows(t)].rearrange("p (k n) -> p k n", k=nk)
            if t == SAMPLE:
                dst, high = xs_hl2[:, 0:nk, TS:2 * TS], xs_hl2[:, 0:nk, 0:TS]
            else:
                dst, high = xt_l2[:, 0:nk, t * 128:(t + 1) * 128], xt_h2[:, 0:nk, t * 128:(t + 1) * 128]
            nc.vector.tensor_tensor(dst, src, high.bitcast(F), ALU.subtract).then_inc(xt_ready, 1)

        for t in range(3):
            low(0, t)
        for w in range(W_DN, N_W):
            c, n = divmod(w - W_DN, 2)
            for t in range(NT):
                if c == 0 and n == 0 and t + 3 < NT:
                    low(0, t + 3)
                add_rows(t, n, banks_before(w) + t, N_TM + 3 + w - W_DN)
                if n and c + 1 < len(DOWN_K):
                    low(c + 1, t)
                if w == N_W - 1:
                    if t == 0:
                        dve.wait_ge(gain_loaded, 48)
                    if t:
                        finish_rows(dve, t - 1)
        finish_rows(dve, SAMPLE)

    def finish_rows(dve, t):
        dve_rstd(dve, "final", t)
        h = h_rows[0:rows(t), t, :]
        nc.vector.scalar_tensor_tensor(h, h, rstd[0:rows(t), t:t + 1], gain[0:rows(t), :], ALU.mult,
                                       ALU.mult).then_inc(norm_sems["final"]["scaled"], 1)

    @block.gpsimd
    def _(pool):
        gpsimd_program(pool)

    @block.sync
    def _(sp):
        sp_project(sp)
        end_stage(sp, 1)
        sp_attention(sp)
        end_stage(sp, 2)
        sp_mixers(sp)
        end_stage(sp, 3)
        sp_finish(sp)

    @block.tensor
    def _(pe):
        pe_project(pe)
        end_stage(pe, 1)
        pe_attention(pe)
        end_stage(pe, 2)
        pe_mixers(pe)
        end_stage(pe, 3)
        pe_finish(pe)

    @block.scalar
    def _(act):
        act_project(act)
        act.wait_ge(bank_free, RING + banks_before(W_PA))
        end_stage(act, 1)
        act_attention(act)
        end_stage(act, 2)
        act_mixers(act)
        end_stage(act, 3)
        act_finish(act)

    @block.vector
    def _(dve):
        dve_project(dve)
        dve.wait_ge(bank_free, RING + G_FM + 48)
        end_stage(dve, 1)
        dve_attention(dve)
        end_stage(dve, 2)
        dve_mixers(dve)
        end_stage(dve, 3)
        dve_finish(dve)

    ctx.close()


def tables():
    f = np.float32
    pos = np.concatenate([np.arange(TP), np.tile(np.arange(DS) + PAST, DB)]).astype(f)
    pad = np.concatenate([pos, np.zeros(NT * 128 - T, f)])

    def tiles(x):
        return np.ascontiguousarray(x.reshape(NT, 128, *x.shape[1:]).swapaxes(0, 1))

    def exp(arg):
        return np.exp(arg.astype(f).astype(np.float64)).astype(f)

    freq = exp(f(-math.log(500000.0)) * np.arange(8, dtype=f) * f(2.0 / 16))
    ang = (pad[:, None] * freq[None, :]).astype(f).astype(np.float64)
    cos, sin = np.cos(ang).astype(f), np.sin(ang).astype(f)
    rope_diff = tiles(np.stack([np.concatenate([cos, cos], 1), np.concatenate([-sin, sin], 1)], 1))
    freq = exp(f(-math.log(10000.0)) * (np.arange(RK // 2, dtype=f) * (f(1) / f(RK // 2 - 1))))
    ang = (pad[:, None] * freq[None, :]).astype(f).astype(np.float64)
    cos, sin = np.cos(ang).astype(f), np.sin(ang).astype(f)
    rope_ret = tiles(np.stack([np.repeat(cos, 2, 1), np.stack([-sin, sin], 2).reshape(-1, RK)], 1))

    i = np.arange(128)
    causal = np.where(i[:, None] >= i[None, :], 0.0, NEG).astype(f)
    tok = i % DS
    new = np.arange(TS)
    new_mask = np.stack([np.where((new[None, :] // DS == b) & (new[None, :] % DS <= tok[:, None]), 0.0, NEG)
                         for b in range(DB)], 1).astype(f)
    comb = (np.arange(TS)[None, :] == (i // 16 * DS + tok)[:, None]).astype(f)
    comb = np.concatenate([comb, (i // DS % 2 == 0)[:, None], (i // DS % 2 == 1)[:, None]], 1).astype(f)

    lg = np.log(f(1) - np.exp2(f(-5) - np.arange(RH, dtype=f)).astype(f)).astype(f).astype(np.float64)
    k_scale = RK ** -0.5
    ret = np.zeros((RH, 128, 132), f)
    ret_new = np.zeros((RH, TS, TS + DB), f)
    qdec = np.zeros((RH, 128, TS), f)
    rel = i[None, :] - i[:, None]
    nrel = new[None, :] % DS - new[:, None] % DS
    same = new[None, :] // DS == new[:, None] // DS
    for h in range(RH):
        ret[h, :, 0:128] = np.where(rel >= 0, np.exp(-(i[:, None] + 1) * lg[h]), 0) * k_scale
        ret[h, :, 128] = np.exp((i + 1) * lg[h])
        ret[h, :, 129] = np.exp((CH - 1 - i) * lg[h]) * k_scale
        ret[h, :, 130] = np.exp(CH * lg[h])
        ret[h, :, 131] = np.exp(DS * lg[h])
        ret_new[h, :, 0:TS] = np.where(same & (nrel >= 0), np.exp(lg[h] * np.maximum(nrel, 0)), 0) * k_scale
        ret_new[h, :, TS:] = np.where(new[:, None] // DS == np.arange(DB)[None, :],
                                      np.exp((DS - 1 - new % DS) * lg[h])[:, None] * k_scale, 0)
        qdec[h] = np.exp((new % DS + 1) * lg[h])[None, :]
    return {"c_ident": np.eye(128, dtype=f), "c_rope_diff": rope_diff, "c_rope_ret": rope_ret,
            "c_causal": causal, "c_new_mask": np.ascontiguousarray(new_mask), "c_comb": comb,
            "c_ret": ret, "c_ret_new": ret_new, "c_ret_qdec": qdec}


_INS = ["x_prompt", "x_sample", "cache_k", "cache_v", "state_ret", "page_table", "norm_mix_g", "w_in", "b_gate",
        "lambda_q1", "lambda_k1", "lambda_q2", "lambda_k2", "subln_g", "w_pa", "w_pb", "w_o", "norm_ffn_g",
        "w_gu", "w_down", "norm_final_g"]
_OUTS = [(1, TP, D), (DB, DS, D), (1, 1, TP, DH, 2, DHD), (1, 1, TP, DH, DV), (1, 1, RH, RK, RV),
         (1, DB, DS, DH, 2, DHD), (1, DB, DS, DH, DV), (1, DB, RH, RK, RV)]


def kernel(**inputs):
    import concourse.bacc as bacc
    from concourse.bass_utils import run_bass_kernel_spmd

    nc = bacc.Bacc("TRN2", target_bir_lowering=False, num_devices=1)
    arrays, args = {}, []
    for name, a in [*((n, inputs[n]) for n in _INS), *tables().items()]:
        a = np.ascontiguousarray(a)
        arrays[f"in_{name}_dram"] = a
        args.append(nc.dram_tensor(f"in_{name}_dram", a.shape, mybir.dt.from_np(a.dtype), kind="ExternalInput").ap())
    for i, shape in enumerate(_OUTS):
        args.append(nc.dram_tensor(f"out_{i}_dram", shape, F, kind="ExternalOutput").ap())
    hybrid_layer(nc, *args)
    r = run_bass_kernel_spmd(nc, [arrays], core_ids=[0])
    return tuple(r.results[0][f"out_{i}_dram"] for i in range(len(_OUTS)))
```
